# Optimizing a Trainium2 kernel written in Bass

```python
import math
import jax, jax.numpy as jnp
from jax import lax
import numpy as np

D_MODEL = 1024
BATCH = 1
SEQ = 256
DEPTH = 2

N_MIXERS = 2
HEAD_DIM = 128
GDN_HEADS = D_MODEL // HEAD_DIM
GDN_CONV = 4
GDN_CHUNK = 64
NSA_Q_HEADS = D_MODEL // HEAD_DIM
NSA_KV_HEADS = NSA_Q_HEADS // 4
CMP_LEN = 32
CMP_STRIDE = 16
SLC_BLOCK = 64
SLC_TOPK = 16
WINDOW = 512
NSA_Q_BLOCK = 64
MEM_TOKENS = 256
MEM_HEADS = 4
NUM_BUCKETS = 32
MAX_DISTANCE = 128
D_FF = ((8 * D_MODEL // 3 + 255) // 256) * 256
FFN_CONV = 3
MEM_WIDTH = MEM_HEADS * HEAD_DIM
MIX_WIDTH = D_MODEL + MEM_WIDTH
GDN_COLS = 4 * GDN_HEADS * HEAD_DIM + 2 * GDN_HEADS
NSA_KV_WIDTH = NSA_KV_HEADS * HEAD_DIM
NSA_COLS = NSA_Q_HEADS * HEAD_DIM + 6 * NSA_KV_WIDTH + 3 * NSA_Q_HEADS
N_GDN = (DEPTH + 1) // 2
N_NSA = DEPTH // 2
EPS = 1e-6


def rms_norm(x, w):
    xf = x.astype(jnp.float32)
    y = xf * lax.rsqrt(jnp.mean(xf * xf, axis=-1, keepdims=True) + EPS)
    return (y * w.astype(jnp.float32)).astype(x.dtype)

def l2norm(x):
    xf = x.astype(jnp.float32)
    return xf * lax.rsqrt(jnp.sum(xf * xf, axis=-1, keepdims=True) + EPS)

def causal_dwconv(x, w):
    K = w.shape[0]
    S = x.shape[1]
    xp = jnp.pad(x, ((0, 0), (K - 1, 0), (0, 0)))
    y = xp[:, 0:S] * w[0]
    for j in range(1, K):
        y = y + xp[:, j:j + S] * w[j]
    return y

def t5_bucket(dist):
    n = jnp.maximum(dist, 0)
    max_exact = NUM_BUCKETS // 2
    logv = jnp.log(jnp.maximum(n, 1).astype(jnp.float32) / max_exact) / math.log(MAX_DISTANCE / max_exact)
    large = max_exact + (logv * (NUM_BUCKETS - max_exact)).astype(jnp.int32)
    large = jnp.minimum(large, NUM_BUCKETS - 1)
    return jnp.where(n < max_exact, n, large)

def masked_softmax(s, mask):
    s = jnp.where(mask, s.astype(jnp.float32), -jnp.inf)
    m = jnp.max(s, axis=-1, keepdims=True)
    m = jnp.where(jnp.isfinite(m), m, 0.0)
    p = jnp.where(mask, jnp.exp(s - m), 0.0)
    return p / jnp.maximum(jnp.sum(p, axis=-1, keepdims=True), 1e-30)

def gated_delta_rule_chunked(q, k, v, g, beta):
    f32 = jnp.float32
    B, H, S, dk = q.shape
    dv = v.shape[-1]
    C = GDN_CHUNK
    N = S // C
    q = (q.astype(f32) * dk ** -0.5).reshape(B, H, N, C, dk)
    k = k.astype(f32).reshape(B, H, N, C, dk)
    v = v.astype(f32).reshape(B, H, N, C, dv)
    beta = beta.astype(f32).reshape(B, H, N, C)
    gc = jnp.cumsum(g.astype(f32).reshape(B, H, N, C), axis=-1)
    incl = jnp.tril(jnp.ones((C, C), bool))
    strict = jnp.tril(jnp.ones((C, C), bool), -1)
    diff = gc[..., :, None] - gc[..., None, :]
    decay = jnp.where(incl, jnp.exp(jnp.where(incl, diff, 0.0)), 0.0)
    kb = k * beta[..., None]
    L = jnp.where(strict, jnp.einsum('bhnid,bhnjd->bhnij', kb, k) * decay, 0.0)
    eye = jnp.eye(C, dtype=f32)
    T = lax.linalg.triangular_solve(eye + L, jnp.broadcast_to(eye, L.shape),
                                    left_side=True, lower=True, unit_diagonal=True)
    u = jnp.einsum('bhnij,bhnjd->bhnid', T, v * beta[..., None])
    w = jnp.einsum('bhnij,bhnjd->bhnid', T, kb * jnp.exp(gc)[..., None])
    a_intra = jnp.where(incl, jnp.einsum('bhnid,bhnjd->bhnij', q, k) * decay, 0.0)
    q_dec = q * jnp.exp(gc)[..., None]
    k_dec = k * jnp.exp(gc[..., -1:] - gc)[..., None]
    g_last = jnp.exp(gc[..., -1])

    def chunk_step(state, xs):
        u_n, w_n, a_n, qd_n, kd_n, gl_n = xs
        v_new = u_n - jnp.einsum('bhcd,bhde->bhce', w_n, state)
        o_n = jnp.einsum('bhcd,bhde->bhce', qd_n, state) + jnp.einsum('bhij,bhje->bhie', a_n, v_new)
        state = state * gl_n[..., None, None] + jnp.einsum('bhcd,bhce->bhde', kd_n, v_new)
        return state, o_n

    to_n = lambda t: jnp.moveaxis(t, 2, 0)
    state0 = jnp.zeros((B, H, dk, dv), f32)
    _, o = lax.scan(chunk_step, state0,
                    (to_n(u), to_n(w), to_n(a_intra), to_n(q_dec), to_n(k_dec), to_n(g_last)))
    return jnp.moveaxis(o, 0, 2).reshape(B, H, S, dv)

def gdn_mixer(cols, conv_w, a_log, dt_bias, norm_w):
    B, S, _ = cols.shape
    H, dh = GDN_HEADS, HEAD_DIM
    wd = H * dh
    qkv = jax.nn.silu(causal_dwconv(cols[..., :3 * wd], conv_w)).reshape(B, S, 3, H, dh)
    q, k, v = qkv[:, :, 0], qkv[:, :, 1], qkv[:, :, 2]
    z = cols[..., 3 * wd:4 * wd].reshape(B, S, H, dh)
    b = cols[..., 4 * wd:4 * wd + H]
    a = cols[..., 4 * wd + H:4 * wd + 2 * H]
    beta = jax.nn.sigmoid(b.astype(jnp.float32))
    g = -jnp.exp(a_log.astype(jnp.float32)) * jax.nn.softplus(a.astype(jnp.float32) + dt_bias.astype(jnp.float32))
    heads = lambda t: jnp.swapaxes(t, 1, 2)
    o = gated_delta_rule_chunked(heads(l2norm(q)), heads(l2norm(k)), heads(v.astype(jnp.float32)),
                                 heads(g), heads(beta))
    o = jnp.swapaxes(o, 1, 2)
    o = rms_norm(o, norm_w) * jax.nn.silu(z.astype(jnp.float32))
    return o.reshape(B, S, wd).astype(cols.dtype)

def compress_blocks(t, pos_emb, w1, w2):
    B, S, G, dh = t.shape
    n_cmp = (S - CMP_LEN) // CMP_STRIDE + 1
    idx = (np.arange(n_cmp, dtype=np.int32)[:, None] * CMP_STRIDE
           + np.arange(CMP_LEN, dtype=np.int32)[None, :])
    blk = t[:, idx] + pos_emb[:, None, :]
    flat = jnp.transpose(blk, (0, 3, 1, 2, 4)).reshape(B, G, n_cmp, CMP_LEN * dh)
    return jax.nn.silu(flat @ w1) @ w2

def nsa_mixer(cols, rel_bias, pos_k, w1_k, w2_k, pos_v, w1_v, w2_v):
    B, S, _ = cols.shape
    HQ, G, dh = NSA_Q_HEADS, NSA_KV_HEADS, HEAD_DIM
    R = HQ // G
    Q = NSA_Q_BLOCK
    scale = dh ** -0.5
    qw = HQ * dh
    q = cols[..., :qw]
    kvs = [cols[..., qw + j * NSA_KV_WIDTH:qw + (j + 1) * NSA_KV_WIDTH].reshape(B, S, G, dh) for j in range(6)]
    k_cmp, v_cmp, k_slc, v_slc, k_win, v_win = kvs
    gates = jax.nn.sigmoid(cols[..., qw + 6 * NSA_KV_WIDTH:].astype(jnp.float32)).reshape(B, S, HQ, 3)

    n_q = S // Q
    n_cmp = (S - CMP_LEN) // CMP_STRIDE + 1
    n_slc = S // SLC_BLOCK
    n_sel = min(SLC_TOPK, n_slc)

    kc = compress_blocks(k_cmp, pos_k, w1_k, w2_k)
    vc = compress_blocks(v_cmp, pos_v, w1_v, w2_v)
    c_start = np.arange(n_cmp, dtype=np.int32) * CMP_STRIDE
    c_end = c_start + CMP_LEN - 1
    s_start = np.arange(n_slc, dtype=np.int32) * SLC_BLOCK
    sel_map = ((c_start[:, None] < s_start[None, :] + SLC_BLOCK)
               & (s_start[None, :] <= c_end[:, None])).astype(np.float32)
    to_blocks = lambda t: jnp.swapaxes(t, 1, 2).reshape(B, G, n_slc, SLC_BLOCK, dh)
    ks, vs = to_blocks(k_slc), to_blocks(v_slc)
    pad = lambda t: jnp.pad(jnp.swapaxes(t, 1, 2), ((0, 0), (0, 0), (WINDOW, 0), (0, 0)))
    kw, vw = pad(k_win), pad(v_win)
    tab = rel_bias.reshape(NUM_BUCKETS, G, R)
    c_end_j = jnp.asarray(c_end)
    bi = jnp.arange(B)[:, None, None, None]
    gi = jnp.arange(G)[None, :, None, None]

    def head_bias(dist):
        return jnp.moveaxis(tab[t5_bucket(dist)], (-2, -1), (0, 1))

    qh = jnp.moveaxis(q.reshape(B, S, G, R, dh).transpose(0, 2, 3, 1, 4).reshape(B, G, R, n_q, Q, dh), 3, 0)
    gh = jnp.moveaxis(gates.reshape(B, S, G, R, 3).transpose(0, 2, 3, 1, 4).reshape(B, G, R, n_q, Q, 3), 3, 0)

    def step(args):
        qi, qb, gb = args
        s0 = qi * Q
        t = s0 + jnp.arange(Q, dtype=jnp.int32)
        dist_c = t[:, None] - c_end_j[None, :]
        sc = jnp.einsum('bgrqd,bgcd->bgrqc', qb, kc).astype(jnp.float32) * scale + head_bias(dist_c)
        p_c = masked_softmax(sc, dist_c >= 0)
        o_c = jnp.einsum('bgrqc,bgcd->bgrqd', p_c, vc.astype(jnp.float32))
        imp = jnp.einsum('bgqc,cs->bgqs', jnp.sum(p_c, axis=2), sel_map)
        jb = jnp.arange(n_slc, dtype=jnp.int32)[None, :]
        tb = (t // SLC_BLOCK)[:, None]
        forced = (jb == 0) | (jb == tb) | (jb == tb - 1)
        score = jnp.where(jb <= tb, jnp.where(forced, jnp.inf, imp), -jnp.inf)
        vals, idx = lax.top_k(score, n_sel)
        ok = vals > -jnp.inf
        kg = ks[bi, gi, idx].reshape(B, G, Q, n_sel * SLC_BLOCK, dh)
        vg = vs[bi, gi, idx].reshape(B, G, Q, n_sel * SLC_BLOCK, dh)
        pos = idx[..., None] * SLC_BLOCK + jnp.arange(SLC_BLOCK, dtype=jnp.int32)
        dist_s = t[:, None, None] - pos
        mask_s = (ok[..., None] & (dist_s >= 0)).reshape(B, G, Q, n_sel * SLC_BLOCK)
        bias_s = jnp.moveaxis(tab[t5_bucket(dist_s).reshape(B, G, Q, n_sel * SLC_BLOCK), gi], -1, 2)
        ss = jnp.einsum('bgrqd,bgqkd->bgrqk', qb, kg).astype(jnp.float32) * scale + bias_s
        p_s = masked_softmax(ss, mask_s[:, :, None])
        o_s = jnp.einsum('bgrqk,bgqkd->bgrqd', p_s, vg.astype(jnp.float32))
        kwb = lax.dynamic_slice_in_dim(kw, s0, Q + WINDOW, axis=2)
        vwb = lax.dynamic_slice_in_dim(vw, s0, Q + WINDOW, axis=2)
        kpos = s0 - WINDOW + jnp.arange(Q + WINDOW, dtype=jnp.int32)
        dist_w = t[:, None] - kpos[None, :]
        mask_w = (dist_w >= 0) & (dist_w < WINDOW) & (kpos[None, :] >= 0)
        sw = jnp.einsum('bgrqd,bgkd->bgrqk', qb, kwb).astype(jnp.float32) * scale + head_bias(dist_w)
        p_w = masked_softmax(sw, mask_w)
        o_w = jnp.einsum('bgrqk,bgkd->bgrqd', p_w, vwb.astype(jnp.float32))
        o = gb[..., 0:1] * o_c + gb[..., 1:2] * o_s + gb[..., 2:3] * o_w
        return o.astype(cols.dtype)

    out = lax.map(step, (jnp.arange(n_q, dtype=jnp.int32), qh, gh))
    return jnp.transpose(out, (1, 0, 4, 2, 3, 5)).reshape(B, S, HQ * dh)

def memory_attention(qm, mem_n, w_kv):
    B, S = qm.shape[:2]
    kv = (mem_n @ w_kv).reshape(B, -1, 2, MEM_HEADS, HEAD_DIM)
    k, v = kv[:, :, 0], kv[:, :, 1]
    s = jnp.einsum('bshd,bmhd->bhsm', qm, k).astype(jnp.float32) * HEAD_DIM ** -0.5
    p = jax.nn.softmax(s, axis=-1)
    o = jnp.einsum('bhsm,bmhd->bshd', p, v.astype(jnp.float32))
    return o.reshape(B, S, MEM_WIDTH).astype(qm.dtype)

def conv_glu(h, w_up, conv_w, conv_b, w_down):
    gate, val = jnp.split(h @ w_up, 2, axis=-1)
    gate = causal_dwconv(gate, conv_w) + conv_b
    return (jax.nn.silu(gate) * val) @ w_down

def first_inputs(seed: int = 0) -> dict:
    key = jax.random.key(seed)
    ks = iter(jax.random.split(key, 32))
    f32 = jnp.float32
    nrm = lambda shape, scale: scale * jax.random.normal(next(ks), shape, f32)
    gain = lambda shape: 1.0 + nrm(shape, 0.02)
    x = nrm((BATCH, SEQ, D_MODEL), 1.0)
    mem = nrm((BATCH, MEM_TOKENS, D_MODEL), 1.0)
    rel_bias = nrm((NUM_BUCKETS, NSA_Q_HEADS), 0.2)
    norm_mix_w = gain((DEPTH, D_MODEL))
    norm_ffn_w = gain((DEPTH, D_MODEL))
    final_norm_w = gain((D_MODEL,))
    mem_norm_w = gain((DEPTH, D_MODEL))
    mem_w_kv = nrm((DEPTH, D_MODEL, 2 * MEM_WIDTH), D_MODEL ** -0.5)
    w_out = nrm((DEPTH, MIX_WIDTH, D_MODEL), MIX_WIDTH ** -0.5)
    gdn_w_in = nrm((N_GDN, D_MODEL, GDN_COLS + MEM_WIDTH), D_MODEL ** -0.5)
    gdn_conv_w = nrm((N_GDN, GDN_CONV, 3 * GDN_HEADS * HEAD_DIM), GDN_CONV ** -0.5)
    gdn_a_log = jnp.log(jax.random.uniform(next(ks), (N_GDN, GDN_HEADS), f32, 1.0, 16.0))
    dt = jnp.exp(jax.random.uniform(next(ks), (N_GDN, GDN_HEADS), f32, math.log(1e-3), math.log(1e-1)))
    gdn_dt_bias = dt + jnp.log(-jnp.expm1(-dt))
    gdn_norm_w = gain((N_GDN, HEAD_DIM))
    nsa_w_in = nrm((N_NSA, D_MODEL, NSA_COLS + MEM_WIDTH), D_MODEL ** -0.5)
    nsa_cmp_pos_k = nrm((N_NSA, CMP_LEN, HEAD_DIM), 0.1)
    nsa_cmp_w1_k = nrm((N_NSA, CMP_LEN * HEAD_DIM, HEAD_DIM), (CMP_LEN * HEAD_DIM) ** -0.5)
    nsa_cmp_w2_k = nrm((N_NSA, HEAD_DIM, HEAD_DIM), HEAD_DIM ** -0.5)
    nsa_cmp_pos_v = nrm((N_NSA, CMP_LEN, HEAD_DIM), 0.1)
    nsa_cmp_w1_v = nrm((N_NSA, CMP_LEN * HEAD_DIM, HEAD_DIM), (CMP_LEN * HEAD_DIM) ** -0.5)
    nsa_cmp_w2_v = nrm((N_NSA, HEAD_DIM, HEAD_DIM), HEAD_DIM ** -0.5)
    ffn_w_up = nrm((DEPTH, D_MODEL, 2 * D_FF), D_MODEL ** -0.5)
    ffn_conv_w = nrm((DEPTH, FFN_CONV, D_FF), FFN_CONV ** -0.5)
    ffn_conv_b = nrm((DEPTH, D_FF), 0.02)
    ffn_w_down = nrm((DEPTH, D_FF, D_MODEL), D_FF ** -0.5)
    return {'x': x, 'mem': mem, 'rel_bias': rel_bias, 'norm_mix_w': norm_mix_w,
            'norm_ffn_w': norm_ffn_w, 'final_norm_w': final_norm_w, 'mem_norm_w': mem_norm_w,
            'mem_w_kv': mem_w_kv, 'w_out': w_out, 'gdn_w_in': gdn_w_in, 'gdn_conv_w': gdn_conv_w,
            'gdn_a_log': gdn_a_log, 'gdn_dt_bias': gdn_dt_bias, 'gdn_norm_w': gdn_norm_w,
            'nsa_w_in': nsa_w_in, 'nsa_cmp_pos_k': nsa_cmp_pos_k, 'nsa_cmp_w1_k': nsa_cmp_w1_k,
            'nsa_cmp_w2_k': nsa_cmp_w2_k, 'nsa_cmp_pos_v': nsa_cmp_pos_v, 'nsa_cmp_w1_v': nsa_cmp_w1_v,
            'nsa_cmp_w2_v': nsa_cmp_w2_v, 'ffn_w_up': ffn_w_up, 'ffn_conv_w': ffn_conv_w,
            'ffn_conv_b': ffn_conv_b, 'ffn_w_down': ffn_w_down}

def first_block(x, mem, rel_bias, norm_mix_w, norm_ffn_w, final_norm_w, mem_norm_w, mem_w_kv, w_out,
              gdn_w_in, gdn_conv_w, gdn_a_log, gdn_dt_bias, gdn_norm_w, nsa_w_in, nsa_cmp_pos_k,
              nsa_cmp_w1_k, nsa_cmp_w2_k, nsa_cmp_pos_v, nsa_cmp_w1_v, nsa_cmp_w2_v, ffn_w_up,
              ffn_conv_w, ffn_conv_b, ffn_w_down):
    B, S, _ = x.shape
    for i in range(DEPTH):
        h = rms_norm(x, norm_mix_w[i])
        mem_n = rms_norm(mem, mem_norm_w[i])
        j = i // N_MIXERS
        if i % N_MIXERS == 0:
            proj = h @ gdn_w_in[j]
            mix = gdn_mixer(proj[..., :GDN_COLS], gdn_conv_w[j], gdn_a_log[j], gdn_dt_bias[j], gdn_norm_w[j])
            qm = proj[..., GDN_COLS:]
        else:
            proj = h @ nsa_w_in[j]
            mix = nsa_mixer(proj[..., :NSA_COLS], rel_bias, nsa_cmp_pos_k[j], nsa_cmp_w1_k[j],
                            nsa_cmp_w2_k[j], nsa_cmp_pos_v[j], nsa_cmp_w1_v[j], nsa_cmp_w2_v[j])
            qm = proj[..., NSA_COLS:]
        mo = memory_attention(qm.reshape(B, S, MEM_HEADS, HEAD_DIM), mem_n, mem_w_kv[i])
        x = x + jnp.concatenate([mix, mo], axis=-1) @ w_out[i]
        x = x + conv_glu(rms_norm(x, norm_ffn_w[i]), ffn_w_up[i], ffn_conv_w[i], ffn_conv_b[i], ffn_w_down[i])
    return rms_norm(x, final_norm_w)


GRID_W = 64
CTX_LEN = 256
HEAD_DIM_2 = 64
ATTN_WIDTH = D_MODEL // 2
N_Q_HEADS = ATTN_WIDTH // HEAD_DIM_2
N_KV_HEADS = 2
Q_GROUP = N_Q_HEADS // N_KV_HEADS
KV_WIDTH = N_KV_HEADS * HEAD_DIM_2
ATTN_SCALE = HEAD_DIM_2 ** -0.5
Q_BLOCK = 128
ROPE_THETA = 10000.0
POOL_WINDOWS = (2, 4, 8, 16)
POOL_WIDTH = D_MODEL - ATTN_WIDTH
POOL_GROUP_DIM = POOL_WIDTH // len(POOL_WINDOWS)
IN_A_WIDTH = ATTN_WIDTH + 2 * KV_WIDTH + POOL_WIDTH
OUT_A_WIDTH = ATTN_WIDTH + POOL_WIDTH
CHUNK = 128
GMLP_WIDTH = D_MODEL
GMLP_GROUPS = 8
GMLP_GROUP_DIM = GMLP_WIDTH // GMLP_GROUPS
D_FF_2 = 2816
N_MOD = 9
N_EVEN = (DEPTH + 1) // 2
N_ODD = DEPTH // 2


def rms_norm_2(x, g):
    xf = x.astype(jnp.float32)
    y = xf * lax.rsqrt(jnp.mean(xf * xf, axis=-1, keepdims=True) + EPS)
    return (y * g.astype(jnp.float32)).astype(x.dtype)

def modulate(x, g, shift, scale):
    return rms_norm_2(x, g) * (1 + scale) + shift

def swiglu(h, w13, w2):
    a, b = jnp.split(h @ w13, 2, axis=-1)
    return (jax.nn.silu(a) * b) @ w2

def half_ffn(x, g, shift, scale, gate, w13, w2):
    return x + 0.5 * gate * swiglu(modulate(x, g, shift, scale), w13, w2)

def axial_rope_tables(n_tokens, dtype):
    n_rows = n_tokens // GRID_W
    rows = jnp.repeat(jnp.arange(n_rows), GRID_W).astype(jnp.float32)
    cols = jnp.tile(jnp.arange(GRID_W), n_rows).astype(jnp.float32)
    half = HEAD_DIM_2 // 2
    inv_freq = ROPE_THETA ** (-jnp.arange(0, half, 2, dtype=jnp.float32) / half)
    ang_r = rows[:, None] * inv_freq[None, :]
    ang_c = cols[:, None] * inv_freq[None, :]
    return (jnp.cos(ang_r).astype(dtype), jnp.sin(ang_r).astype(dtype),
            jnp.cos(ang_c).astype(dtype), jnp.sin(ang_c).astype(dtype))

def rope_half(x, cos, sin):
    x1, x2 = jnp.split(x, 2, axis=-1)
    cos = cos[None, :, None, :]
    sin = sin[None, :, None, :]
    return jnp.concatenate([x1 * cos - x2 * sin, x1 * sin + x2 * cos], axis=-1)

def apply_axial_rope(x, tabs):
    cr, sr, cc, sc = tabs
    xr, xc = jnp.split(x, 2, axis=-1)
    return jnp.concatenate([rope_half(xr, cr, sr), rope_half(xc, cc, sc)], axis=-1)

def gqa_attend(q, k, v):
    b, nq = q.shape[:2]
    qg = q.reshape(b, nq, N_KV_HEADS, Q_GROUP, HEAD_DIM_2)
    sc = jnp.einsum('bqhgd,bkhd->bhgqk', qg, k, preferred_element_type=jnp.float32) * ATTN_SCALE
    pr = jax.nn.softmax(sc, axis=-1).astype(v.dtype)
    return jnp.einsum('bhgqk,bkhd->bqhgd', pr, v).reshape(b, nq, ATTN_WIDTH)

def latent_attention(q, k_lat, v_lat, k_ctx, v_ctx):
    b, s = q.shape[:2]
    k_all = jnp.concatenate([k_ctx, k_lat], axis=1)
    v_all = jnp.concatenate([v_ctx, v_lat], axis=1)
    nb = s // Q_BLOCK
    qb = jnp.moveaxis(q.reshape(b, nb, Q_BLOCK, N_Q_HEADS, HEAD_DIM_2), 1, 0)
    ob = lax.map(lambda qblk: gqa_attend(qblk, k_all, v_all), qb)
    return jnp.moveaxis(ob, 0, 1).reshape(b, s, ATTN_WIDTH)

def project_a(h, w_in, qk_g):
    b, n = h.shape[:2]
    z = h @ w_in
    q = rms_norm_2(z[..., :ATTN_WIDTH].reshape(b, n, N_Q_HEADS, HEAD_DIM_2), qk_g[0])
    k = rms_norm_2(z[..., ATTN_WIDTH:ATTN_WIDTH + KV_WIDTH].reshape(b, n, N_KV_HEADS, HEAD_DIM_2), qk_g[1])
    v = z[..., ATTN_WIDTH + KV_WIDTH:ATTN_WIDTH + 2 * KV_WIDTH].reshape(b, n, N_KV_HEADS, HEAD_DIM_2)
    p = z[..., ATTN_WIDTH + 2 * KV_WIDTH:]
    return q, k, v, p

def project_ctx_kv(h, w_in, qk_g):
    b, n = h.shape[:2]
    z = h @ w_in[:, ATTN_WIDTH:ATTN_WIDTH + 2 * KV_WIDTH]
    k = rms_norm_2(z[..., :KV_WIDTH].reshape(b, n, N_KV_HEADS, HEAD_DIM_2), qk_g[1])
    v = z[..., KV_WIDTH:].reshape(b, n, N_KV_HEADS, HEAD_DIM_2)
    return k, v

def multiscale_pool(p, pool_w, pool_scale):
    n = p.shape[1]
    pf = p.astype(jnp.float32)
    cs = jnp.concatenate([jnp.zeros_like(pf[:, :1]), jnp.cumsum(pf, axis=1)], axis=1)
    t = jnp.arange(n)
    outs = []
    for gi, w in enumerate(POOL_WINDOWS):
        sl = slice(gi * POOL_GROUP_DIM, (gi + 1) * POOL_GROUP_DIM)
        lo = jnp.clip(t - w // 2, 0, n)
        hi = jnp.clip(t + w // 2, 0, n)
        csg = cs[..., sl]
        mean = (csg[:, hi] - csg[:, lo]) / (hi - lo).astype(jnp.float32)[None, :, None]
        outs.append((mean - pf[..., sl]).astype(p.dtype) @ pool_w[gi])
    return jnp.concatenate(outs, axis=-1) * pool_scale

def combine_a(attn, p, pool_w, pool_scale, w_out):
    return jnp.concatenate([attn, multiscale_pool(p, pool_w, pool_scale)], axis=-1) @ w_out

def mixer_c(h, w_in, v_g, w_sp, b_sp, w_out):
    b, n = h.shape[:2]
    z = jax.nn.gelu(h @ w_in)
    u, v = jnp.split(z, 2, axis=-1)
    v = rms_norm_2(v, v_g)
    vc = v.reshape(b, n // CHUNK, CHUNK, GMLP_GROUPS, GMLP_GROUP_DIM)
    sv = jnp.einsum('gpq,bnqgc->bnpgc', w_sp, vc) + b_sp.T[None, None, :, :, None]
    return (u * sv.reshape(b, n, GMLP_WIDTH)) @ w_out

def second_inputs(seed: int = 0) -> dict:
    key = jax.random.key(seed)
    ks = jax.random.split(key, 20)
    f32 = jnp.float32

    def nrm(k, shape, fan_in):
        return jax.random.normal(k, shape, f32) * (fan_in ** -0.5)

    def gain(k, shape):
        return 1.0 + 0.05 * jax.random.normal(k, shape, f32)

    return {
        "x": jax.random.normal(ks[0], (BATCH, SEQ, D_MODEL), f32),
        "c": jax.random.normal(ks[1], (BATCH, D_MODEL), f32),
        "ctx": jax.random.normal(ks[2], (BATCH, CTX_LEN, D_MODEL), f32),
        "c_ctx": jax.random.normal(ks[3], (D_MODEL,), f32),
        "w_mod": 0.5 * nrm(ks[4], (DEPTH, D_MODEL, N_MOD * D_MODEL), D_MODEL),
        "b_mod": 0.01 * jax.random.normal(ks[5], (DEPTH, N_MOD * D_MODEL), f32),
        "norm_g": gain(ks[6], (DEPTH, 3, D_MODEL)),
        "ffn_w13": nrm(ks[7], (DEPTH, 2, D_MODEL, 2 * D_FF_2), D_MODEL),
        "ffn_w2": nrm(ks[8], (DEPTH, 2, D_FF_2, D_MODEL), D_FF_2),
        "w_in_a": nrm(ks[9], (N_EVEN, D_MODEL, IN_A_WIDTH), D_MODEL),
        "qk_norm_g": gain(ks[10], (N_EVEN, 2, HEAD_DIM_2)),
        "pool_w": nrm(ks[11], (N_EVEN, len(POOL_WINDOWS), POOL_GROUP_DIM, POOL_GROUP_DIM), POOL_GROUP_DIM),
        "pool_scale": gain(ks[12], (N_EVEN, POOL_WIDTH)),
        "w_out_a": nrm(ks[13], (N_EVEN, OUT_A_WIDTH, D_MODEL), OUT_A_WIDTH),
        "w_in_c": nrm(ks[14], (N_ODD, D_MODEL, 2 * GMLP_WIDTH), D_MODEL),
        "v_norm_g": gain(ks[15], (N_ODD, GMLP_WIDTH)),
        "w_sp": nrm(ks[16], (N_ODD, GMLP_GROUPS, CHUNK, CHUNK), CHUNK),
        "b_sp": gain(ks[17], (N_ODD, GMLP_GROUPS, CHUNK)),
        "w_out_c": nrm(ks[18], (N_ODD, GMLP_WIDTH, D_MODEL), GMLP_WIDTH),
    }

def second_block(x, c, ctx, c_ctx, w_mod, b_mod, norm_g, ffn_w13, ffn_w2,
              w_in_a, qk_norm_g, pool_w, pool_scale, w_out_a,
              w_in_c, v_norm_g, w_sp, b_sp, w_out_c):
    b, s, d = x.shape
    rope_tabs = axial_rope_tables(s, x.dtype)
    silu_c = jax.nn.silu(c)
    silu_cc = jax.nn.silu(c_ctx)
    cs = ctx
    for i in range(DEPTH):
        m = (silu_c @ w_mod[i] + b_mod[i]).reshape(b, 1, N_MOD, d)
        reads_ctx = (i % 2 == 0)
        later_reads_ctx = any(j % 2 == 0 for j in range(i + 1, DEPTH))
        ctx_needed = reads_ctx or later_reads_ctx
        if ctx_needed:
            mc = (silu_cc @ w_mod[i] + b_mod[i]).reshape(1, 1, N_MOD, d)
            cs = half_ffn(cs, norm_g[i, 0], mc[:, :, 0], mc[:, :, 1], mc[:, :, 2],
                          ffn_w13[i, 0], ffn_w2[i, 0])
        x = half_ffn(x, norm_g[i, 0], m[:, :, 0], m[:, :, 1], m[:, :, 2], ffn_w13[i, 0], ffn_w2[i, 0])

        h = modulate(x, norm_g[i, 1], m[:, :, 3], m[:, :, 4])
        if i % 2 == 0:
            e = i // 2
            hc = modulate(cs, norm_g[i, 1], mc[:, :, 3], mc[:, :, 4])
            if later_reads_ctx:
                qc, kc, vc, pc = project_a(hc, w_in_a[e], qk_norm_g[e])
            else:
                kc, vc = project_ctx_kv(hc, w_in_a[e], qk_norm_g[e])
            q, k, v, p = project_a(h, w_in_a[e], qk_norm_g[e])
            q = apply_axial_rope(q, rope_tabs)
            k = apply_axial_rope(k, rope_tabs)
            attn = latent_attention(q, k, v, kc, vc)
            x = x + m[:, :, 5] * combine_a(attn, p, pool_w[e], pool_scale[e], w_out_a[e])
            if later_reads_ctx:
                attn_c = gqa_attend(qc, kc, vc)
                cs = cs + mc[:, :, 5] * combine_a(attn_c, pc, pool_w[e], pool_scale[e], w_out_a[e])
        else:
            o = i // 2
            x = x + m[:, :, 5] * mixer_c(h, w_in_c[o], v_norm_g[o], w_sp[o], b_sp[o], w_out_c[o])
            if later_reads_ctx:
                hc = modulate(cs, norm_g[i, 1], mc[:, :, 3], mc[:, :, 4])
                cs = cs + mc[:, :, 5] * mixer_c(hc, w_in_c[o], v_norm_g[o], w_sp[o], b_sp[o], w_out_c[o])

        if later_reads_ctx:
            cs = half_ffn(cs, norm_g[i, 2], mc[:, :, 6], mc[:, :, 7], mc[:, :, 8],
                          ffn_w13[i, 1], ffn_w2[i, 1])
        x = half_ffn(x, norm_g[i, 2], m[:, :, 6], m[:, :, 7], m[:, :, 8], ffn_w13[i, 1], ffn_w2[i, 1])
    return x


def setup_inputs(seed=0):
    out = dict(first_inputs(seed))
    for name, value in second_inputs(seed + 1).items():
        if name != "x":
            out[name + "_2"] = value
    return out


def reference(
    x, mem, rel_bias, norm_mix_w, norm_ffn_w, final_norm_w, mem_norm_w, mem_w_kv, w_out,
    gdn_w_in, gdn_conv_w, gdn_a_log, gdn_dt_bias, gdn_norm_w, nsa_w_in, nsa_cmp_pos_k,
    nsa_cmp_w1_k, nsa_cmp_w2_k, nsa_cmp_pos_v, nsa_cmp_w1_v, nsa_cmp_w2_v, ffn_w_up, ffn_conv_w,
    ffn_conv_b, ffn_w_down, c_2, ctx_2, c_ctx_2, w_mod_2, b_mod_2, norm_g_2, ffn_w13_2,
    ffn_w2_2, w_in_a_2, qk_norm_g_2, pool_w_2, pool_scale_2, w_out_a_2, w_in_c_2, v_norm_g_2,
    w_sp_2, b_sp_2, w_out_c_2,
):
    x = first_block(
        x, mem, rel_bias, norm_mix_w, norm_ffn_w, final_norm_w, mem_norm_w, mem_w_kv, w_out,
        gdn_w_in, gdn_conv_w, gdn_a_log, gdn_dt_bias, gdn_norm_w, nsa_w_in, nsa_cmp_pos_k,
        nsa_cmp_w1_k, nsa_cmp_w2_k, nsa_cmp_pos_v, nsa_cmp_w1_v, nsa_cmp_w2_v, ffn_w_up,
        ffn_conv_w, ffn_conv_b, ffn_w_down,
    )
    return second_block(
        x, c_2, ctx_2, c_ctx_2, w_mod_2, b_mod_2, norm_g_2, ffn_w13_2, ffn_w2_2, w_in_a_2,
        qk_norm_g_2, pool_w_2, pool_scale_2, w_out_a_2, w_in_c_2, v_norm_g_2, w_sp_2, b_sp_2,
        w_out_c_2,
    )


_drawn_inputs = setup_inputs


def setup_inputs(seed=0):
    import zlib

    import numpy as np

    out = dict(_drawn_inputs(seed))
    spreads = {}
    factors = {'norm_mix_w': 3.047,
     'norm_ffn_w': 2.767,
     'mem_norm_w': 8.0,
     'gdn_norm_w': 4.857,
     'nsa_cmp_pos_k': 8.0,
     'nsa_cmp_pos_v': 10.825,
     'ffn_conv_b': 4.04,
     'ctx_2': 5.216,
     'b_mod_2': 3.765,
     'qk_norm_g_2': 8.0,
     'pool_scale_2': 5.241,
     'v_norm_g_2': 5.536,
     'b_sp_2': 5.444,
     'rel_bias': 2.908}
    for name, (base, spread) in spreads.items():
        noise = np.random.default_rng([zlib.crc32(name.encode()), seed]).standard_normal(out[name].shape)
        drawn = base * np.exp(spread * noise) if base else spread * noise
        out[name] = __import__('jax').numpy.asarray(drawn.astype(out[name].dtype))
    for name, factor in factors.items():
        out[name] = (out[name] * factor).astype(out[name].dtype)
    return out
```

```python
import math

import numpy as np

import concourse.bass as bass
from concourse import mybir

F32 = mybir.dt.float32
BF16 = mybir.dt.bfloat16
ALU = mybir.AluOpType
ACT = mybir.ActivationFunctionType
AX_X = mybir.AxisListType.X

P = 128
S = 256
D = 1024
DK = D // P
TT2 = S // P
NH = 8
C = 64
F = 2816
FB = F // P
MEMH = 4
NCMP = (S - 32) // 16 + 1
NMOD = 9 * DK
EPS = 1e-6
SCALE = P ** -0.5
NEG = -1e30
R = 6
TILES = 16
BUCKETS = 32



def columns(parts):
    at, out = 0, {}
    for name, width in parts:
        out[name] = (at, at + width)
        at += width
    return out, at


VEC, NVEC = columns([
    ("norm_mix", 2 * DK), ("norm_ffn", 2 * DK), ("final_norm", DK), ("mem_norm", 2 * DK),
    ("gdn_conv", 4 * 3 * NH), ("gdn_norm", 1), ("ffn_conv", 2 * 3 * FB), ("ffn_bias", 2 * FB),
    ("pos_k", 32), ("pos_v", 32), ("b_mod", 2 * NMOD), ("norm_g", 6 * DK), ("qk_norm", 2),
    ("pool_scale", 4), ("v_norm", DK), ("cond", 2 * DK)])
SMALL, NSMALL = columns([
    ("w_ba", DK * 16), ("w_gate", DK * 24), ("w2_k", P), ("w2_v", P), ("pool_w", 4 * P),
    ("w_sp", NH * P)])
CST, NCST = columns([
    ("ident", P), ("ones", P), ("tri", P), ("half", P), ("neg", P), ("before", P), ("flip", P),
    ("levels", 6 * P), ("rope", P), ("cos", S), ("sin", S), ("count", 4 * S)])
STREAM = [("mem_kv0", 4), ("gdn_in", 18), ("out0", 6), ("ffn0", 33),
          ("mem_kv1", 4), ("nsa_in", 12), ("cmp_k", 2), ("cmp_v", 2), ("out1", 6), ("ffn1", 33),
          ("mod0", 36), ("mod1", 36), ("ffn2c", 33), ("ffn2", 33), ("in_a", 6), ("out_a", 4), ("ffn3", 33),
          ("ffn4", 33), ("in_c", 8), ("out_c", 4), ("ffn5", 33)]
NSLOT = sum(n for _, n in STREAM)



class Queue:

    def __init__(self, engine, sem, apart=None):
        self.engine, self.sem, self.n, self.i = engine, sem, 0, None
        self.seen, self.apart = {}, apart

    def wait(self, *ticks):
        for sem, value in ticks:
            if isinstance(value, int):
                if self.seen.get(sem.name, 0) >= value:
                    continue
                self.seen[sem.name] = value
            self.engine.wait_ge(sem, value)

    def done(self, instruction):
        instruction.then_inc(self.sem, 1)
        if self.i is None:
            self.n += 1
            return (self.sem, self.n)
        self.k += 1
        return (self.sem, self.i * self.per + (self.n + self.k))

    def run(self, op, *args, after=(), **kw):
        self.wait(*after)
        if self.apart is not None and self.i is not None:
            self.engine.sem_inc(self.apart, 1)
        return self.done(op(*args, **kw))

    def last(self):
        return (self.sem, self.n)

    def enter(self, i, per):
        self.i, self.per, self.k = i, per, 0

    def leave(self, times):
        assert self.k == self.per
        self.n += times * self.per
        self.i = None


class Ring:

    def __init__(self, tile, filled, used):
        self.tile, self.filled, self.used, self.g = tile, filled, used, 0

    def slot(self, i, u):
        at = self.g + u
        tiles = self.tile[:, at % R, :].rearrange("p (t c) -> p t c", c=P)
        return tiles, (self.filled[at % R], i * 16 + 16 * (at // R + 1)), (self.used, i * R + (at + 1))


def program(nc, src, weights, y_out, scratch):

    def sbuf(name, shape, dt=F32):
        return nc.alloc_sbuf_tensor(name, [P] + shape, dt)

    V = Queue(nc.vector, nc.alloc_semaphore("vector_done"))
    A = Queue(nc.scalar, nc.alloc_semaphore("scalar_done"), apart=nc.alloc_semaphore("apart"))
    T = Queue(nc.tensor, nc.alloc_semaphore("tensor_done"))
    ring = Ring(sbuf("ring", [R, TILES * P]), [nc.alloc_semaphore(f"filled{r}") for r in range(R)],
                nc.alloc_semaphore("slots_used"))
    ve, ac, te = nc.vector, nc.scalar, nc.tensor

    X = sbuf("X", [DK, S])
    SIDE = sbuf("SIDE", [DK, S])
    PROJ = sbuf("PROJ", [36, S])
    MIX = sbuf("MIX", [12, S])
    KV = sbuf("KV", [DK, S])
    AR = [sbuf(f"AR{n}", [2048]) for n in range(5)]
    STATE = sbuf("STATE", [NH, P])
    VNEW = sbuf("VNEW", [NH, P])
    vec = sbuf("vec", [NVEC])
    small = sbuf("small", [NSMALL])
    cst = sbuf("cst", [NCST])
    rows = sbuf("rows", [16])
    tab = sbuf("tab", [NH])
    onehot = sbuf("onehot", [512])
    bsp = sbuf("bsp", [NH * P])
    RINV = sbuf("RINV", [S])
    RINV2 = sbuf("RINV2", [S])
    zeros = sbuf("zeros", [512], BF16)
    epsc = sbuf("epsc", [4])
    mod = [sbuf("mod0", [NMOD, 2]), sbuf("mod1", [NMOD, 2])]
    gainA = sbuf("gainA", [DK])
    gainB = sbuf("gainB", [DK])
    tiny = sbuf("tiny", [512])
    ACC = nc.alloc_psum_tensor("ACC", [P, 4, 512], F32)
    WRK = nc.alloc_psum_tensor("WRK", [P, 4, 512], F32)

    def v_(name, k=0, n=None):
        a, b = VEC[name]
        return vec[:, a + k:(a + k + n if n else b)]

    def s_(name):
        return small[:, SMALL[name][0]:SMALL[name][1]]

    def c_(name):
        return cst[:, CST[name][0]:CST[name][1]]

    ident, ones = c_("ident"), c_("ones")

    def heads(ap, h=NH):
        return ap.rearrange("p (h i) -> p h i", h=h)

    def over_rows(ap, h=NH):
        return ap.unsqueeze(1).broadcast_to([ap.shape[0], h, ap.shape[1]])

    def over_cols(ap, n=P):
        return ap.unsqueeze(2).broadcast_to([ap.shape[0], ap.shape[1], n])

    def flat(ps, a, b):
        return ps[:, a:b, :].rearrange("p b c -> p (b c)")

    def everything():
        return [V.last(), A.last(), T.last(), (ring.used, ring.g)]

    loaded = {}

    def load(name, dst, source):
        loaded[name] = (nc.alloc_semaphore("load_" + name), 16)
        nc.sync.dma_start(dst, source).then_inc(loaded[name][0], 16)

    load("side", SIDE[:, :, :], src["mem"])
    load("vec", vec[:, :], src["vec"])
    load("cst", cst[:, :], src["cst"])

    def fill(n, pos, source):
        nc.sync.dma_start(ring.tile[:, pos, :], source).then_inc(ring.filled[pos], 16)

    for n in range(R):
        fill(n, n, weights[n, :, :])
        if n == 1:
            load("x", X[:, :, :], src["x"])
            load("small", small[:, :], src["small"])
            load("rows", rows[:, :], src["rows"].partition_broadcast(P))
            load("tab", tab[0:BUCKETS, :], src["tab"])
            load("onehot", onehot[0:BUCKETS + 1, :], src["onehot"])
            load("bsp", bsp[0:1, :], src["bsp"].unsqueeze(0))

    bias_table = {}

    def stream_from(n0, n1):
        full = (n1 - n0) // R
        with nc.sync.Fori(0, full) as i:
            for u in range(R):
                nc.sync.wait_ge(ring.used, i * R + (n0 + u - R + 1))
                nc.sync.dma_start(ring.tile[:, (n0 + u) % R, :],
                                  weights[bass.ds(i * R + (n0 + u), 1), :, :].rearrange("a p n -> p (a n)")
                                  ).then_inc(ring.filled[(n0 + u) % R], 16)
        for n in range(n0 + full * R, n1):
            nc.sync.wait_ge(ring.used, n - R + 1)
            fill(n, n % R, weights[n, :, :])

    V.run(ve.memset, zeros[:, :], 0.0)
    V.run(ve.memset, epsc[:, 0:1], EPS)
    V.run(ve.memset, epsc[:, 1:2], 1.0)
    V.run(ve.memset, STATE[:, :, :], 0.0)
    V.run(ve.memset, tab[BUCKETS:BUCKETS + 1, :], NEG)
    made = V.last()
    for q in (V, A, T):
        q.wait(made, loaded["vec"], loaded["cst"])


    def mm(out, lhsT, rhs, start=True, stop=True, **kw):
        return te.matmul(out, lhsT, rhs, start=start, stop=stop, **kw)

    def inverse_norm(out, source, sq, sums, blocks, ones_, divisor, after):
        sq = sq.rearrange("p (k t) -> p k t", t=S)[:, 0:blocks, :]
        t = A.run(ac.activation, sq, source, ACT.Square, after=after)
        T.wait(t)
        for k in range(blocks):
            last = mm(sums, ones_, sq[:, k, :], k == 0, k == blocks - 1)
        t = A.run(ac.activation, out, sums, ACT.Sqrt, scale=1.0 / divisor, bias=epsc[:, 0:1], after=[T.done(last)])
        return V.run(ve.reciprocal, out, out, after=[t])

    def rms_norm(dst, source, gain, after, shift=None, rinv=None):
        rinv = RINV if rinv is None else rinv
        t = inverse_norm(rinv[:, :], source[:, :, :], AR[0][:, :], WRK[:, 3, 0:S], DK, ones, D, after)
        for k in range(DK):
            t = V.run(ve.scalar_tensor_tensor, dst[:, k, :], source[:, k, :], gain[:, k:k + 1], rinv[:, :],
                      ALU.mult, ALU.mult, after=[t])
            if shift is not None:
                A.run(ac.activation, dst[:, k, :], dst[:, k, :], ACT.Identity, bias=shift[:, k:k + 1], after=[t])
        return A.last() if shift is not None else t

    def in_blocks(tiles, b, k):
        return tiles[:, b * DK + k, :]

    def steps(n, body, per):
        full = n // R if n // R > 1 else 0
        if full:
            with nc.Fori(0, full) as i:
                for q, k in per.items():
                    q.enter(i, k * R)
                for u in range(R):
                    body(i, u)
                for q in per:
                    q.leave(full)
        for u in range(full * R, n):
            body(0, u)
        ring.g += n

    def project(n, rhs, evacuate, reader, per, first=0):
        base, c = reader.n, per[reader]

        def body(i, u):
            tiles, arrived, used = ring.slot(i, u)
            bank = u % 3
            if not isinstance(i, int) or u >= 3:
                T.wait((reader.sem, i * (R * c) + (base + c * (u - 2))))
            T.wait(arrived)
            for b in range(2):
                for k in range(DK):
                    last = mm(WRK[:, bank, b * S:(b + 1) * S], in_blocks(tiles, b, k), rhs[:, k, :], k == 0, k == DK - 1)
            last.then_inc(*used[:1], 1)
            evacuate(i * (2 * R) + 2 * (first + u), WRK[:, bank, :].rearrange("p (b t) -> p b t", b=2), used)

        steps(n, body, per)

    def to_proj(dst, off=0):
        def evacuate(block, bank, ready):
            A.run(ac.activation, dst[:, bass.ds(block + off, 2), :], bank, ACT.Copy, after=[ready])
        return evacuate

    def open_sums(after):
        T.wait(*after)
        for b in range(4):
            mm(ACC[:, b, :], zeros[:, 0:P], zeros[:, :], skip_group_check=True)

    def add_down(tiles, source):
        for kk in range(2):
            for m in range(DK):
                last = mm(ACC[:, m // 2, (m % 2) * S:(m % 2 + 1) * S], tiles[:, kk * DK + m, :], source(kk),
                          False, True, skip_group_check=True)
        return last

    def out_projection(n, source, after):
        open_sums(after)

        def body(i, u):
            tiles, arrived, used = ring.slot(i, u)
            T.wait(arrived)
            add_down(tiles, lambda kk: source[:, 2 * u + kk, :]).then_inc(used[0], 1)

        for u in range(n):
            body(0, u)
        ring.g += n
        return (ring.used, ring.g)

    def add_sums(dst, ready, gate=None):
        V.wait(ready)
        for m in range(DK):
            s = ACC[:, m // 2, (m % 2) * S:(m % 2 + 1) * S]
            if gate is None:
                V.run(ve.tensor_tensor, dst[:, m, :], s, dst[:, m, :], ALU.add)
            else:
                V.run(ve.scalar_tensor_tensor, dst[:, m, :], s, gate[:, m:m + 1], dst[:, m, :], ALU.mult, ALU.add)
        return V.last()

    def feed_forward(h, conv, after):
        hid = AR[1][:, 0:4 * S].rearrange("p (j t) -> p j t", t=S)
        open_sums(after)
        ca, cv = (2, 3) if conv is not None else (1, 1)
        base_v, base_u = V.n, ring.g

        def up(i, j, u):
            tiles, arrived, used = ring.slot(i, u)
            bank = WRK[:, j % 4, :]
            if not isinstance(i, int) or j >= 4:
                T.wait((V.sem, i * (4 * cv) + (base_v + cv * (j - 3))))
            T.wait(arrived)
            for b in range(2):
                for k in range(DK):
                    last = mm(bank[:, b * S:(b + 1) * S], in_blocks(tiles, b, k), h[:, k, :], k == 0, k == DK - 1)
            last.then_inc(used[0], 1)
            if not isinstance(i, int) or j >= 4:
                A.wait((ring.used, i * R + (base_u + 3 * ((j - 4) // 2) + 5)))
            gate, val, out = bank[:, 0:S], bank[:, S:2 * S], hid[:, j % 4, :]
            if conv is None:
                t = A.run(ac.activation, out, gate, ACT.Silu, after=[used])
            else:
                def col(tap):
                    at = VEC["ffn_conv"][0] + (conv * 3 + tap) * FB if tap < 3 else VEC["ffn_bias"][0] + conv * FB
                    return vec[:, bass.ds(i * 4 + (at + j), 1)]
                t = A.run(ac.activation, out, gate, ACT.Identity, scale=col(2), bias=col(3), after=[used])
                t = V.run(ve.scalar_tensor_tensor, out[:, 1:S], gate[:, 0:S - 1], col(1), out[:, 1:S],
                          ALU.mult, ALU.add, after=[t])
                t = V.run(ve.scalar_tensor_tensor, out[:, 2:S], gate[:, 0:S - 2], col(0), out[:, 2:S],
                          ALU.mult, ALU.add, after=[t])
                t = A.run(ac.activation, out, out, ACT.Silu, after=[t])
            V.run(ve.tensor_tensor, out, out, val, ALU.mult, after=[t])

        def down(i, p, u):
            tiles, arrived, used = ring.slot(i, u)
            T.wait(arrived, (V.sem, i * (4 * cv) + (base_v + cv * (2 * p + 2))))
            add_down(tiles, lambda kk: hid[:, (2 * p + kk) % 4, :]).then_inc(used[0], 1)

        up(0, 0, 0)
        up(0, 1, 1)
        ring.g += 2
        trips = (FB - 2) // 4
        v0, a0 = V.n, A.n
        with nc.Fori(0, trips) as i:
            V.enter(i, 4 * cv)
            A.enter(i, 4 * ca)
            for half in range(2):
                up(i, 2 + 2 * half, 3 * half)
                up(i, 3 + 2 * half, 3 * half + 1)
                down(i, half, 3 * half + 2)
            V.leave(trips)
            A.leave(trips)
        ring.g += trips * R
        down(0, FB // 2 - 1, 0)
        ring.g += 1
        return (ring.used, ring.g)

    def softmax_unit(scores, prob, n, nk, scale, stats, after, gate=None):
        mx, tot = stats[:, 0:n], stats[:, n:2 * n]
        t = V.run(ve.tensor_reduce, mx, scores, AX_X, ALU.max, after=after)
        t = V.run(ve.tensor_scalar, mx, mx, -scale, None, ALU.mult, after=[t])
        for h in range(n):
            t = A.run(ac.activation, prob[:, h, :], scores[:, h, :], ACT.Exp, bias=mx[:, h:h + 1], scale=scale,
                      accum_out=tot[:, h:h + 1], after=[t])
        t = V.run(ve.reciprocal, tot, tot, after=[t])
        if gate is not None:
            t = V.run(ve.tensor_tensor, tot, tot, gate, ALU.mult, after=[t])
        return V.run(ve.tensor_tensor, prob, prob, over_cols(tot, nk), ALU.mult, after=[t])

    def transpose_unit(dst, prob, n, kts, space, after, free):
        T.wait(*after)
        T.wait(*free)
        for h in range(n):
            for kt in range(kts):
                at = h * kts + kt
                last = te.transpose(space[:, at // 4, (at % 4) * P:(at % 4 + 1) * P],
                                    prob[:, h, kt * P:(kt + 1) * P], ident)
        t = T.done(last)
        nb = n * kts // 4
        return A.run(ac.activation, dst,
                     flat(space, 0, nb).rearrange("p (h k q) -> p h k q", h=n, k=kts), ACT.Copy, after=[t])

    def memory_attention(qm, layer):
        ev = everything()
        vtok = AR[2][:, 0:1024].rearrange("p (m h d) -> p m h d", m=TT2, h=MEMH)
        T.wait(*ev)
        for m in range(TT2):
            for h in range(MEMH):
                last = te.transpose(WRK[:, m, h * P:(h + 1) * P], KV[:, MEMH + h, m * P:(m + 1) * P], ident)
        t = A.run(ac.activation, AR[2][:, 0:1024], flat(WRK, 0, 2), ACT.Copy, after=[T.done(last)] + ev)
        PT = AR[1][:, :].rearrange("p (h m q) -> p h m q", h=MEMH, m=TT2)
        free = [t]
        moved = []
        for a in range(TT2):
            prob = heads(AR[0][:, a * 1024:(a + 1) * 1024], MEMH)
            sc = ACC[:, 2 * a:2 * a + 2, :]
            for h in range(MEMH):
                last = mm(ACC[:, 2 * a + h // 2, (h % 2) * S:(h % 2 + 1) * S], qm[:, h, a * P:(a + 1) * P], KV[:, h, :])
            t = softmax_unit(flat(ACC, 2 * a, 2 * a + 2).rearrange("p (h k) -> p h k", h=MEMH), prob, MEMH, S, SCALE,
                             tiny[:, 16 * a:16 * a + 8], [T.done(last)] + ev)
            t = transpose_unit(PT[:, :, :, a * P:(a + 1) * P], prob, MEMH, TT2, WRK[:, 0:2, :], [t], free)
            free = [t]
        T.wait(*free)
        for h in range(MEMH):
            for m in range(TT2):
                last = mm(WRK[:, 2 + h // 2, (h % 2) * S:(h % 2 + 1) * S], vtok[:, m, h, :], PT[:, h, m, :],
                          m == 0, m == TT2 - 1)
        return A.run(ac.activation, MIX[:, 8:12, :], flat(WRK, 2, 4).rearrange("p (h q) -> p h q", h=MEMH), ACT.Copy,
                     after=[T.done(last)])

    def memory_keys(layer):
        mem_n = AR[4][:, :].rearrange("p (k t) -> p k t", t=S)
        t = rms_norm(mem_n, SIDE, v_("mem_norm", layer * DK, DK), [loaded["side"]] + everything())
        T.wait(t)
        project(4, mem_n, to_proj(KV), A, {A: 1})
        return A.last()


    def gated_delta_mixer():
        H = AR[3][:, :].rearrange("p (k t) -> p k t", t=S)
        t = rms_norm(H, X, v_("norm_mix", 0, DK), [loaded["x"]] + everything())
        T.wait(t, loaded["small"])
        V.wait(loaded["small"])

        ba = tiny[:, 0:32].rearrange("p (t c) -> p t c", t=2)
        wba = s_("w_ba").rearrange("p (k c) -> p k c", c=16)
        for a in range(TT2):
            for k in range(DK):
                last = mm(WRK[:, 3, a * 16:(a + 1) * 16], H[:, k, a * P:(a + 1) * P], wba[:, k, :], k == 0, k == DK - 1)
        V.run(ve.tensor_copy, tiny[:, 0:32], WRK[:, 3, 0:32], after=[T.done(last)])

        def conv_silu(block, bank, ready):
            def tap(b, j):
                return vec[:, bass.ds(block + (b + VEC["gdn_conv"][0] + j * 3 * NH), 1)]

            def out(b, j=3):
                return PROJ[:, bass.ds(block + b, 1), 3 - j:S].rearrange("p a t -> p (a t)")

            for b in range(2):
                t = A.run(ac.activation, out(b), bank[:, b, :], ACT.Copy, scale=tap(b, 3), after=[ready])
            for b in range(2):
                for j in range(3):
                    t = V.run(ve.scalar_tensor_tensor, out(b, j), bank[:, b, 0:S - 3 + j], tap(b, j), out(b, j),
                              ALU.mult, ALU.add, after=[t])
                A.run(ac.activation, out(b), out(b), ACT.Silu, after=[t])

        project(12, H, conv_silu, V, {V: 6, A: 4})
        T.wait(*everything())
        project(6, H, to_proj(PROJ, 24), A, {A: 1})
        q, k, v, z = (PROJ[:, 8 * n:8 * n + 8, :] for n in range(4))

        ev = everything()
        for n, part in enumerate((q, k)):
            sq = AR[0][:, :]
            rt = AR[1][:, :]
            t = A.run(ac.activation, sq.rearrange("p (k t) -> p k t", t=S), part, ACT.Square, after=ev)
            T.wait(t, *ev)
            for b in range(4):
                last = mm(ACC[:, b, :], ones, sq[:, b * 512:(b + 1) * 512])
            t = A.run(ac.activation, rt, flat(ACC, 0, 4), ACT.Sqrt, bias=epsc[:, 0:1], after=[T.done(last)])
            t = V.run(ve.reciprocal, rt, rt, after=[t])
            t = V.run(ve.scalar_tensor_tensor, part, rt.rearrange("p (k t) -> p k t", t=S), SCALE if n == 0 else 1.0,
                      part, ALU.mult, ALU.mult, after=[t])
            ev = [t]

        beta = tiny[:, 32:48].rearrange("p (t h) -> p t h", t=2)
        g = tiny[:, 48:64].rearrange("p (t h) -> p t h", t=2)
        w0 = tiny[:, 64:80].rearrange("p (t h) -> p t h", t=2)
        w1 = tiny[:, 80:96].rearrange("p (t h) -> p t h", t=2)
        V.wait(loaded["rows"])
        A.wait(loaded["rows"])
        t = A.run(ac.activation, beta, ba[:, :, 0:8], ACT.Exp, scale=-1.0, after=ev)
        t = V.run(ve.tensor_scalar, beta, beta, 1.0, None, ALU.add, after=[t])
        t = V.run(ve.reciprocal, beta, beta, after=[t])
        t = V.run(ve.tensor_tensor, w0, ba[:, :, 8:16], over_rows(rows[:, 8:16], 2), ALU.add, after=[t])
        ta = A.run(ac.activation, w1, w0, ACT.Abs, after=[t])
        ta = A.run(ac.activation, w1, w1, ACT.Exp, scale=-1.0, after=[ta])
        ta = A.run(ac.activation, w1, w1, ACT.Ln, bias=epsc[:, 1:2], after=[ta])
        ea = A.run(ac.activation, rows[:, 0:8], rows[:, 0:8], ACT.Exp)
        t = V.run(ve.scalar_tensor_tensor, g, w0, 0.0, w1, ALU.max, ALU.add, after=[ta])
        t = V.run(ve.scalar_tensor_tensor, g, g, -1.0, over_rows(rows[:, 0:8], 2), ALU.mult, ALU.mult, after=[t, ea])

        T.wait(t)
        for a in range(TT2):
            mm(WRK[:, 0, a * 8:a * 8 + 8], c_("tri"), g[:, a, :])
            last = mm(WRK[:, 0, 16 + a * 8:24 + a * 8], c_("half"), g[:, a, :])
        gc = tiny[:, 96:112].rearrange("p (t h) -> p t h", t=2)
        gtot = tiny[:, 112:128].rearrange("p (t h) -> p t h", t=2)
        t = V.run(ve.tensor_copy, tiny[:, 96:128], WRK[:, 0, 0:32], after=[T.done(last)])
        bg = tiny[:, 128:144].rearrange("p (t h) -> p t h", t=2)
        kg = tiny[:, 144:160].rearrange("p (t h) -> p t h", t=2)
        ta = A.run(ac.activation, bg, gc, ACT.Exp, after=[t])
        V.run(ve.tensor_tensor, bg, bg, beta, ALU.mult, after=[ta])
        t = V.run(ve.tensor_tensor, kg, gtot, gc, ALU.subtract)
        small_done = A.run(ac.activation, kg, kg, ACT.Exp, after=[t])

        EA, EG, LT = AR[1], AR[2], AR[3]
        fre = everything()
        eg_done = []
        for a in range(TT2):
            work = heads(AR[0][:, a * 1024:(a + 1) * 1024])
            E = heads(EA[:, a * 1024:(a + 1) * 1024])
            G = heads(EG[:, a * 1024:(a + 1) * 1024])
            L = heads(LT[:, a * 1024:(a + 1) * 1024])
            tok = slice(a * P, (a + 1) * P)
            t = V.run(ve.tensor_tensor, work, over_rows(c_("tri")), over_cols(g[:, a, :]), ALU.mult, after=fre)
            T.wait(t, *fre)
            for b in range(2):
                last = mm(ACC[:, b, :], ones, AR[0][:, a * 1024 + b * 512:a * 1024 + (b + 1) * 512])
            t = T.done(last)
            gsum = flat(ACC, 0, 2).rearrange("p (h i) -> p h i", h=NH)
            te_ = A.run(ac.activation, G, gsum, ACT.Exp, after=[t])
            t = V.run(ve.tensor_tensor, E, gsum, over_cols(gc[:, a, :]), ALU.subtract, after=[te_])
            t = V.run(ve.tensor_tensor, E, E, over_rows(c_("neg")), ALU.add, after=[t])
            decayed = A.run(ac.activation, E, E, ACT.Exp, after=[t])
            t = V.run(ve.tensor_tensor, work, over_rows(ident), over_cols(beta[:, a, :]), ALU.mult, after=[t])
            T.wait(t)
            for b in range(2):
                mm(ACC[:, 2 + b, :], c_("before"), AR[0][:, a * 1024 + b * 512:a * 1024 + (b + 1) * 512])
            for h in range(NH):
                mm(WRK[:, h // 4, (h % 4) * P:(h % 4 + 1) * P], k[:, h, tok], k[:, h, tok])
            for h in range(NH):
                last = mm(WRK[:, 2 + h // 4, (h % 4) * P:(h % 4 + 1) * P], k[:, h, tok], q[:, h, tok])
            t = T.done(last)
            t = V.run(ve.tensor_tensor, L, flat(ACC, 2, 4).rearrange("p (h i) -> p h i", h=NH), E, ALU.mult, after=[t, decayed])
            V.run(ve.tensor_tensor, L, flat(WRK, 0, 2).rearrange("p (h i) -> p h i", h=NH), L, ALU.mult, after=[t])
            t = V.run(ve.tensor_tensor, E, flat(WRK, 2, 4).rearrange("p (h i) -> p h i", h=NH), E, ALU.mult)
            fre = [t, te_]
        AT = EA
        gl = tiny[:, 160:192].rearrange("p (n h) -> p n h", n=4)
        for a in range(TT2):
            G = heads(EG[:, a * 1024:(a + 1) * 1024])
            for r in range(2):
                V.run(ve.tensor_copy, gl[:, 2 * a + r, :], G[:, :, r * C + C - 1], after=fre)
            V.run(ve.tensor_tensor, q[:, :, a * P:(a + 1) * P], q[:, :, a * P:(a + 1) * P], G, ALU.mult, after=fre)

        TI, TTr, PM = AR[2], AR[4], AR[0]
        t = V.last()
        for a in range(TT2):
            V.run(ve.tensor_copy, heads(TI[:, a * 1024:(a + 1) * 1024]), over_rows(ident), after=[t])
            V.run(ve.tensor_copy, heads(TTr[:, a * 1024:(a + 1) * 1024]), over_rows(ident))
        T.wait(V.last())
        base = V.n
        per = 6
        with nc.Fori(0, 6) as lv:
            V.enter(lv, per)
            mask = cst[:, bass.ds(lv * P + CST["levels"][0], P)]
            for a in range(TT2):
                hs = [slice(a * 1024 + h * P, a * 1024 + (h + 1) * P) for h in range(NH)]
                bank = ACC if a == 0 else WRK
                T.wait((V.sem, lv * per + (base - 1 if a == 0 else base)))
                for h in range(NH):
                    last = mm(bank[:, h // 4, (h % 4) * P:(h % 4 + 1) * P], LT[:, hs[h]], TI[:, hs[h]])
                last.then_inc(T.sem, 1)
            for a in range(TT2):
                bank = ACC if a == 0 else WRK
                V.run(ve.tensor_tensor, heads(PM[:, a * 1024:(a + 1) * 1024]),
                      flat(bank, 0, 2).rearrange("p (h i) -> p h i", h=NH),
                      mask.unsqueeze(1).broadcast_to([P, NH, P]), ALU.mult, after=[(T.sem, lv * 4 + (T.n + 1 + a))])
            for a in range(TT2):
                hs = [slice(a * 1024 + h * P, a * 1024 + (h + 1) * P) for h in range(NH)]
                bank = ACC if a == 0 else WRK
                T.wait((V.sem, lv * per + (base + 1 + a)))
                for h in range(NH):
                    mm(bank[:, h // 4, (h % 4) * P:(h % 4 + 1) * P], TTr[:, hs[h]], PM[:, hs[h]])
                for h in range(NH):
                    last = mm(bank[:, 2 + h // 4, (h % 4) * P:(h % 4 + 1) * P], PM[:, hs[h]], TTr[:, hs[h]])
                last.then_inc(T.sem, 1)
            for a in range(TT2):
                bank = ACC if a == 0 else WRK
                for n, dst in enumerate((TI, TTr)):
                    part = dst[:, a * 1024:(a + 1) * 1024]
                    V.run(ve.tensor_tensor, part, part, flat(bank, 2 * n, 2 * n + 2), ALU.subtract,
                          after=[(T.sem, lv * 4 + (T.n + 3 + a))])
            V.leave(6)
        T.n += 24

        KB, KD, VB = AR[3], AR[2], AR[0]
        U = PROJ[:, 16:24, :].rearrange("p b t -> p (b t)")
        WT = PROJ[:, 8:16, :].rearrange("p b t -> p (b t)")
        done = V.last()
        T.wait(done)
        for a in range(TT2):
            tok = slice(a * P, (a + 1) * P)
            cols = slice(a * 1024, (a + 1) * 1024)
            if a:
                T.wait(V.last())
            for h in range(NH):
                te.transpose(ACC[:, h // 4, (h % 4) * P:(h % 4 + 1) * P], k[:, h, tok], ident)
            for h in range(NH):
                last = te.transpose(ACC[:, 2 + h // 4, (h % 4) * P:(h % 4 + 1) * P], v[:, h, tok], ident)
            t = T.done(last)
            kt = flat(ACC, 0, 2).rearrange("p (h i) -> p h i", h=NH)
            vt = flat(ACC, 2, 4).rearrange("p (h i) -> p h i", h=NH)
            V.run(ve.tensor_tensor, heads(KB[:, cols]), kt, over_cols(bg[:, a, :]), ALU.mult, after=[t, done])
            V.run(ve.tensor_tensor, heads(KD[:, cols]), kt, over_cols(kg[:, a, :]), ALU.mult, after=[small_done])
            V.run(ve.tensor_tensor, heads(VB[:, cols]), vt, over_cols(beta[:, a, :]), ALU.mult)
        T.wait(V.last())
        moved = []
        for a in range(TT2):
            hs = [slice(a * 1024 + h * P, a * 1024 + (h + 1) * P) for h in range(NH)]
            cols = slice(a * 1024, (a + 1) * 1024)
            bank = ACC if a == 0 else WRK
            for h in range(NH):
                mm(bank[:, h // 4, (h % 4) * P:(h % 4 + 1) * P], TTr[:, hs[h]], VB[:, hs[h]])
            for h in range(NH):
                last = mm(bank[:, 2 + h // 4, (h % 4) * P:(h % 4 + 1) * P], KB[:, hs[h]], TTr[:, hs[h]])
            t = T.done(last)
            V.run(ve.tensor_copy, U[:, cols], flat(bank, 0, 2), after=[t])
            A.run(ac.activation, WT[:, cols], flat(bank, 2, 4), ACT.Copy, after=[t])

        ready = [V.last(), A.last()]
        T.wait(*ready)
        state = STATE[:, :, :].rearrange("p h d -> p (h d)")
        for n in range(S // C):
            a, r = n // 2, n % 2
            rows_ = slice(r * C, (r + 1) * C)
            cols = slice(a * 1024, (a + 1) * 1024)
            hs = [slice(a * 1024 + h * P, a * 1024 + (h + 1) * P) for h in range(NH)]
            at = [slice(a * 1024 + h * P + r * C, a * 1024 + h * P + (r + 1) * C) for h in range(NH)]
            for h in range(NH):
                last = mm(WRK[rows_, h // 4, (h % 4) * P:(h % 4 + 1) * P], WT[:, at[h]], STATE[:, h, :])
            t = T.done(last)
            vn = VNEW[rows_, :, :].rearrange("p h d -> p (h d)")
            t = V.run(ve.tensor_tensor, vn, U[rows_, cols], WRK[rows_, 0:2, :].rearrange("p b c -> p (b c)"),
                      ALU.subtract, after=[t])
            for h in range(NH):
                mm(ACC[:, 2 + n % 2, h * C:(h + 1) * C], STATE[:, h, :], q[:, h, n * C:(n + 1) * C],
                   h == 0, True, skip_group_check=True)
            T.wait(t)
            for h in range(NH):
                last = mm(ACC[:, 2 + n % 2, h * C:(h + 1) * C], VNEW[rows_, h, :], AT[rows_, at[h]],
                          False, True, skip_group_check=True)
            out_t = T.done(last)
            if n < S // C - 1:
                for h in range(NH):
                    last = mm(ACC[:, h // 4, (h % 4) * P:(h % 4 + 1) * P], KD[rows_, hs[h]], VNEW[rows_, h, :])
                t = T.done(last)
                s1 = V.run(ve.tensor_tensor, STATE[:, :, :], STATE[:, :, :], over_cols(gl[:, n, :]), ALU.mult, after=[out_t])
                t = V.run(ve.tensor_tensor, state, flat(ACC, 0, 2), state, ALU.add, after=[t, s1])
            ob = A.run(ac.activation, MIX[:, 0:8, n * C:(n + 1) * C], heads(ACC[:, 2 + n % 2, :]), ACT.Copy, after=[out_t])
            T.wait(t, ob)

        ev = everything()
        o = MIX[:, 0:8, :]
        sq, rt = AR[0], AR[1]
        t = A.run(ac.activation, sq[:, :].rearrange("p (k t) -> p k t", t=S), o, ACT.Square, after=ev)
        T.wait(t)
        for b in range(4):
            last = mm(ACC[:, b, :], ones, sq[:, b * 512:(b + 1) * 512])
        t = A.run(ac.activation, rt[:, :], flat(ACC, 0, 4), ACT.Sqrt, scale=1.0 / P, bias=epsc[:, 0:1], after=[T.done(last)])
        tz = A.run(ac.activation, z, z, ACT.Silu)
        t = V.run(ve.reciprocal, rt[:, :], rt[:, :], after=[t])
        t = V.run(ve.scalar_tensor_tensor, o, o, v_("gdn_norm"), rt[:, :].rearrange("p (k t) -> p k t", t=S),
                  ALU.mult, ALU.mult, after=[t])
        V.run(ve.tensor_tensor, o, o, z, ALU.mult, after=[t, tz])


    def sparse_mixer():
        H = AR[3][:, :].rearrange("p (k t) -> p k t", t=S)
        t = rms_norm(H, X, v_("norm_mix", DK, DK), everything())
        T.wait(t, loaded["tab"], loaded["onehot"])
        last = mm(WRK[0:NH, 3, :], tab[0:BUCKETS + 1, :], onehot[0:BUCKETS + 1, :])
        line = AR[4][0:NH, 0:512]
        t = A.run(ac.activation, line, WRK[0:NH, 3, :], ACT.Copy, after=[T.done(last)])
        put, got = nc.alloc_semaphore("bias_line_stored"), nc.alloc_semaphore("bias_table_loaded")
        A.wait(t)
        nc.scalar.dma_start(scratch, line).then_inc(put, 16)
        nc.scalar.wait_ge(put, 16)
        table = PROJ[:, 24:36, :].rearrange("p b t -> p (b t)").rearrange("p (h y) -> p h y", h=NH)
        over = bass.AP(tensor=scratch.tensor, offset=0, ap=[[1, P], [512, NH], [1, 384]])
        nc.scalar.dma_start(table, over).then_inc(got, 16)
        wg = s_("w_gate").rearrange("p (k c) -> p k c", c=24)
        T.wait(t)
        for a in range(TT2):
            for k in range(DK):
                last = mm(WRK[:, 3, a * 24:(a + 1) * 24], H[:, k, a * P:(a + 1) * P], wg[:, k, :], k == 0, k == DK - 1)
        gates = tiny[:, 192:240].rearrange("p (t h c) -> p t h c", t=2, c=3)
        t = A.run(ac.activation, tiny[:, 192:240], WRK[:, 3, 0:48], ACT.Exp, scale=-1.0, after=[T.done(last)])
        t = V.run(ve.tensor_scalar, tiny[:, 192:240], tiny[:, 192:240], 1.0, None, ALU.add, after=[t])
        V.run(ve.reciprocal, tiny[:, 192:240], tiny[:, 192:240], after=[t])

        project(12, H, to_proj(PROJ), A, {A: 1})
        q, kvp, qm = PROJ[:, 0:8, :], PROJ[:, 8:20, :], PROJ[:, 20:24, :]
        ev = everything()
        qs = V.run(ve.tensor_scalar, q, q, SCALE, None, ALU.mult, after=ev)

        small_ = AR[2][:, 1024:2048]
        hidden = [small_[:, 0:30], small_[:, 32:62]]
        kcT = small_[:, 64:94].rearrange("p (g c) -> p g c", g=2)
        vc = small_[0:NCMP, 128:384].rearrange("p (g d) -> p g d", g=2)
        for n, (part, pos) in enumerate((("k", "pos_k"), ("v", "pos_v"))):
            blk = AR[n][:, 0:960].rearrange("p (l g c) -> p l g c", l=32, g=2)
            for g in range(2):
                for hl in range(2):
                    x = kvp[:, 2 * n + g, hl * 16:hl * 16 + 16 * NCMP].rearrange("p (c l) -> p l c", l=16)
                    V.run(ve.tensor_tensor, blk[:, hl * 16:(hl + 1) * 16, g, :], x,
                          v_(pos, hl * 16, 16).unsqueeze(2).broadcast_to([P, 16, NCMP]), ALU.add, after=ev)
        t = V.last()
        T.wait(t, *ev)
        for n in range(2):
            for s in range(2):
                tiles, arrived, used = ring.slot(0, 2 * n + s)
                T.wait(arrived)
                for l in range(16):
                    at = (s * 16 + l) * 30
                    last = mm(WRK[:, n, 0:30], tiles[:, l, :], AR[n][:, at:at + 30], s == 0 and l == 0, s == 1 and l == 15)
                last.then_inc(used[0], 1)
            A.run(ac.activation, hidden[n], WRK[:, n, 0:30], ACT.Silu, after=[used])
        ring.g += 4
        T.wait(A.last())
        mm(WRK[:, 2, 0:30], s_("w2_k"), hidden[0])
        for g in range(2):
            last = mm(WRK[0:NCMP, 3, g * P:(g + 1) * P], hidden[1][:, g * NCMP:(g + 1) * NCMP], s_("w2_v"))
        t = T.done(last)
        A.run(ac.activation, kcT, WRK[:, 2, 0:30].rearrange("p (g c) -> p g c", g=2), ACT.Copy, after=[t])
        cmp_done = A.run(ac.activation, vc, WRK[0:NCMP, 3, 0:S].rearrange("p (g d) -> p g d", g=2), ACT.Copy, after=[t])

        vtok = AR[2][:, 0:1024].rearrange("p (m j d) -> p m j d", m=TT2, j=4)
        T.wait(cmp_done)
        for m in range(TT2):
            for j in range(4):
                block = (6 if j < 2 else 10) + j % 2
                last = te.transpose(WRK[:, m, j * P:(j + 1) * P], kvp[:, block, m * P:(m + 1) * P], ident)
        vt_done = A.run(ac.activation, AR[2][:, 0:1024], flat(WRK, 0, 2), ACT.Copy, after=[T.done(last)])

        T.wait((got, 16), qs)
        flip = c_("flip")
        PCT = MIX[:, 0:8, :]
        pcT = AR[4][0:NCMP, :].rearrange("p (h q) -> p h q", h=NH)
        V.wait(vt_done)
        for a in range(TT2):
            pc = AR[3][:, a * 256:a * 256 + 120].rearrange("p (h c) -> p h c", h=NH)
            sc = WRK[:, 2, a * 128:a * 128 + 120].rearrange("p (h c) -> p h c", h=NH)
            y0 = 31 + P * (1 - a)
            mm(sc, flip, table[:, :, y0:y0 + 16 * (NCMP - 1) + 1:16], skip_group_check=True)
            for h in range(NH):
                last = mm(sc[:, h, :], q[:, h, a * P:(a + 1) * P], kcT[:, h // 4, :], False, True, skip_group_check=True)
            t = T.done(last)
            mx, tot = tiny[:, 256 + a * 16:264 + a * 16], tiny[:, 264 + a * 16:272 + a * 16]
            t = V.run(ve.tensor_reduce, mx, sc, AX_X, ALU.max, after=[t])
            t = V.run(ve.tensor_scalar, mx, mx, NEG / 10, None, ALU.max, after=[t])
            t = V.run(ve.tensor_tensor, pc, sc, over_cols(mx, NCMP), ALU.subtract, after=[t])
            t = A.run(ac.activation, pc, pc, ACT.Exp, after=[t])
            t = V.run(ve.tensor_reduce, tot, pc, AX_X, ALU.add, after=[t])
            t = V.run(ve.tensor_scalar, tot, tot, 1e-30, None, ALU.max, after=[t])
            t = V.run(ve.reciprocal, tot, tot, after=[t])
            t = V.run(ve.tensor_tensor, tot, tot, gates[:, a, :, 0], ALU.mult, after=[t])
            t = V.run(ve.tensor_tensor, pc, pc, over_cols(tot, NCMP), ALU.mult, after=[t])
            T.wait(t)
            for h in range(NH):
                last = te.transpose(WRK[0:NCMP, h // 4, (h % 4) * P:(h % 4 + 1) * P], pc[:, h, :], ident)
            t = A.run(ac.activation, pcT[:, :, a * P:(a + 1) * P],
                      WRK[0:NCMP, 0:2, :].rearrange("p b c -> p (b c)").rearrange("p (h q) -> p h q", h=NH), ACT.Copy,
                      after=[T.done(last)])
            T.wait(t)

        out = flat(ACC, 0, 4).rearrange("p (h q) -> p h q", h=NH)
        for b in range(4):
            mm(ACC[:, b, :], zeros[:, 0:P], zeros[:, :], skip_group_check=True)
        for h in range(NH):
            last = mm(out[:, h, :], vc[:, h // 4, :], pcT[:, h, :], False, True, skip_group_check=True)
        pc_done = T.done(last)
        free_bank = [A.last()]
        unit = 0
        pt_free = [pc_done]
        for j in range(4):
            kblock = (4 if j < 2 else 8) + j % 2
            br, g = j // 2, j % 2
            PTs = AR[1][:, :].rearrange("p (h m q) -> p h m q", h=4, m=TT2)
            for a in range(TT2):
                nk = (a + 1) * P
                prob = heads(AR[0][:, (unit % 2) * 1024:(unit % 2 + 1) * 1024], 4)[:, :, 0:nk]
                T.wait(*free_bank)
                sc = flat(WRK, 0, 2).rearrange("p (h k) -> p h k", h=4)[:, :, 0:nk]
                y0 = P * (1 - a)
                for b in range(2):
                    mm(sc[:, 2 * b:2 * b + 2, :], flip, table[:, g * 4 + 2 * b:g * 4 + 2 * b + 2, y0:y0 + nk],
                       skip_group_check=True)
                for h in range(4):
                    last = mm(sc[:, h, :], q[:, g * 4 + h, a * P:(a + 1) * P], kvp[:, kblock, 0:nk], False, True,
                              skip_group_check=True)
                st = T.done(last)
                t = softmax_unit(sc, prob, 4, nk, 1.0, tiny[:, 288 + 16 * (unit % 2):296 + 16 * (unit % 2)], [st],
                                 gate=gates[:, a, g * 4:g * 4 + 4, 1 + br])
                free_bank = [t]
                t = transpose_unit(PTs[:, :, 0:a + 1, a * P:(a + 1) * P], prob, 4, a + 1, WRK[:, 2:4, :], [t], pt_free)
                pt_free = [t]
                unit += 1
            T.wait(A.last())
            for h in range(4):
                mm(out[:, g * 4 + h, :], vtok[:, 0, j, :], PTs[:, h, 0, :], False, True, skip_group_check=True)
                last = mm(out[:, g * 4 + h, P:S], vtok[:, 1, j, :], PTs[:, h, 1, P:S], False, True, skip_group_check=True)
            pv = T.done(last)
            A.wait(pv)
        V.run(ve.tensor_copy, MIX[:, 0:4, :], out[:, 0:4, :], after=[pv])
        A.run(ac.activation, MIX[:, 4:8, :], out[:, 4:8, :], ACT.Copy, after=[pv])
        memory_attention(qm, 1)


    def modulation(layer):
        bank = WRK[:, 3, 0:2 * NMOD]
        T.wait(*everything())

        def body(i, u):
            tiles, arrived, used = ring.slot(i, u)
            T.wait(arrived)
            for b in range(2):
                for k in range(DK):
                    last = mm(WRK[:, 3, bass.ds(i * (4 * R) + (4 * u + 2 * b), 2)], in_blocks(tiles, b, k),
                              v_("cond", 2 * k, 2), k == 0, k == DK - 1)
            last.then_inc(used[0], 1)

        steps(NMOD // 2, body, {})
        a = VEC["b_mod"][0] + layer * NMOD
        V.run(ve.tensor_tensor, mod[layer][:, :, :], bank.rearrange("p (k w) -> p k w", w=2),
              over_cols(vec[:, a:a + NMOD], 2), ALU.add, after=[(ring.used, ring.g)])

    def modulate_gain(dst, layer, n, which, scale_at):
        return V.run(ve.scalar_tensor_tensor, dst[:, :], mod[layer][:, scale_at * DK:(scale_at + 1) * DK, which], 1.0,
                     v_("norm_g", (layer * 3 + n) * DK, DK), ALU.add, ALU.mult, after=[V.last()])

    def modulated(dst, source, layer, n, which, gain, rinv=None):
        shift_at = 3 * n
        modulate_gain(gain, layer, n, which, shift_at + 1)
        t = V.last()
        ev = everything()
        V.wait(t)
        return rms_norm(dst, source, gain, ev, mod[layer][:, shift_at * DK:(shift_at + 1) * DK, which], rinv)

    def half_ffn(stream, layer, n, which):
        h = AR[3][:, :].rearrange("p (k t) -> p k t", t=S)
        t = modulated(h, stream, layer, n, which, gainA)
        ready = feed_forward(h, None, [t] + everything())
        gate = tiny[:, 320:328]
        V.run(ve.tensor_scalar, gate, mod[layer][:, (3 * n + 2) * DK:(3 * n + 3) * DK, which], 0.5, None, ALU.mult,
              after=[ready])
        V.wait(V.last())
        add_sums(stream, ready, gate)

    def attention_and_pool():
        H = AR[3][:, :].rearrange("p (k t) -> p k t", t=S)
        HC = AR[4][:, :].rearrange("p (k t) -> p k t", t=S)
        modulated(HC, SIDE, 0, 1, 1, gainB, RINV2)
        modulated(H, X, 0, 1, 0, gainA)
        KK = PROJ[:, 4:8, :].rearrange("p b t -> p (b t)").rearrange("p (g t) -> p g t", g=2)
        VT = PROJ[:, 8:10, :].rearrange("p b t -> p (b t)")
        pool = PROJ[:, 10:14, :]
        T.wait(*everything())
        for s in range(6):
            tiles, arrived, used = ring.slot(0, s)
            T.wait(arrived)
            ev = [A.last()]
            A.wait(*ev)
            for b in range(2):
                if s == 5 and b == 1:
                    continue
                for w, h in enumerate((HC, H)):
                    if w == 0 and (s > 1 or (s == 1 and b == 1)):
                        continue
                    for k in range(DK):
                        last = mm(WRK[:, (s % 2) * 2 + b, w * S:(w + 1) * S], in_blocks(tiles, b, k), h[:, k, :],
                                  k == 0, k == DK - 1)
            last.then_inc(used[0], 1)
            for b in range(2):
                bank = WRK[:, (s % 2) * 2 + b, :]
                if s == 0:
                    A.run(ac.activation, KK[:, b, :], bank, ACT.Copy, after=[used])
                elif s == 1 and b == 0:
                    A.run(ac.activation, VT, bank, ACT.Copy, after=[used])
                elif s in (2, 3):
                    A.run(ac.activation, PROJ[:, 2 * (s - 2) + b, :], bank[:, S:2 * S], ACT.Copy, after=[used])
                elif not (s == 5 and b == 1):
                    A.run(ac.activation, pool[:, 0 if s == 1 else 2 * (s - 4) + 1 + b, :], bank[:, S:2 * S], ACT.Copy,
                          after=[used])
            T.wait(A.last())
        ring.g += 6
        ev = everything()

        sq, rt = AR[0], AR[1]
        for n in range(2):
            part = PROJ[:, 4 * n:4 * n + 4, :]
            t = A.run(ac.activation, sq[:, 0:1024].rearrange("p (k t) -> p k t", t=S), part, ACT.Square, after=ev)
            T.wait(t, *ev)
            for b in range(2):
                last = mm(WRK[:, b, :], c_("half"), sq[:, b * 512:(b + 1) * 512])
            t = A.run(ac.activation, rt[:, 0:1024], flat(WRK, 0, 2), ACT.Sqrt, scale=1.0 / C, bias=epsc[:, 0:1],
                      after=[T.done(last)])
            t = V.run(ve.reciprocal, rt[:, 0:1024], rt[:, 0:1024], after=[t])
            t = V.run(ve.scalar_tensor_tensor, part, part, v_("qk_norm", n, 1),
                      rt[:, 0:1024].rearrange("p (k t) -> p k t", t=S), ALU.mult, ALU.mult, after=[t])
            ev = [t]
        T.wait(*ev)
        for b in range(4):
            mm(WRK[:, b // 2, (b % 2) * S:(b % 2 + 1) * S], c_("rope"), PROJ[:, b, :])
        for g in range(2):
            last = mm(WRK[:, 2, g * S:(g + 1) * S], c_("rope"), KK[:, g, S:2 * S])
        t = T.done(last)
        swapped = flat(WRK, 0, 3).rearrange("p (b t) -> p b t", t=S)
        turn = sq[:, 0:1536].rearrange("p (b t) -> p b t", t=S)
        V.run(ve.tensor_tensor, turn, swapped, over_rows(c_("sin"), 6), ALU.mult, after=[t])
        for dst, part in ((PROJ[:, 0:4, :], turn[:, 0:4, :]), (KK[:, :, S:2 * S], turn[:, 4:6, :])):
            n = dst.shape[1]
            t = V.run(ve.tensor_tensor, dst, dst, over_rows(c_("cos"), n), ALU.mult, after=[V.last()])
            V.run(ve.tensor_tensor, dst, dst, part, ALU.add, after=[t])
        ev = everything()

        T.wait(*ev)
        for kt in range(4):
            last = te.transpose(WRK[:, 3, kt * P:(kt + 1) * P], VT[:, kt * P:(kt + 1) * P], ident)
        t = A.run(ac.activation, AR[2][:, 0:512], WRK[:, 3, :], ACT.Copy, after=[T.done(last)] + ev)
        vtok = AR[2][:, 0:512].rearrange("p (k d) -> p k d", k=4)
        PTs = PROJ[:, 14:30, :].rearrange("p b t -> p (b t)").rearrange("p (h k q) -> p h k q", h=4, k=4)
        T.wait(t)
        for g in range(2):
            for a in range(TT2):
                for h in range(4):
                    hh = g * 4 + h
                    part = slice((hh % 2) * C, (hh % 2 + 1) * C)
                    last = mm(ACC[:, h, :], PROJ[part, hh // 2, a * P:(a + 1) * P], KK[part, g, :])
                prob = heads(AR[0][:, :], 4)
                t = softmax_unit(ACC[:, :, :], prob, 4, 512, C ** -0.5, tiny[:, 336:344], [T.done(last)])
                t = transpose_unit(PTs[:, :, :, a * P:(a + 1) * P], prob, 4, 4, WRK[:, :, :], [t], [A.last()])
                T.wait(t)
            for h in range(4):
                hh = g * 4 + h
                part = slice((hh % 2) * C, (hh % 2 + 1) * C)
                for kt in range(4):
                    last = mm(WRK[part, h // 2, 0:S], vtok[:, kt, g * C:(g + 1) * C], PTs[:, h, kt, :],
                              kt == 0, kt == 3)
            t = A.run(ac.activation, MIX[:, 2 * g:2 * g + 2, :], WRK[:, 0:2, 0:S], ACT.Copy, after=[T.done(last)])
            T.wait(t)

        ev = everything()
        wide = S + 16
        pa = AR[0][:, 0:4 * wide].rearrange("p (g t) -> p g t", g=4)
        pb = AR[1][:, 0:4 * wide].rearrange("p (g t) -> p g t", g=4)
        V.run(ve.memset, pa, 0.0, after=ev)
        t = V.run(ve.memset, pb, 0.0)
        t = V.run(ve.tensor_copy, pa[:, :, 8:8 + S], pool, after=[t])
        t = V.run(ve.tensor_tensor, pb[:, :, 1:wide], pa[:, :, 0:wide - 1], pa[:, :, 1:wide], ALU.add, after=[t])
        t = V.run(ve.tensor_tensor, pa[:, 1:4, 1:wide - 1], pb[:, 1:4, 0:wide - 2], pb[:, 1:4, 2:wide], ALU.add, after=[t])
        t = V.run(ve.tensor_tensor, pb[:, 2:4, 2:wide - 2], pa[:, 2:4, 0:wide - 4], pa[:, 2:4, 4:wide], ALU.add, after=[t])
        t = V.run(ve.tensor_tensor, pa[:, 3:4, 4:wide - 4], pb[:, 3:4, 0:wide - 8], pb[:, 3:4, 8:wide], ALU.add, after=[t])
        cnt = c_("count").rearrange("p (g t) -> p g t", g=4)
        out = AR[2][:, 0:1024].rearrange("p (g t) -> p g t", g=4)
        for g, place in enumerate((pb, pa, pb, pa)):
            V.run(ve.tensor_tensor, out[:, g, :], place[:, g, 8:8 + S], cnt[:, g, :], ALU.mult, after=[t])
        t = V.run(ve.tensor_tensor, out, out, pool, ALU.subtract, after=[V.last()])
        T.wait(t)
        for g in range(4):
            last = mm(WRK[:, 2 + g // 2, (g % 2) * S:(g % 2 + 1) * S], s_("pool_w")[:, g * P:(g + 1) * P], out[:, g, :])
        t = T.done(last)
        for g in range(4):
            V.run(ve.tensor_scalar, MIX[:, 4 + g, :], WRK[:, 2 + g // 2, (g % 2) * S:(g % 2 + 1) * S],
                  v_("pool_scale", g, 1), None, ALU.mult, after=[t])
        ready = out_projection(4, MIX, everything())
        add_sums(X, ready, mod[0][:, 5 * DK:6 * DK, 0])

    def gmlp():
        H = AR[3][:, :].rearrange("p (k t) -> p k t", t=S)
        t = modulated(H, X, 1, 1, 0, gainA)
        T.wait(*everything())

        def gelu(block, bank, ready):
            A.run(ac.activation, PROJ[:, bass.ds(block, 2), :], bank, ACT.Gelu_apprx_tanh, after=[ready])

        project(8, H, gelu, A, {A: 1})
        u, v = PROJ[:, 0:8, :], PROJ[:, 8:16, :]
        VN = AR[4][:, :].rearrange("p (k t) -> p k t", t=S)
        t = rms_norm(VN, v, v_("v_norm"), everything())
        vtok = AR[1][:, :].rearrange("p (a g c) -> p a g c", a=2, g=NH)
        T.wait(t)
        for a in range(TT2):
            for g in range(NH):
                last = te.transpose(ACC[:, 2 * a + g // 4, (g % 4) * P:(g % 4 + 1) * P], VN[:, g, a * P:(a + 1) * P], ident)
        t = A.run(ac.activation, AR[1][:, :], flat(ACC, 0, 4), ACT.Copy, after=[T.done(last), V.last()])
        T.wait(t, loaded["bsp"])
        wsp = s_("w_sp").rearrange("p (g q) -> p g q", g=NH)
        for a in range(TT2):
            for g in range(NH):
                o = WRK[:, 2 * a + g // 4, (g % 4) * P:(g % 4 + 1) * P]
                mm(o, vtok[:, a, g, :], wsp[:, g, :], True, False)
                last = mm(o, ones[0:1, :], bsp[0:1, g * P:(g + 1) * P], False, True)
            t = T.done(last)
            V.run(ve.tensor_tensor, MIX[:, 0:8, a * P:(a + 1) * P],
                  flat(WRK, 2 * a, 2 * a + 2).rearrange("p (g t) -> p g t", g=NH), u[:, :, a * P:(a + 1) * P],
                  ALU.mult, after=[t])
        ready = out_projection(4, MIX, everything())
        add_sums(X, ready, mod[1][:, 5 * DK:6 * DK, 0])


    stream_from(R, NSLOT)

    H = AR[3][:, :].rearrange("p (k t) -> p k t", t=S)
    memory_keys(0)
    gated_delta_mixer()
    memory_attention(PROJ[:, 32:36, :], 0)
    add_sums(X, out_projection(6, MIX, everything()))
    t = rms_norm(H, X, v_("norm_ffn", 0, DK), everything())
    add_sums(X, feed_forward(H, 0, [t] + everything()))

    memory_keys(1)
    sparse_mixer()
    ev = everything()
    nc.scalar.wait_ge(A.sem, A.n)
    nc.scalar.wait_ge(T.sem, T.n)
    load_side = nc.alloc_semaphore("in_context")
    nc.scalar.dma_start(SIDE[:, :, :], src["ctx"]).then_inc(load_side, 16)
    add_sums(X, out_projection(6, MIX, everything()))
    t = rms_norm(H, X, v_("norm_ffn", DK, DK), everything())
    add_sums(X, feed_forward(H, 1, [t] + everything()))
    t = rms_norm(H, X, v_("final_norm"), everything())
    V.run(ve.tensor_copy, X[:, :, :], H, after=[t])

    t = A.run(ac.activation, v_("cond"), v_("cond"), ACT.Silu)
    T.wait(t)
    modulation(0)
    modulation(1)
    for q_ in (V, A):
        q_.wait((load_side, 16))
    half_ffn(SIDE, 0, 0, 1)
    half_ffn(X, 0, 0, 0)
    attention_and_pool()
    half_ffn(X, 0, 2, 0)
    half_ffn(X, 1, 0, 0)
    gmlp()
    half_ffn(X, 1, 2, 0)
    assert ring.g == NSLOT

    stored = nc.alloc_semaphore("out_stored")
    nc.sync.wait_ge(V.sem, V.n)
    nc.sync.dma_start(y_out, X[:, :, :]).then_inc(stored, 16)
    nc.sync.wait_ge(stored, 16)



def shape_constants():
    i = np.arange(P)
    same = (i[:, None] // C) == (i[None, :] // C)
    c = {}
    c["ident"] = np.eye(P)
    c["ones"] = np.ones((P, P))
    c["tri"] = (same & (i[:, None] <= i[None, :]))
    c["half"] = same
    c["neg"] = np.where(c["tri"], 0.0, NEG)
    c["before"] = same & (i[:, None] > i[None, :])
    c["flip"] = np.eye(P)[::-1]
    levels = []
    for s in (1, 2, 4, 8, 16, 32):
        block = (i[:, None] // (2 * s)) == (i[None, :] // (2 * s))
        levels.append(block & ((i[:, None] // s) % 2 == 1) & ((i[None, :] // s) % 2 == 0))
    c["levels"] = np.concatenate(levels, axis=1)
    rope = np.zeros((P, P))
    for m in range(P):
        if m % 32 < 16:
            rope[m + 16, m] = -1.0
        else:
            rope[m - 16, m] = 1.0
    c["rope"] = rope
    half = 32
    inv = (np.float32(10000.0) ** (-np.arange(0, half, 2, dtype=np.float32) / np.float32(half))).astype(np.float32)
    t = np.arange(S)
    axis = np.where(((i % C) // 32 == 0)[:, None], (t // 64)[None, :], (t % 64)[None, :]).astype(np.float32)
    ang = axis * inv[i % 16][:, None]
    c["cos"], c["sin"] = np.cos(ang), np.sin(ang)
    cnt = [1.0 / (np.clip(t + w // 2, 0, S) - np.clip(t - w // 2, 0, S)) for w in (2, 4, 8, 16)]
    c["count"] = np.broadcast_to(np.concatenate(cnt)[None, :], (P, 4 * S))
    out = np.zeros((P, NCST), np.float32)
    for name, (a, b) in CST.items():
        out[:, a:b] = c[name]
    dist = np.arange(S)
    exact = BUCKETS // 2
    logv = (np.log(np.maximum(dist, 1).astype(np.float32) / np.float32(exact)) / np.float32(math.log(128 / exact))).astype(np.float32)
    large = np.minimum(exact + (logv * np.float32(BUCKETS - exact)).astype(np.int32), BUCKETS - 1)
    bucket = np.where(dist < exact, dist, large)
    onehot = np.zeros((BUCKETS + 1, 512), np.float32)
    onehot[bucket, 255 - dist] = 1.0
    onehot[BUCKETS, 256:] = 1.0
    return out, onehot



def fm(x):
    x = np.asarray(x)
    return x.reshape(-1, P).T


def in_slots(w):
    n = w.shape[1] // 256
    return w.reshape(DK, P, n, 2, P).transpose(2, 1, 3, 0, 4).reshape(n, P, TILES * P)


def up_slots(w):
    return w.reshape(DK, P, 2, FB, P).transpose(3, 1, 2, 0, 4).reshape(FB, P, TILES * P)


def down_slots(w):
    return w.reshape(-1, 2, P, D).transpose(0, 2, 1, 3).reshape(-1, P, TILES * P)


def ffn_slots(up, down):
    u, d = up_slots(up), down_slots(down)
    order = [u[0:2]]
    for p in range(1, FB // 2):
        order += [u[2 * p:2 * p + 2], d[p - 1:p]]
    return np.concatenate(order + [d[FB // 2 - 1:]])


def kernel(**inputs):
    import concourse.bacc as bacc
    from concourse.bass_utils import run_bass_kernel_spmd

    g = {k: np.asarray(v) for k, v in inputs.items()}
    tokens = lambda x: np.ascontiguousarray(x.reshape(S, DK, P).transpose(2, 1, 0))
    gdn, nsa = g["gdn_w_in"][0], g["nsa_w_in"][0]
    wa = g["w_in_a_2"][0]
    k0, k1 = wa[:, 512:576], wa[:, 576:640]
    in_a = np.concatenate([k0, k0, k1, k1, wa[:, 640:768], wa[:, 768:896], wa[:, 0:512], wa[:, 896:1280],
                           np.zeros((D, P), np.float32)], axis=1)
    cmp_ = lambda w: w[0].reshape(2, 16, P, P).transpose(0, 2, 1, 3).reshape(2, P, TILES * P)
    parts = {
        "mem_kv0": in_slots(g["mem_w_kv"][0]),
        "gdn_in": in_slots(np.concatenate([gdn[:, :4096], gdn[:, 4112:]], axis=1)),
        "out0": down_slots(g["w_out"][0]),
        "ffn0": ffn_slots(g["ffn_w_up"][0], g["ffn_w_down"][0]),
        "mem_kv1": in_slots(g["mem_w_kv"][1]),
        "nsa_in": in_slots(np.concatenate([nsa[:, :2560], nsa[:, 2584:]], axis=1)),
        "cmp_k": cmp_(g["nsa_cmp_w1_k"]), "cmp_v": cmp_(g["nsa_cmp_w1_v"]),
        "out1": down_slots(g["w_out"][1]),
        "ffn1": ffn_slots(g["ffn_w_up"][1], g["ffn_w_down"][1]),
        "mod0": in_slots(g["w_mod_2"][0]), "mod1": in_slots(g["w_mod_2"][1]),
        "in_a": in_slots(in_a), "out_a": down_slots(g["w_out_a_2"][0]),
        "in_c": in_slots(g["w_in_c_2"][0]), "out_c": down_slots(g["w_out_c_2"][0]),
    }
    ff = {(i, j): ffn_slots(g["ffn_w13_2"][i, j], g["ffn_w2_2"][i, j]) for i in range(2) for j in range(2)}
    parts.update(ffn2c=ff[0, 0], ffn2=ff[0, 0], ffn3=ff[0, 1], ffn4=ff[1, 0], ffn5=ff[1, 1])
    weights = np.concatenate([parts[name] for name, _ in STREAM])

    v = {
        "norm_mix": fm(g["norm_mix_w"]), "norm_ffn": fm(g["norm_ffn_w"]), "final_norm": fm(g["final_norm_w"]),
        "mem_norm": fm(g["mem_norm_w"]), "gdn_conv": fm(g["gdn_conv_w"]), "gdn_norm": fm(g["gdn_norm_w"]),
        "ffn_conv": fm(g["ffn_conv_w"]), "ffn_bias": fm(g["ffn_conv_b"]),
        "pos_k": g["nsa_cmp_pos_k"][0].T, "pos_v": g["nsa_cmp_pos_v"][0].T,
        "b_mod": fm(g["b_mod_2"]), "norm_g": fm(g["norm_g_2"]),
        "qk_norm": np.concatenate([g["qk_norm_g_2"][0]] * 2, axis=1).T,
        "pool_scale": fm(g["pool_scale_2"]), "v_norm": fm(g["v_norm_g_2"]),
        "cond": np.stack([fm(g["c_2"]), fm(g["c_ctx_2"])], axis=2).reshape(P, 2 * DK),
    }
    kc = lambda w: w.reshape(DK, P, -1).transpose(1, 0, 2).reshape(P, -1)
    sm = {
        "w_ba": kc(gdn[:, 4096:4112]), "w_gate": kc(nsa[:, 2560:2584]),
        "w2_k": g["nsa_cmp_w2_k"][0], "w2_v": g["nsa_cmp_w2_v"][0],
        "pool_w": g["pool_w_2"][0].transpose(1, 0, 2).reshape(P, 4 * P),
        "w_sp": g["w_sp_2"][0].transpose(2, 0, 1).reshape(P, NH * P),
    }
    cst, onehot = shape_constants()
    arrays = {
        "x": tokens(g["x"]), "mem": tokens(g["mem"]), "ctx": tokens(g["ctx_2"]),
        "vec": np.concatenate([v[n] for n in VEC], axis=1), "small": np.concatenate([sm[n] for n in SMALL], axis=1),
        "cst": cst, "onehot": onehot, "rows": np.concatenate([g["gdn_a_log"][0], g["gdn_dt_bias"][0]]),
        "tab": g["rel_bias"], "bsp": g["b_sp_2"].reshape(-1), "weights": weights,
    }
    arrays = {k: np.ascontiguousarray(a) for k, a in arrays.items()}

    nc = bacc.Bacc("TRN2", target_bir_lowering=False, num_devices=1)
    aps = {k: nc.dram_tensor("in_" + k, a.shape, F32, kind="ExternalInput").ap() for k, a in arrays.items()}
    y = nc.dram_tensor("y", (P, DK, S), F32, kind="ExternalOutput").ap()
    scratch = nc.dram_tensor("bias_line", (NH, 512), F32, kind="Internal").ap()
    program(nc, aps, aps["weights"], y, scratch)
    r = run_bass_kernel_spmd(nc, [{"in_" + k: a for k, a in arrays.items()}], core_ids=[0])
    return r.results[0]["y"].transpose(2, 1, 0).reshape(1, S, D)
```

```python
import math

import numpy as np

import concourse.bass as bass
from concourse import mybir

F32 = mybir.dt.float32
F32R = mybir.dt.float32r
BF16 = mybir.dt.bfloat16
ALU = mybir.AluOpType
ACT = mybir.ActivationFunctionType
AX_X = mybir.AxisListType.X

P = 128
S = 256
D = 1024
DK = D // P
TT2 = S // P
NH = 8
C = 64
F = 2816
FB = F // P
MEMH = 4
NCMP = (S - 32) // 16 + 1
NMOD = 9 * DK
EPS = 1e-6
SCALE = P ** -0.5
NEG = -1e30
RAW = 3
PAIRS = 2
R = 6
MODS = 4
TILES = 16
BUCKETS = 32



def columns(parts):
    at, out = 0, {}
    for name, width in parts:
        out[name] = (at, at + width)
        at += width
    return out, at


VEC, NVEC = columns([
    ("norm_mix", 2 * DK), ("norm_ffn", 2 * DK), ("final_norm", DK), ("mem_norm", 2 * DK),
    ("gdn_conv", 4 * 3 * NH), ("gdn_norm", 1), ("ffn_conv", 2 * 3 * FB), ("ffn_bias", 2 * FB),
    ("pos_k", 32), ("pos_v", 32), ("b_mod", 2 * NMOD), ("norm_g", 6 * DK), ("qk_norm", 2),
    ("pool_scale", 4), ("v_norm", DK)])
SMALL, NSMALL = columns([
    ("w_ba", DK * 16), ("w_gate", DK * 24), ("w2_k", P), ("w2_v", P), ("pool_w", 4 * P)])
CST, NCST = columns([
    ("ident", P), ("ones", P), ("tri", P), ("half", P), ("neg", P), ("before", P), ("flip", P),
    ("levels", 6 * P), ("rope", P), ("cos", S), ("sin", S), ("count", 4 * S),
    ("pick", 31), ("pick_half", 30)])
STREAM = [("mem_kv0", 4), ("gdn_in", 18), ("out0", 6), ("ffn0", 33),
          ("mem_kv1", 4), ("nsa_in", 12), ("cmp_k", 2), ("cmp_v", 2), ("out1", 6), ("ffn1", 33),
          ("ffn2c", 33), ("ffn2", 33), ("in_ac", 2), ("in_a", 6), ("out_a", 4), ("ffn3", 33),
          ("ffn4", 33), ("in_c", 8), ("out_c", 4), ("ffn5", 33)]
NSLOT = sum(n for _, n in STREAM)



class Queue:

    def __init__(self, engine, sem, apart=None):
        self.engine, self.sem, self.n, self.i = engine, sem, 0, None
        self.seen, self.apart = {}, apart

    def wait(self, *ticks):
        for sem, value in ticks:
            if isinstance(value, int):
                if self.seen.get(sem.name, 0) >= value:
                    continue
                self.seen[sem.name] = value
            self.engine.wait_ge(sem, value)

    def done(self, instruction):
        instruction.then_inc(self.sem, 1)
        if self.i is None:
            self.n += 1
            return (self.sem, self.n)
        self.k += 1
        return (self.sem, self.i * self.per + (self.n + self.k))

    def run(self, op, *args, after=(), **kw):
        self.wait(*after)
        if self.apart is not None and self.i is not None:
            self.engine.sem_inc(self.apart, 1)
        return self.done(op(*args, **kw))

    def last(self):
        return (self.sem, self.n)

    def enter(self, i, per):
        self.i, self.per, self.k = i, per, 0

    def leave(self, times):
        assert self.k == self.per
        self.n += times * self.per
        self.i = None


class Ring:

    def __init__(self, raw, high, low, arrived, rounded, split, used):
        self.raw, self.high, self.low = raw, high, low
        self.arrived, self.rounded, self.split_, self.used = arrived, rounded, split, used
        self.g = 0

    def slot(self, i, u):
        at = self.g + u
        high, low = (x[:, at % PAIRS, :].rearrange("p (t c) -> p t c", c=P) for x in (self.high, self.low))
        return (high, low), (self.split_, i * R + (at + 1)), (self.used, i * R + (at + 1))

    def split(self, V, A, i, u, halves=(0, 1)):
        at = self.g + u
        if 0 in halves:
            A.wait((self.arrived[at % RAW], i * (16 * (R // RAW)) + 16 * (at // RAW + 1)))
            if not isinstance(i, int) or at >= PAIRS:
                A.wait((self.used, i * R + (at - PAIRS + 1)))
        n = TILES * P // 2
        for half in halves:
            cols = slice(half * n, (half + 1) * n)
            A.engine.activation(self.high[:, at % PAIRS, cols], self.raw[:, at % RAW, cols], ACT.Copy
                                ).then_inc(self.rounded, 1)
            V.wait((self.rounded, i * (2 * R) + (2 * at + 1 + half)))
            last = V.engine.tensor_tensor(self.low[:, at % PAIRS, cols], self.raw[:, at % RAW, cols],
                                          self.high[:, at % PAIRS, cols].bitcast(F32), ALU.subtract)
        if 1 in halves:
            last.then_inc(self.split_, 1)


def program(nc, src, weights, y_out, scratch):

    def sbuf(name, shape, dt=F32):
        return nc.alloc_sbuf_tensor(name, [P] + shape, dt)

    V = Queue(nc.vector, nc.alloc_semaphore("vector_done"))
    A = Queue(nc.scalar, nc.alloc_semaphore("scalar_done"), apart=nc.alloc_semaphore("apart"))
    T = Queue(nc.tensor, nc.alloc_semaphore("tensor_done"))
    ring = Ring(sbuf("raw", [RAW, TILES * P]), sbuf("high", [PAIRS, TILES * P], F32R),
                sbuf("low", [PAIRS, TILES * P], F32R), [nc.alloc_semaphore(f"arrived{r}") for r in range(RAW)],
                nc.alloc_semaphore("halves_rounded"), nc.alloc_semaphore("slots_split"),
                nc.alloc_semaphore("slots_used"))
    ve, ac, te = nc.vector, nc.scalar, nc.tensor

    X = sbuf("X", [DK, S])
    SIDE = sbuf("SIDE", [DK, S])
    at_proj = nc.sbuf_base
    PROJ = sbuf("PROJ", [36, S])
    MIX = sbuf("MIX", [12, S])
    KV = sbuf("KV", [DK, S])
    at_areas = nc.sbuf_base
    AR = [sbuf(f"AR{n}", [2048]) for n in range(5)]
    STATE = sbuf("STATE", [NH, P])
    VNEW = sbuf("VNEW", [NH, P])
    vec = sbuf("vec", [NVEC])
    small = sbuf("small", [NSMALL])
    cst = sbuf("cst", [NCST])
    rows = sbuf("rows", [16])
    tab = sbuf("tab", [NH])
    onehot = sbuf("onehot", [512])
    RINV = sbuf("RINV", [S])
    RINV2 = sbuf("RINV2", [S])
    zeros = sbuf("zeros", [512], BF16)
    epsc = sbuf("epsc", [4])
    mods = sbuf("mods", [2 * NMOD])
    modc = sbuf("modc", [5 * DK])
    gainA = sbuf("gainA", [DK])
    gainB = sbuf("gainB", [DK])
    tiny = sbuf("tiny", [512])
    XH, XL = (nc.alloc_sbuf_tensor_at(name, [P, 12, S], F32R, offset=at_areas + n * 12 * S * 4)
              for n, name in enumerate(("XH", "XL")))
    HIDH, HIDL = (nc.alloc_sbuf_tensor_at(name, [P, 4, S], F32R, offset=at_proj + n * 4 * S * 4)
                  for n, name in enumerate(("HIDH", "HIDL")))
    BH, BL = (nc.alloc_sbuf_tensor_at(name, [P, 2, 960], F32R, offset=at_areas + n * 2 * 1024 * 4)
              for n, name in enumerate(("BH", "BL")))
    MRING = nc.alloc_sbuf_tensor_at("MRING", [P, MODS, D], F32, offset=at_proj + 8 * S * 4)
    ACC = nc.alloc_psum_tensor("ACC", [P, 4, 512], F32)
    WRK = nc.alloc_psum_tensor("WRK", [P, 4, 512], F32)

    def v_(name, k=0, n=None):
        a, b = VEC[name]
        return vec[:, a + k:(a + k + n if n else b)]

    def s_(name):
        return small[:, SMALL[name][0]:SMALL[name][1]]

    def c_(name):
        return cst[:, CST[name][0]:CST[name][1]]

    ident, ones = c_("ident"), c_("ones")

    def heads(ap, h=NH):
        return ap.rearrange("p (h i) -> p h i", h=h)

    def over_rows(ap, h=NH):
        return ap.unsqueeze(1).broadcast_to([ap.shape[0], h, ap.shape[1]])

    def over_cols(ap, n=P):
        return ap.unsqueeze(2).broadcast_to([ap.shape[0], ap.shape[1], n])

    def flat(ps, a, b):
        return ps[:, a:b, :].rearrange("p b c -> p (b c)")

    def everything():
        return [V.last(), A.last(), T.last(), (ring.used, ring.g)]

    loaded = {}

    def load(name, dst, source):
        loaded[name] = (nc.alloc_semaphore("load_" + name), 16)
        nc.sync.dma_start(dst, source).then_inc(loaded[name][0], 16)

    load("side", SIDE[:, :, :], src["mem"])
    load("vec", vec[:, :], src["vec"])
    load("cst", cst[:, :], src["cst"])

    def fill(n):
        nc.sync.dma_start(ring.raw[:, n % RAW, :], weights[n % NSLOT, :, :]).then_inc(ring.arrived[n % RAW], 16)

    for n in range(RAW):
        fill(n)
        if n == 1:
            load("x", X[:, :, :], src["x"])
            load("small", small[:, :], src["small"])
            load("rows", rows[:, :], src["rows"].partition_broadcast(P))
            load("tab", tab[0:BUCKETS, :], src["tab"])
            load("onehot", onehot[0:BUCKETS + 1, :], src["onehot"])

    def stream_from(n0, n1):
        full = (n1 - n0) // R
        with nc.sync.Fori(0, full) as i:
            for u in range(R):
                nc.sync.wait_ge(ring.split_, i * R + (n0 + u - RAW + 1))
                nc.sync.dma_start(ring.raw[:, (n0 + u) % RAW, :],
                                  weights[bass.ds(i * R + (n0 + u), 1), :, :].rearrange("a p n -> p (a n)")
                                  ).then_inc(ring.arrived[(n0 + u) % RAW], 16)
        for n in range(n0 + full * R, n1):
            nc.sync.wait_ge(ring.split_, n - RAW + 1)
            fill(n)

    V.run(ve.memset, zeros[:, :], 0.0)
    V.run(ve.memset, epsc[:, 0:1], EPS)
    V.run(ve.memset, epsc[:, 1:4], 1.0)
    V.run(ve.memset, STATE[:, :, :], 0.0)
    V.run(ve.memset, tab[BUCKETS:BUCKETS + 1, :], NEG)
    made = V.last()
    for q in (V, A, T):
        q.wait(made, loaded["vec"], loaded["cst"])


    def mm(out, lhsT, rhs, start=True, stop=True, **kw):
        return te.matmul(out, lhsT, rhs, start=start, stop=stop, **kw)

    def mm3(out, parts, tile, xh, xl, start, stop, **kw):
        high, low = parts
        mm(out, high[:, tile, :], xh, start, False, **kw)
        mm(out, high[:, tile, :], xl, False, False, **kw)
        return mm(out, low[:, tile, :], xh, False, stop, **kw)

    def next_split(i, u):
        at = ring.g + u + PAIRS
        if not isinstance(i, int) or at <= NSLOT:
            ring.split(V, A, i, u + PAIRS)

    owed = []

    def later_split():
        if ring.g + PAIRS - 1 <= NSLOT:
            owed.extend([0, 1])

    def owed_split(n):
        for half in owed[:n]:
            ring.split(V, A, 0, PAIRS - 1, (half,))
        del owed[:n]

    def root_table():
        A.run(ac.activation, epsc[:, 2:3], epsc[:, 3:4], ACT.Sqrt)

    def root_mean_square(dst, source, after, blocks=None):
        sq = AR[4][:, :].rearrange("p (k t) -> p k t", t=S)
        sums = WRK[:, 3, 0:S]
        A.wait(*after)
        V.wait(*after)
        T.wait(*after)
        for k in range(DK):
            t = A.run(ac.activation, sq[:, k, :], source[:, k, :], ACT.Square, after=[blocks[k]] if blocks else ())
            if k % 2:
                T.wait(V.run(ve.tensor_tensor, sq[:, k, :], sq[:, k - 1, :], sq[:, k, :], ALU.add, after=[t]))
                last = mm(sums, ones, sq[:, k, :], k == 1, k == DK - 1)
        t = T.done(last)
        owed_split(1)
        t = A.run(ac.activation, dst, sums, ACT.Sqrt, scale=1.0 / D, bias=epsc[:, 0:1], after=[t])
        return V.run(ve.reciprocal, dst, dst, after=[t])

    def rms_norm(dst, source, gain, after, shift=None, parts=True, blocks=None):
        t = root_mean_square(RINV[:, :], source, after, blocks)
        ready = normed(dst, source, gain, RINV, t, shift, parts)
        owed_split(1)
        return ready

    def normed(dst, source, gain, rinv, t, shift=None, parts=True):
        ready = []

        def low_part(k, t):
            ready.append(V.run(ve.scalar_tensor_tensor, XL[:, k, :], dst[:, k, :],
                               0.0 if shift is None else shift[:, k:k + 1], XH[:, k, :].bitcast(F32),
                               ALU.add, ALU.subtract, after=[t]))

        for k in range(DK):
            t = V.run(ve.scalar_tensor_tensor, dst[:, k, :], source[:, k, :], gain[:, k:k + 1], rinv[:, :],
                      ALU.mult, ALU.mult, after=[t] if k == 0 else ())
            if not parts:
                ready.append(t)
                continue
            if k:
                low_part(k - 1, high)
            if shift is None:
                high = A.run(ac.activation, XH[:, k, :], dst[:, k, :], ACT.Copy, after=[t])
            else:
                high = A.run(ac.activation, XH[:, k, :], dst[:, k, :], ACT.Identity, bias=shift[:, k:k + 1], after=[t])
        if parts:
            low_part(DK - 1, high)
        return ready

    def head_norm(blocks, half, divisor, factor, after):
        n = 4 * len(blocks)
        sq = [AR[p // 2][:, (p % 2) * 1024:(p % 2 + 1) * 1024].rearrange("p (k t) -> p k t", t=S) for p in range(4)]
        sel = AR[3][0:16, :].rearrange("p (h c) -> p h c", c=C if half else P)
        made = V.run(ve.tensor_copy, sel[:, 0:16, :], over_cols(ident[0:16, 0:16], C if half else P), after=after)
        sums = WRK[0:16, 3, 0:S]
        T.wait(*after)
        for p, piece in enumerate(blocks):
            t = A.run(ac.activation, sq[p], piece, ACT.Square, after=after)
            T.wait(t)
            for k in range(4):
                b = 4 * p + k
                pick = c_("pick_half")[:, 14 - 2 * b:30 - 2 * b] if half else c_("pick")[:, 15 - b:31 - b]
                last = mm(sums, pick, sq[p][:, k, :], b == 0, b == n - 1)
        r = RINV[0:16, :]
        t = A.run(ac.activation, r, sums, ACT.Sqrt, scale=1.0 / divisor, bias=epsc[0:16, 0:1], after=[T.done(last)])
        t = V.run(ve.reciprocal, r, r, after=[t, made])
        T.wait(t)
        sel = AR[3][0:16, :].rearrange("p (b c) -> p b c", c=P)
        for p, piece in enumerate(blocks):
            space = (ACC if p < 2 else WRK)[:, 2 * (p % 2):2 * (p % 2) + 2, :]
            for k in range(4):
                last = mm(space[:, k // 2, (k % 2) * S:(k % 2 + 1) * S], sel[:, 4 * p + k, :], r)
            t = T.done(last)
            V.wait(t)
            factor(p, piece, space.rearrange("p b (k t) -> p (b k) t", t=S))
        return V.last()

    def steps(n, body, per):
        full = n // R if n // R > 1 else 0
        if full:
            with nc.Fori(0, full) as i:
                for q, k in per.items():
                    q.enter(i, k * R)
                for u in range(R):
                    body(i, u)
                for q in per:
                    q.leave(full)
        for u in range(full * R, n):
            body(0, u)
        ring.g += n

    def project(n, evacuate, reader, per, ready=(), banks=()):
        base, c = reader.n, per[reader]

        def body(i, u):
            parts, made, used = ring.slot(i, u)
            bank = u % 3
            if isinstance(i, int) and u < 3:
                T.wait(*banks[u:u + 1])
            else:
                T.wait((reader.sem, i * (R * c) + (base + c * (u - 2))))
            T.wait(made)
            for b in range(2):
                for k in range(DK):
                    if u == 0 and b == 0:
                        T.wait(*ready[k:k + 1])
                    last = mm3(WRK[:, bank, b * S:(b + 1) * S], parts, b * DK + k, XH[:, k, :], XL[:, k, :],
                               k == 0, k == DK - 1)
            last.then_inc(used[0], 1)
            evacuate(i, u, WRK[:, bank, :].rearrange("p (b t) -> p b t", b=2), used)

        steps(n, body, per)
        return [(reader.sem, max(base + c * max(m + 1, 0), 0)) for m in range(n - 3, n)] if n % 3 == 0 else None

    def to_proj(dst, off=0):
        def evacuate(i, u, bank, ready):
            next_split(i, u)
            A.run(ac.activation, dst[:, bass.ds(i * (2 * R) + (2 * u + off), 2), :], bank, ACT.Copy, after=[ready])
        return evacuate

    def open_sums(after):
        T.wait(*after)
        for b in range(4):
            mm(ACC[:, b, :], zeros[:, 0:P], zeros[:, :], skip_group_check=True)

    def add_down(parts, source):
        for kk in range(2):
            for m in range(DK):
                last = mm3(ACC[:, m // 2, (m % 2) * S:(m % 2 + 1) * S], parts, kk * DK + m, *source(kk),
                           False, True, skip_group_check=True)
        return last

    def last_down(parts, source, used):
        ticks = []
        for m in range(DK):
            for kk in range(2):
                last = mm3(ACC[:, m // 2, (m % 2) * S:(m % 2 + 1) * S], parts, kk * DK + m, *source(kk),
                           False, True, skip_group_check=True)
            if m % 2 and m < DK - 1:
                ticks.append(T.done(last))
        last.then_inc(used[0], 1)
        return ticks + [used]

    def out_projection(n, after):
        open_sums(after)
        V.wait(*after)
        A.wait(*after)
        for k in range(n):
            two = slice(2 * k, 2 * k + 2)
            t = A.run(ac.activation, XH[:, two, :], MIX[:, two, :], ACT.Copy)
            V.run(ve.tensor_tensor, XL[:, two, :], MIX[:, two, :], XH[:, two, :].bitcast(F32), ALU.subtract, after=[t])
        first = V.n - n
        root_table()
        for u in range(n):
            parts, made, used = ring.slot(0, u)
            T.wait(made, (V.sem, first + u + 1))
            source = lambda kk: (XH[:, 2 * u + kk, :], XL[:, 2 * u + kk, :])
            if u < n - 1:
                add_down(parts, source).then_inc(used[0], 1)
                next_split(0, u)
        ring.g += n
        ticks = last_down(parts, source, used)
        later_split()
        return ticks

    def add_sums(dst, ready, gate=None):
        for m in range(DK):
            V.wait(ready[m // 2])
            s = ACC[:, m // 2, (m % 2) * S:(m % 2 + 1) * S]
            if gate is None:
                V.run(ve.tensor_tensor, dst[:, m, :], s, dst[:, m, :], ALU.add)
            else:
                V.run(ve.scalar_tensor_tensor, dst[:, m, :], s, gate[:, m:m + 1], dst[:, m, :], ALU.mult, ALU.add)
        return [(V.sem, V.n - DK + 1 + m) for m in range(DK)]

    def feed_forward(conv, after, vectors=(), ready=(), beside=None):
        hid = AR[3][:, 0:4 * S].rearrange("p (j t) -> p j t", t=S)
        V.wait(*after)
        A.wait(*after)
        ca, cv = (3, 4) if conv is not None else (2, 2)
        base_v, base_u = V.n, ring.g
        trips = (FB - 2) // 4
        if vectors:
            modulation_loads(vectors, trips, after)

        def up(i, j, u):
            parts, made, used = ring.slot(i, u)
            bank = WRK[:, j % 4, :]
            if not isinstance(i, int) or j >= 4:
                T.wait((V.sem, i * (4 * cv) + (base_v + cv * (j - 3))))
            T.wait(made)
            for b in range(2):
                for k in range(DK):
                    if isinstance(i, int) and j == 0 and b == 0:
                        T.wait(*ready[k:k + 1])
                    last = mm3(bank[:, b * S:(b + 1) * S], parts, b * DK + k, XH[:, k, :], XL[:, k, :],
                               k == 0, k == DK - 1)
            last.then_inc(used[0], 1)
            gate, out = bank[:, 0:S], hid[:, j % 4, :]
            if conv is None:
                next_split(i, u)
                t = A.run(ac.activation, out, gate, ACT.Silu, after=[used])
                parts_of(i, j, by_value(j, t))
            else:
                if j:
                    t = by_value(j - 1, silu(i, j - 1))
                next_split(i, u)
                if j:
                    parts_of(i, j - 1, t)

                def col(tap):
                    at = VEC["ffn_conv"][0] + (conv * 3 + tap) * FB if tap < 3 else VEC["ffn_bias"][0] + conv * FB
                    return vec[:, bass.ds(i * 4 + (at + j), 1)]
                t = A.run(ac.activation, out, gate, ACT.Identity, scale=col(2), bias=col(3), after=[used])
                t = V.run(ve.scalar_tensor_tensor, out[:, 1:S], gate[:, 0:S - 1], col(1), out[:, 1:S],
                          ALU.mult, ALU.add, after=[t])
                V.run(ve.scalar_tensor_tensor, out[:, 2:S], gate[:, 0:S - 2], col(0), out[:, 2:S],
                      ALU.mult, ALU.add, after=[t])

        def silu(i, j):
            out = hid[:, j % 4, :]
            return A.run(ac.activation, out, out, ACT.Silu, after=[(V.sem, i * (4 * cv) + (base_v + cv * j + 2))])

        def by_value(j, t):
            out = hid[:, j % 4, :]
            return V.run(ve.tensor_tensor, out, out, WRK[:, j % 4, S:2 * S], ALU.mult, after=[t])

        def parts_of(i, j, t):
            out = hid[:, j % 4, :]
            if not isinstance(i, int) or i or j >= 4:
                A.wait((ring.used, i * R + (base_u + 3 * ((j - 4) // 2) + 5)))
            t = A.run(ac.activation, HIDH[:, j % 4, :], out, ACT.Copy, after=[t])
            V.run(ve.tensor_tensor, HIDL[:, j % 4, :], out, HIDH[:, j % 4, :].bitcast(F32), ALU.subtract, after=[t])

        def down(i, p, u):
            parts, made, used = ring.slot(i, u)
            T.wait(made, (V.sem, i * (4 * cv) + (base_v + cv * (2 * p + 2))))
            add_down(parts, lambda kk: (HIDH[:, (2 * p + kk) % 4, :], HIDL[:, (2 * p + kk) % 4, :])
                     ).then_inc(used[0], 1)
            next_split(i, u)

        up(0, 0, 0)
        up(0, 1, 1)
        ring.g += 2
        open_sums(after)
        with nc.Fori(0, trips) as i:
            V.enter(i, 4 * cv)
            A.enter(i, 4 * ca)
            for half in range(2):
                for j in range(2):
                    up(i, 2 + 2 * half + j, 3 * half + j)
                    if vectors:
                        modulation_products(vectors, i, 2 * half + j)
                down(i, half, 3 * half + 2)
            V.leave(trips)
            A.leave(trips)
        ring.g += trips * R
        if conv is not None:
            parts_of(trips, 1, by_value(1, silu(trips, 1)))
        if vectors:
            modulation_rest(vectors, trips)
        if beside is not None:
            beside()
        if conv is not None or not beside:
            root_table()
        parts, made, used = ring.slot(0, 0)
        T.wait(made, (V.sem, base_v + cv * FB))
        ticks = last_down(parts, lambda kk: (HIDH[:, (FB - 2 + kk) % 4, :], HIDL[:, (FB - 2 + kk) % 4, :]), used)
        ring.g += 1
        later_split()
        if beside is not None:
            owed_split(2)
        return ticks

    mod_used = nc.alloc_semaphore("mod_blocks_used")
    mod_arrived = [nc.alloc_semaphore(f"mod_arrived{r}") for r in range(MODS)]
    taken = [0]
    COND = {"c": VNEW[:, :, :].rearrange("p h d -> p (h d)"), "c_ctx": STATE[:, :, :].rearrange("p h d -> p (h d)")}

    def modulation_loads(vectors, trips, after):
        each, first, rest = vectors[0:3]
        n, g = each * trips + rest, taken[0]
        G = Queue(nc.gpsimd, None)
        G.wait(*after)

        def fetch(i, u):
            if not isinstance(i, int) or g + u >= MODS:
                nc.gpsimd.wait_ge(mod_used, i * MODS + (g + u - MODS + 1))
            nc.gpsimd.dma_start(MRING[:, (g + u) % MODS, :],
                                src["wmod"][bass.ds(i * MODS + (first + u), 1), :, :].rearrange("a p k -> p (a k)")
                                ).then_inc(mod_arrived[(g + u) % MODS], 16)

        for u in range(MODS):
            fetch(0, u)
        with nc.gpsimd.Fori(0, n // MODS - 1) as i:
            for u in range(MODS):
                fetch(i, u + MODS)
        assert n % MODS == 0

    def modulation_block(vectors, i, per_trip, u):
        what, dst = vectors[3:5]
        g = taken[0] + u
        V.wait((mod_arrived[g % MODS], i * (16 * per_trip // MODS) + 16 * (g // MODS + 1)))
        at = vectors[1] + u
        ve.scalar_tensor_tensor(MRING[:, g % MODS, :], MRING[:, g % MODS, :], 1.0, COND[what], ALU.mult, ALU.mult,
                                accum_out=dst[:, bass.ds(i * per_trip + at, 1)]).then_inc(mod_used, 1)

    def modulation_products(vectors, i, quarter):
        each = vectors[0]
        assert each % MODS == 0
        for b in range(each // 4):
            modulation_block(vectors, i, each, quarter * (each // 4) + b)

    def modulation_rest(vectors, trips):
        each, _, rest = vectors[0:3]
        for u in range(rest):
            modulation_block(vectors, 0, 0, each * trips + u)
        taken[0] += each * trips + rest

    def attend(units):
        copied, weighted = [], []
        for n in range(len(units) + 2):
            if n >= 2:
                T.wait(copied[n - 2])
                if units[n - 2]["values"]:
                    units[n - 2]["values"]()
            if n < len(units):
                scored = units[n]["scores"]()
            if 1 <= n <= len(units):
                u = units[n - 1]
                prob, space = u["prob"], u["space"]
                count, nk = prob.shape[1:3]
                tot = u["stats"][:, count:2 * count]
                t = V.run(ve.reciprocal, tot, tot, after=[weighted[n - 1]])
                if u["gate"] is not None:
                    t = V.run(ve.tensor_tensor, tot, tot, u["gate"], ALU.mult, after=[t])
                t = V.run(ve.tensor_tensor, prob, prob, over_cols(tot, nk), ALU.mult, after=[t])
                T.wait(t)
                kts = nk // P
                for h in range(count):
                    for kt in range(kts):
                        at = h * kts + kt
                        last = te.transpose(space[:, at // 4, (at % 4) * P:(at % 4 + 1) * P],
                                            prob[:, h, kt * P:(kt + 1) * P], ident)
                copied.append(A.run(ac.activation, u["turned"],
                                    flat(space, 0, count * kts // 4).rearrange("p (h k q) -> p h k q", h=count, k=kts),
                                    ACT.Copy, after=[T.done(last)]))
            if n < len(units):
                u = units[n]
                view, prob = u["view"], u["prob"]
                count = view.shape[1]
                mx, tot = u["stats"][:, 0:count], u["stats"][:, count:2 * count]
                t = V.run(ve.tensor_reduce, mx, view, AX_X, ALU.max, after=[scored])
                t = V.run(ve.tensor_scalar, mx, mx, -u["scale"], None, ALU.mult, after=[t])
                for h in range(count):
                    t = A.run(ac.activation, prob[:, h, :], view[:, h, :], ACT.Exp, bias=mx[:, h:h + 1],
                              scale=u["scale"], accum_out=tot[:, h:h + 1], after=[t])
                weighted.append(t)

    def memory_units(qm):
        vtok = MIX[:, 8:12, :].rearrange("p b t -> p (b t)").rearrange("p (m h d) -> p m h d", m=TT2, h=MEMH)
        PT = AR[1][:, :].rearrange("p (h m q) -> p h m q", h=MEMH, m=TT2)

        def unit(a):
            space = WRK[:, 2 * a:2 * a + 2, :]

            def scores():
                for h in range(MEMH):
                    last = mm(space[:, h // 2, (h % 2) * S:(h % 2 + 1) * S], qm[h][:, a * P:(a + 1) * P], KV[:, h, :])
                return T.done(last)

            def values():
                T.wait(V.last())
                for h in range(MEMH):
                    for m in range(TT2):
                        last = mm(ACC[:, h // 2, (h % 2) * S:(h % 2 + 1) * S], vtok[:, m, h, :], PT[:, h, m, :],
                                  m == 0, m == TT2 - 1)
                A.run(ac.activation, MIX[:, 8:12, :], flat(ACC, 0, 2).rearrange("p (h q) -> p h q", h=MEMH), ACT.Copy,
                      after=[T.done(last)])

            return dict(scores=scores, space=space, view=flat(space, 0, 2).rearrange("p (h k) -> p h k", h=MEMH),
                        prob=heads(AR[0][:, a * 1024:(a + 1) * 1024], MEMH), stats=tiny[:, 288 + 16 * a:304 + 16 * a],
                        scale=SCALE, gate=None, turned=PT[:, :, :, a * P:(a + 1) * P], values=values if a else None)

        return [unit(a) for a in range(TT2)]

    def memory_keys(layer):
        mem_n = AR[3][:, :].rearrange("p (k t) -> p k t", t=S)
        t = rms_norm(mem_n, SIDE, v_("mem_norm", layer * DK, DK), [loaded["side"]] + everything())
        project(4, to_proj(KV), A, {A: 1}, ready=t)
        T.wait(A.last())
        for m in range(TT2):
            for h in range(MEMH):
                last = te.transpose(ACC[:, m, h * P:(h + 1) * P], KV[:, MEMH + h, m * P:(m + 1) * P], ident)
        A.run(ac.activation, MIX[:, 8:12, :].rearrange("p b t -> p (b t)"), flat(ACC, 0, 2), ACT.Copy, after=[T.done(last)])


    def gated_delta_mixer():
        H = AR[3][:, :].rearrange("p (k t) -> p k t", t=S)
        t = rms_norm(H, X, v_("norm_mix", 0, DK), [loaded["x"]] + everything())
        T.wait(t[0])

        def conv_silu(i, u, bank, ready):
            next_split(i, u)
            block = i * (2 * R) + 2 * u
            A.run(ac.activation, before(block), before(block), ACT.Silu, after=[(V.sem, i * (6 * R) + (base + 6 * u))])

            def tap(b, j):
                return vec[:, bass.ds(block + (b + VEC["gdn_conv"][0] + j * 3 * NH), 1)]

            def out(b, j=3):
                return PROJ[:, bass.ds(block + (b + 2), 1), 3 - j:S].rearrange("p a t -> p (a t)")

            for b in range(2):
                t = A.run(ac.activation, out(b), bank[:, b, :], ACT.Copy, scale=tap(b, 3), after=[ready])
            for b in range(2):
                for j in range(3):
                    t = V.run(ve.scalar_tensor_tensor, out(b, j), bank[:, b, 0:S - 3 + j], tap(b, j), out(b, j),
                              ALU.mult, ALU.add, after=[t])

        def before(block):
            return PROJ[:, bass.ds(block, 2), :]

        T.wait(*t)
        V.run(ve.memset, PROJ[:, 0:2, :], 0.0, after=[A.last()])
        base = V.n
        A.wait(V.last())
        banks = project(12, conv_silu, V, {V: 6, A: 3})
        A.run(ac.activation, PROJ[:, 24:26, :], PROJ[:, 24:26, :], ACT.Silu, after=[V.last()])

        def z_and_queries(i, u, bank, ready):
            next_split(i, u)
            at = (26 + 2 * u) % 36
            A.run(ac.activation, PROJ[:, at:at + 2, :], bank, ACT.Copy, after=[ready])

        project(6, z_and_queries, A, {A: 1}, banks=banks)

        T.wait(loaded["small"])
        ba = tiny[:, 0:32].rearrange("p (t c) -> p t c", t=2)
        wba = s_("w_ba").rearrange("p (k c) -> p k c", c=16)
        for a in range(TT2):
            for k in range(DK):
                last = mm(WRK[:, 3, a * 16:(a + 1) * 16], H[:, k, a * P:(a + 1) * P], wba[:, k, :], k == 0, k == DK - 1)
        V.run(ve.tensor_copy, tiny[:, 0:32], WRK[:, 3, 0:32], after=[T.done(last)])
        q, k, v, z = (PROJ[:, 8 * n + 2:8 * n + 10, :] for n in range(4))

        ev = everything()
        qk = [PROJ[:, 4 * n + 2:4 * n + 6, :] for n in range(4)]
        ev = [head_norm(qk, False, 1, lambda n, piece, spread: V.run(
            ve.scalar_tensor_tensor, piece, spread, SCALE if n < 2 else 1.0, piece, ALU.mult, ALU.mult), ev)]

        beta = tiny[:, 32:48].rearrange("p (t h) -> p t h", t=2)
        g = tiny[:, 48:64].rearrange("p (t h) -> p t h", t=2)
        w0 = tiny[:, 64:80].rearrange("p (t h) -> p t h", t=2)
        w1 = tiny[:, 80:96].rearrange("p (t h) -> p t h", t=2)
        V.wait(loaded["rows"])
        A.wait(loaded["rows"])
        t = A.run(ac.activation, beta, ba[:, :, 0:8], ACT.Exp, scale=-1.0, after=ev)
        t = V.run(ve.tensor_scalar, beta, beta, 1.0, None, ALU.add, after=[t])
        t = V.run(ve.reciprocal, beta, beta, after=[t])
        t = V.run(ve.tensor_tensor, w0, ba[:, :, 8:16], over_rows(rows[:, 8:16], 2), ALU.add, after=[t])
        ta = A.run(ac.activation, w1, w0, ACT.Abs, after=[t])
        ta = A.run(ac.activation, w1, w1, ACT.Exp, scale=-1.0, after=[ta])
        ta = A.run(ac.activation, w1, w1, ACT.Ln, bias=epsc[:, 1:2], after=[ta])
        ea = A.run(ac.activation, rows[:, 0:8], rows[:, 0:8], ACT.Exp)
        t = V.run(ve.scalar_tensor_tensor, g, w0, 0.0, w1, ALU.max, ALU.add, after=[ta])
        t = V.run(ve.scalar_tensor_tensor, g, g, -1.0, over_rows(rows[:, 0:8], 2), ALU.mult, ALU.mult, after=[t, ea])

        T.wait(t)
        for a in range(TT2):
            mm(WRK[:, 0, a * 8:a * 8 + 8], c_("tri"), g[:, a, :])
            last = mm(WRK[:, 0, 16 + a * 8:24 + a * 8], c_("half"), g[:, a, :])
        gc = tiny[:, 96:112].rearrange("p (t h) -> p t h", t=2)
        gtot = tiny[:, 112:128].rearrange("p (t h) -> p t h", t=2)
        t = V.run(ve.tensor_copy, tiny[:, 96:128], WRK[:, 0, 0:32], after=[T.done(last)])
        bg = tiny[:, 128:144].rearrange("p (t h) -> p t h", t=2)
        kg = tiny[:, 144:160].rearrange("p (t h) -> p t h", t=2)
        ta = A.run(ac.activation, bg, gc, ACT.Exp, after=[t])
        V.run(ve.tensor_tensor, bg, bg, beta, ALU.mult, after=[ta])
        t = V.run(ve.tensor_tensor, kg, gtot, gc, ALU.subtract)
        small_done = A.run(ac.activation, kg, kg, ACT.Exp, after=[t])

        EA, EG, LT = AR[1], AR[2], AR[3]
        fre = everything()
        eg_done = []
        for a in range(TT2):
            work = heads(AR[0][:, a * 1024:(a + 1) * 1024])
            E = heads(EA[:, a * 1024:(a + 1) * 1024])
            G = heads(EG[:, a * 1024:(a + 1) * 1024])
            L = heads(LT[:, a * 1024:(a + 1) * 1024])
            tok = slice(a * P, (a + 1) * P)
            t = V.run(ve.tensor_tensor, work, over_rows(c_("tri")), over_cols(g[:, a, :]), ALU.mult, after=fre)
            T.wait(t, *fre)
            for b in range(2):
                last = mm(ACC[:, b, :], ones, AR[0][:, a * 1024 + b * 512:a * 1024 + (b + 1) * 512])
            t = T.done(last)
            gsum = flat(ACC, 0, 2).rearrange("p (h i) -> p h i", h=NH)
            te_ = A.run(ac.activation, G, gsum, ACT.Exp, after=[t])
            t = V.run(ve.tensor_tensor, E, gsum, over_cols(gc[:, a, :]), ALU.subtract, after=[te_])
            t = V.run(ve.tensor_tensor, E, E, over_rows(c_("neg")), ALU.add, after=[t])
            decayed = A.run(ac.activation, E, E, ACT.Exp, after=[t])
            t = V.run(ve.tensor_tensor, work, over_rows(ident), over_cols(beta[:, a, :]), ALU.mult, after=[t])
            T.wait(t)
            for b in range(2):
                mm(ACC[:, 2 + b, :], c_("before"), AR[0][:, a * 1024 + b * 512:a * 1024 + (b + 1) * 512])
            for h in range(NH):
                mm(WRK[:, h // 4, (h % 4) * P:(h % 4 + 1) * P], k[:, h, tok], k[:, h, tok])
            for h in range(NH):
                last = mm(WRK[:, 2 + h // 4, (h % 4) * P:(h % 4 + 1) * P], k[:, h, tok], q[:, h, tok])
            t = T.done(last)
            t = V.run(ve.tensor_tensor, L, flat(ACC, 2, 4).rearrange("p (h i) -> p h i", h=NH), E, ALU.mult, after=[t, decayed])
            V.run(ve.tensor_tensor, L, flat(WRK, 0, 2).rearrange("p (h i) -> p h i", h=NH), L, ALU.mult, after=[t])
            t = V.run(ve.tensor_tensor, E, flat(WRK, 2, 4).rearrange("p (h i) -> p h i", h=NH), E, ALU.mult)
            fre = [t, te_]
        AT = EA
        gl = tiny[:, 160:192].rearrange("p (n h) -> p n h", n=4)
        for a in range(TT2):
            G = heads(EG[:, a * 1024:(a + 1) * 1024])
            for r in range(2):
                V.run(ve.tensor_copy, gl[:, 2 * a + r, :], G[:, :, r * C + C - 1], after=fre)
            V.run(ve.tensor_tensor, q[:, :, a * P:(a + 1) * P], q[:, :, a * P:(a + 1) * P], G, ALU.mult, after=fre)

        TI, TTr, PM = AR[2], AR[4], AR[0]
        t = V.last()
        for a in range(TT2):
            V.run(ve.tensor_copy, heads(TI[:, a * 1024:(a + 1) * 1024]), over_rows(ident), after=[t])
            V.run(ve.tensor_copy, heads(TTr[:, a * 1024:(a + 1) * 1024]), over_rows(ident))
        T.wait(V.last())
        base = V.n
        per = 6
        with nc.Fori(0, 6) as lv:
            V.enter(lv, per)
            mask = cst[:, bass.ds(lv * P + CST["levels"][0], P)]
            for a in range(TT2):
                hs = [slice(a * 1024 + h * P, a * 1024 + (h + 1) * P) for h in range(NH)]
                bank = ACC if a == 0 else WRK
                T.wait((V.sem, lv * per + (base - 1 if a == 0 else base)))
                for h in range(NH):
                    last = mm(bank[:, h // 4, (h % 4) * P:(h % 4 + 1) * P], LT[:, hs[h]], TI[:, hs[h]])
                last.then_inc(T.sem, 1)
            for a in range(TT2):
                bank = ACC if a == 0 else WRK
                V.run(ve.tensor_tensor, heads(PM[:, a * 1024:(a + 1) * 1024]),
                      flat(bank, 0, 2).rearrange("p (h i) -> p h i", h=NH),
                      mask.unsqueeze(1).broadcast_to([P, NH, P]), ALU.mult, after=[(T.sem, lv * 4 + (T.n + 1 + a))])
            for a in range(TT2):
                hs = [slice(a * 1024 + h * P, a * 1024 + (h + 1) * P) for h in range(NH)]
                bank = ACC if a == 0 else WRK
                T.wait((V.sem, lv * per + (base + 1 + a)))
                for h in range(NH):
                    mm(bank[:, h // 4, (h % 4) * P:(h % 4 + 1) * P], TTr[:, hs[h]], PM[:, hs[h]])
                for h in range(NH):
                    last = mm(bank[:, 2 + h // 4, (h % 4) * P:(h % 4 + 1) * P], PM[:, hs[h]], TTr[:, hs[h]])
                last.then_inc(T.sem, 1)
            for a in range(TT2):
                bank = ACC if a == 0 else WRK
                for n, dst in enumerate((TI, TTr)):
                    part = dst[:, a * 1024:(a + 1) * 1024]
                    V.run(ve.tensor_tensor, part, part, flat(bank, 2 * n, 2 * n + 2), ALU.subtract,
                          after=[(T.sem, lv * 4 + (T.n + 3 + a))])
            V.leave(6)
        T.n += 24

        KB, KD, VB = AR[3], AR[2], AR[0]
        U = v.rearrange("p b t -> p (b t)")
        WT = k.rearrange("p b t -> p (b t)")
        done = V.last()
        T.wait(done)
        for a in range(TT2):
            tok = slice(a * P, (a + 1) * P)
            cols = slice(a * 1024, (a + 1) * 1024)
            if a:
                T.wait(V.last())
            for h in range(NH):
                te.transpose(ACC[:, h // 4, (h % 4) * P:(h % 4 + 1) * P], k[:, h, tok], ident)
            for h in range(NH):
                last = te.transpose(ACC[:, 2 + h // 4, (h % 4) * P:(h % 4 + 1) * P], v[:, h, tok], ident)
            t = T.done(last)
            kt = flat(ACC, 0, 2).rearrange("p (h i) -> p h i", h=NH)
            vt = flat(ACC, 2, 4).rearrange("p (h i) -> p h i", h=NH)
            V.run(ve.tensor_tensor, heads(KB[:, cols]), kt, over_cols(bg[:, a, :]), ALU.mult, after=[t, done])
            V.run(ve.tensor_tensor, heads(KD[:, cols]), kt, over_cols(kg[:, a, :]), ALU.mult, after=[small_done])
            V.run(ve.tensor_tensor, heads(VB[:, cols]), vt, over_cols(beta[:, a, :]), ALU.mult)
        T.wait(V.last())
        moved = []
        for a in range(TT2):
            hs = [slice(a * 1024 + h * P, a * 1024 + (h + 1) * P) for h in range(NH)]
            cols = slice(a * 1024, (a + 1) * 1024)
            bank = ACC if a == 0 else WRK
            for h in range(NH):
                mm(bank[:, h // 4, (h % 4) * P:(h % 4 + 1) * P], TTr[:, hs[h]], VB[:, hs[h]])
            for h in range(NH):
                last = mm(bank[:, 2 + h // 4, (h % 4) * P:(h % 4 + 1) * P], KB[:, hs[h]], TTr[:, hs[h]])
            t = T.done(last)
            V.run(ve.tensor_copy, U[:, cols], flat(bank, 0, 2), after=[t])
            A.run(ac.activation, WT[:, cols], flat(bank, 2, 4), ACT.Copy, after=[t])

        ready = [V.last(), A.last()]
        T.wait(*ready)
        state = STATE[:, :, :].rearrange("p h d -> p (h d)")
        for n in range(S // C):
            a, r = n // 2, n % 2
            rows_ = slice(r * C, (r + 1) * C)
            cols = slice(a * 1024, (a + 1) * 1024)
            hs = [slice(a * 1024 + h * P, a * 1024 + (h + 1) * P) for h in range(NH)]
            at = [slice(a * 1024 + h * P + r * C, a * 1024 + h * P + (r + 1) * C) for h in range(NH)]
            for h in range(NH):
                last = mm(WRK[rows_, h // 4, (h % 4) * P:(h % 4 + 1) * P], WT[:, at[h]], STATE[:, h, :])
            t = T.done(last)
            vn = VNEW[rows_, :, :].rearrange("p h d -> p (h d)")
            t = V.run(ve.tensor_tensor, vn, U[rows_, cols], WRK[rows_, 0:2, :].rearrange("p b c -> p (b c)"),
                      ALU.subtract, after=[t])
            for h in range(NH):
                mm(ACC[:, 2 + n % 2, h * C:(h + 1) * C], STATE[:, h, :], q[:, h, n * C:(n + 1) * C],
                   h == 0, True, skip_group_check=True)
            T.wait(t)
            for h in range(NH):
                last = mm(ACC[:, 2 + n % 2, h * C:(h + 1) * C], VNEW[rows_, h, :], AT[rows_, at[h]],
                          False, True, skip_group_check=True)
            out_t = T.done(last)
            if n < S // C - 1:
                for h in range(NH):
                    last = mm(ACC[:, h // 4, (h % 4) * P:(h % 4 + 1) * P], KD[rows_, hs[h]], VNEW[rows_, h, :])
                t = T.done(last)
                s1 = V.run(ve.tensor_tensor, STATE[:, :, :], STATE[:, :, :], over_cols(gl[:, n, :]), ALU.mult, after=[out_t])
                t = V.run(ve.tensor_tensor, state, flat(ACC, 0, 2), state, ALU.add, after=[t, s1])
            ob = A.run(ac.activation, MIX[:, 0:8, n * C:(n + 1) * C], heads(ACC[:, 2 + n % 2, :]), ACT.Copy, after=[out_t])
            T.wait(t, ob)

        ev = everything()
        o = MIX[:, 0:8, :]
        tz = A.run(ac.activation, z, z, ACT.Silu)
        t = head_norm([o[:, 0:4, :], o[:, 4:8, :]], False, P, lambda n, piece, spread: V.run(
            ve.scalar_tensor_tensor, piece, spread, v_("gdn_norm"), piece, ALU.mult, ALU.mult), ev)
        V.run(ve.tensor_tensor, o, o, z, ALU.mult, after=[t, tz])


    def sparse_mixer():
        H = AR[3][:, :].rearrange("p (k t) -> p k t", t=S)
        t = rms_norm(H, X, v_("norm_mix", DK, DK), everything())
        T.wait(*t, loaded["tab"], loaded["onehot"])
        last = mm(WRK[0:NH, 3, :], tab[0:BUCKETS + 1, :], onehot[0:BUCKETS + 1, :])
        line = AR[4][0:NH, 0:512]
        t = A.run(ac.activation, line, WRK[0:NH, 3, :], ACT.Copy, after=[T.done(last)])
        put, got = nc.alloc_semaphore("bias_line_stored"), nc.alloc_semaphore("bias_table_loaded")
        A.wait(t)
        nc.scalar.dma_start(scratch, line).then_inc(put, 16)
        nc.scalar.wait_ge(put, 16)
        table = PROJ[:, 24:36, :].rearrange("p b t -> p (b t)").rearrange("p (h y) -> p h y", h=NH)
        over = bass.AP(tensor=scratch.tensor, offset=0, ap=[[1, P], [512, NH], [1, 384]])
        nc.scalar.dma_start(table, over).then_inc(got, 16)
        wg = s_("w_gate").rearrange("p (k c) -> p k c", c=24)
        T.wait(t)
        for a in range(TT2):
            for k in range(DK):
                last = mm(WRK[:, 3, a * 24:(a + 1) * 24], H[:, k, a * P:(a + 1) * P], wg[:, k, :], k == 0, k == DK - 1)
        gates = tiny[:, 192:240].rearrange("p (t h c) -> p t h c", t=2, c=3)
        t = A.run(ac.activation, tiny[:, 192:240], WRK[:, 3, 0:48], ACT.Exp, scale=-1.0, after=[T.done(last)])
        t = V.run(ve.tensor_scalar, tiny[:, 192:240], tiny[:, 192:240], 1.0, None, ALU.add, after=[t])
        V.run(ve.reciprocal, tiny[:, 192:240], tiny[:, 192:240], after=[t])

        project(12, to_proj(PROJ), A, {A: 1})
        q, kvp, qm = PROJ[:, 0:8, :], PROJ[:, 8:20, :], [PROJ[:, 20 + h, :] for h in range(MEMH)]
        ev = everything()
        qs = V.run(ve.tensor_scalar, q, q, SCALE, None, ALU.mult, after=ev)

        small_ = AR[2][:, 1024:2048]
        hidden = [small_[:, 0:30], small_[:, 32:62]]
        kcT = small_[:, 64:94].rearrange("p (g c) -> p g c", g=2)
        vc = small_[0:NCMP, 128:384].rearrange("p (g d) -> p g d", g=2)
        for n, (part, pos) in enumerate((("k", "pos_k"), ("v", "pos_v"))):
            blk = AR[n + 3][:, 0:960].rearrange("p (l g c) -> p l g c", l=32, g=2)
            for g in range(2):
                for hl in range(2):
                    x = kvp[:, 2 * n + g, hl * 16:hl * 16 + 16 * NCMP].rearrange("p (c l) -> p l c", l=16)
                    V.run(ve.tensor_tensor, blk[:, hl * 16:(hl + 1) * 16, g, :], x,
                          v_(pos, hl * 16, 16).unsqueeze(2).broadcast_to([P, 16, NCMP]), ALU.add, after=ev)
        t = V.last()
        T.wait(t, *ev)
        for n in range(2):
            t = A.run(ac.activation, BH[:, n, :], AR[n + 3][:, 0:960], ACT.Copy, after=[t])
            V.run(ve.tensor_tensor, BL[:, n, :], AR[n + 3][:, 0:960], BH[:, n, :].bitcast(F32), ALU.subtract, after=[t])
        for n in range(2):
            for s in range(2):
                u = 2 * n + s
                parts, made, used = ring.slot(0, u)
                T.wait(made, (V.sem, V.n - 1 + n))
                for l in range(16):
                    at = slice((s * 16 + l) * 30, (s * 16 + l) * 30 + 30)
                    high, low = parts
                    mm(WRK[0:30, n, 0:P], BH[:, n, at], high[:, l, :], s == 0 and l == 0, False)
                    mm(WRK[0:30, n, 0:P], BL[:, n, at], high[:, l, :], False, False)
                    last = mm(WRK[0:30, n, 0:P], BH[:, n, at], low[:, l, :], False, s == 1 and l == 15)
                last.then_inc(used[0], 1)
                next_split(0, u)
            hid_t = small_[0:30, 384 + n * P:384 + (n + 1) * P]
            T.wait(A.run(ac.activation, hid_t, WRK[0:30, n, 0:P], ACT.Silu, after=[used]))
            t = T.done(te.transpose(WRK[:, 2 + n, 0:30], hid_t, ident[0:30, 0:30]))
            A.run(ac.activation, hidden[n], WRK[:, 2 + n, 0:30], ACT.Copy, after=[t])
        ring.g += 4
        T.wait(A.last())
        mm(WRK[:, 2, 0:30], s_("w2_k"), hidden[0])
        for g in range(2):
            last = mm(WRK[0:NCMP, 3, g * P:(g + 1) * P], hidden[1][:, g * NCMP:(g + 1) * NCMP], s_("w2_v"))
        t = T.done(last)
        A.run(ac.activation, kcT, WRK[:, 2, 0:30].rearrange("p (g c) -> p g c", g=2), ACT.Copy, after=[t])
        cmp_done = A.run(ac.activation, vc, WRK[0:NCMP, 3, 0:S].rearrange("p (g d) -> p g d", g=2), ACT.Copy, after=[t])

        vtok = AR[2][:, 0:1024].rearrange("p (m j d) -> p m j d", m=TT2, j=4)
        T.wait(cmp_done)
        for m in range(TT2):
            for j in range(4):
                block = (6 if j < 2 else 10) + j % 2
                last = te.transpose(WRK[:, m, j * P:(j + 1) * P], kvp[:, block, m * P:(m + 1) * P], ident)
        vt_done = A.run(ac.activation, AR[2][:, 0:1024], flat(WRK, 0, 2), ACT.Copy, after=[T.done(last)])

        T.wait((got, 16), qs)
        flip = c_("flip")
        PCT = MIX[:, 0:8, :]
        pcT = AR[4][0:NCMP, :].rearrange("p (h q) -> p h q", h=NH)
        V.wait(vt_done)
        for a in range(TT2):
            pc = AR[3][:, a * 256:a * 256 + 120].rearrange("p (h c) -> p h c", h=NH)
            sc = WRK[:, 2, a * 128:a * 128 + 120].rearrange("p (h c) -> p h c", h=NH)
            y0 = 31 + P * (1 - a)
            mm(sc, flip, table[:, :, y0:y0 + 16 * (NCMP - 1) + 1:16], skip_group_check=True)
            for h in range(NH):
                last = mm(sc[:, h, :], q[:, h, a * P:(a + 1) * P], kcT[:, h // 4, :], False, True, skip_group_check=True)
            t = T.done(last)
            mx, tot = tiny[:, 256 + a * 16:264 + a * 16], tiny[:, 264 + a * 16:272 + a * 16]
            t = V.run(ve.tensor_reduce, mx, sc, AX_X, ALU.max, after=[t])
            t = V.run(ve.tensor_scalar, mx, mx, NEG / 10, None, ALU.max, after=[t])
            t = V.run(ve.tensor_tensor, pc, sc, over_cols(mx, NCMP), ALU.subtract, after=[t])
            t = A.run(ac.activation, pc, pc, ACT.Exp, after=[t])
            t = V.run(ve.tensor_reduce, tot, pc, AX_X, ALU.add, after=[t])
            t = V.run(ve.tensor_scalar, tot, tot, 1e-30, None, ALU.max, after=[t])
            t = V.run(ve.reciprocal, tot, tot, after=[t])
            t = V.run(ve.tensor_tensor, tot, tot, gates[:, a, :, 0], ALU.mult, after=[t])
            t = V.run(ve.tensor_tensor, pc, pc, over_cols(tot, NCMP), ALU.mult, after=[t])
            T.wait(t)
            for h in range(NH):
                last = te.transpose(WRK[0:NCMP, h // 4, (h % 4) * P:(h % 4 + 1) * P], pc[:, h, :], ident)
            t = A.run(ac.activation, pcT[:, :, a * P:(a + 1) * P],
                      WRK[0:NCMP, 0:2, :].rearrange("p b c -> p (b c)").rearrange("p (h q) -> p h q", h=NH), ACT.Copy,
                      after=[T.done(last)])
            T.wait(t)

        out = flat(ACC, 0, 4).rearrange("p (h q) -> p h q", h=NH)
        for b in range(4):
            mm(ACC[:, b, :], zeros[:, 0:P], zeros[:, :], skip_group_check=True)
        for h in range(NH):
            last = mm(out[:, h, :], vc[:, h // 4, :], pcT[:, h, :], False, True, skip_group_check=True)
        pc_done = T.done(last)
        V.wait(pc_done)
        A.wait(pc_done)
        PTs = AR[1][:, :].rearrange("p (h m q) -> p h m q", h=4, m=TT2)

        def unit(j, a):
            br, g = j // 2, j % 2
            kblock = (4 if j < 2 else 8) + j % 2
            nk = (a + 1) * P
            space = WRK[:, 2 * a:2 * a + 2, :]
            sc = flat(space, 0, 2).rearrange("p (h k) -> p h k", h=4)[:, :, 0:nk]

            def scores():
                y0 = P * (1 - a)
                for b in range(2):
                    mm(sc[:, 2 * b:2 * b + 2, :], flip, table[:, g * 4 + 2 * b:g * 4 + 2 * b + 2, y0:y0 + nk],
                       skip_group_check=True)
                for h in range(4):
                    last = mm(sc[:, h, :], q[:, g * 4 + h, a * P:(a + 1) * P], kvp[:, kblock, 0:nk], False, True,
                              skip_group_check=True)
                return T.done(last)

            def values():
                for h in range(4):
                    mm(out[:, g * 4 + h, :], vtok[:, 0, j, :], PTs[:, h, 0, :], False, True, skip_group_check=True)
                    last = mm(out[:, g * 4 + h, P:S], vtok[:, 1, j, :], PTs[:, h, 1, P:S], False, True,
                              skip_group_check=True)
                if j >= 2:
                    V.run(ve.tensor_copy, MIX[:, 4 * g:4 * g + 4, :], out[:, 4 * g:4 * g + 4, :], after=[T.done(last)])

            return dict(scores=scores, space=space, view=sc, stats=tiny[:, 288 + 16 * a:304 + 16 * a], scale=1.0,
                        prob=heads(AR[0][:, a * 1024:(a + 1) * 1024], 4)[:, :, 0:nk], gate=gates[:, a, g * 4:g * 4 + 4, 1 + br],
                        turned=PTs[:, :, 0:a + 1, a * P:(a + 1) * P], values=values if a else None)

        attend([unit(j, a) for j in range(4) for a in range(TT2)] + memory_units(qm))


    def modulation_of(layer, part, which):
        if which == "c_ctx":
            return modc[:, part * DK:(part + 1) * DK]
        return mods[:, layer * NMOD + part * DK:layer * NMOD + (part + 1) * DK]

    def add_bias(dst, first, n):
        V.run(ve.tensor_tensor, dst, dst, v_("b_mod", first, n), ALU.add, after=[(mod_used, taken[0])])

    def modulated(source, layer, n, which, blocks):
        dst = AR[3][:, :].rearrange("p (k t) -> p k t", t=S)
        ev = everything() if blocks is None else []
        V.run(ve.scalar_tensor_tensor, gainA[:, :], modulation_of(layer, 3 * n + 1, which), 1.0,
              v_("norm_g", (layer * 3 + n) * DK, DK), ALU.add, ALU.mult, after=ev)
        return rms_norm(dst, source, gainA, ev, modulation_of(layer, 3 * n, which), blocks=blocks)

    def half_ffn(stream, layer, n, which, blocks=None, vectors=(), ready=None, beside=None):
        free = everything()
        gate = tiny[:, 320:328]
        V.run(ve.tensor_scalar, gate, modulation_of(layer, 3 * n + 2, which), 0.5, None, ALU.mult, after=[V.last()])
        if ready is None:
            ready = modulated(stream, layer, n, which, blocks)
        return add_sums(stream, feed_forward(None, free, vectors, ready, beside), gate)

    def attention_and_pool(blocks):
        KK = PROJ[:, 4:8, :].rearrange("p b t -> p (b t)").rearrange("p (g t) -> p g t", g=2)
        VT = PROJ[:, 8:10, :].rearrange("p b t -> p (b t)")
        pool = PROJ[:, 10:14, :]
        T.wait(*modulated(SIDE, 0, 1, "c_ctx", None))

        def keys_values(w):
            def evacuate(i, u, bank, ready):
                next_split(i, u)
                block = 2 * u
                if block == 0:
                    A.run(ac.activation, KK[:, :, w * S:(w + 1) * S], bank, ACT.Copy, after=[ready])
                elif block == 2:
                    A.run(ac.activation, VT[:, w * S:(w + 1) * S], bank[:, 0, :], ACT.Copy, after=[ready])
                    if w == 1:
                        A.run(ac.activation, pool[:, 0, :], bank[:, 1, :], ACT.Copy, after=[ready])
                elif block in (4, 6):
                    A.run(ac.activation, PROJ[:, block - 4:block - 2, :], bank, ACT.Copy, after=[ready])
                elif block == 8:
                    A.run(ac.activation, pool[:, 1:3, :], bank, ACT.Copy, after=[ready])
                else:
                    A.run(ac.activation, pool[:, 3, :], bank[:, 0, :], ACT.Copy, after=[ready])
            return evacuate

        project(2, keys_values(0), A, {A: 1})
        T.wait(*modulated(X, 0, 1, "c", None), A.last())
        base = A.n
        for u in range(6):
            parts, made, used = ring.slot(0, u)
            if u >= 3:
                T.wait((A.sem, base + (1, 3, 4)[u - 3]))
            T.wait(made)
            for b in range(2):
                if u == 5 and b == 1:
                    continue
                for k in range(DK):
                    last = mm3(WRK[:, u % 3, b * S:(b + 1) * S], parts, b * DK + k, XH[:, k, :], XL[:, k, :],
                               k == 0, k == DK - 1)
            last.then_inc(used[0], 1)
            keys_values(1)(0, u, WRK[:, u % 3, :].rearrange("p (b t) -> p b t", b=2), used)
        ring.g += 6
        ev = everything()

        sq = AR[0]
        ev = [head_norm([PROJ[:, 0:4, :], PROJ[:, 4:8, :]], True, C, lambda n, piece, spread: V.run(
            ve.scalar_tensor_tensor, piece, spread, v_("qk_norm", n, 1), piece, ALU.mult, ALU.mult), ev)]
        T.wait(*ev)
        for b in range(4):
            mm(WRK[:, b // 2, (b % 2) * S:(b % 2 + 1) * S], c_("rope"), PROJ[:, b, :])
        for g in range(2):
            last = mm(WRK[:, 2, g * S:(g + 1) * S], c_("rope"), KK[:, g, S:2 * S])
        t = T.done(last)
        swapped = flat(WRK, 0, 3).rearrange("p (b t) -> p b t", t=S)
        turn = sq[:, 0:1536].rearrange("p (b t) -> p b t", t=S)
        V.run(ve.tensor_tensor, turn, swapped, over_rows(c_("sin"), 6), ALU.mult, after=[t])
        for dst, part in ((PROJ[:, 0:4, :], turn[:, 0:4, :]), (KK[:, :, S:2 * S], turn[:, 4:6, :])):
            n = dst.shape[1]
            t = V.run(ve.tensor_tensor, dst, dst, over_rows(c_("cos"), n), ALU.mult, after=[V.last()])
            V.run(ve.tensor_tensor, dst, dst, part, ALU.add, after=[t])
        ev = everything()

        T.wait(*ev)
        for kt in range(4):
            last = te.transpose(WRK[:, 3, kt * P:(kt + 1) * P], VT[:, kt * P:(kt + 1) * P], ident)
        t = A.run(ac.activation, AR[2][:, 0:512], WRK[:, 3, :], ACT.Copy, after=[T.done(last)] + ev)
        vtok = AR[2][:, 0:512].rearrange("p (k d) -> p k d", k=4)
        PTs = PROJ[:, 14:30, :].rearrange("p b t -> p (b t)").rearrange("p (h k q) -> p h k q", h=4, k=4)
        T.wait(t)

        def unit(g, a):
            space = ACC if a == 0 else WRK

            def scores():
                for h in range(4):
                    part = slice(((g * 4 + h) % 2) * C, ((g * 4 + h) % 2 + 1) * C)
                    last = mm(space[:, h, :], PROJ[part, (g * 4 + h) // 2, a * P:(a + 1) * P], KK[part, g, :])
                return T.done(last)

            def values():
                for h in range(4):
                    part = slice(((g * 4 + h) % 2) * C, ((g * 4 + h) % 2 + 1) * C)
                    for kt in range(4):
                        last = mm(WRK[part, h // 2, 0:S], vtok[:, kt, g * C:(g + 1) * C], PTs[:, h, kt, :],
                                  kt == 0, kt == 3)
                T.wait(A.run(ac.activation, MIX[:, 2 * g:2 * g + 2, :], WRK[:, 0:2, 0:S], ACT.Copy, after=[T.done(last)]))

            return dict(scores=scores, space=space, view=space[:, :, :], prob=heads(AR[0 if a == 0 else 3][:, :], 4),
                        stats=tiny[:, 336 + 8 * a:344 + 8 * a], scale=C ** -0.5, gate=None,
                        turned=PTs[:, :, :, a * P:(a + 1) * P], values=values if a else None)

        attend([unit(g, a) for g in range(2) for a in range(TT2)])

        ev = everything()
        wide = S + 16
        pa = AR[0][:, 0:4 * wide].rearrange("p (g t) -> p g t", g=4)
        pb = AR[1][:, 0:4 * wide].rearrange("p (g t) -> p g t", g=4)
        V.run(ve.memset, pa, 0.0, after=ev)
        t = V.run(ve.memset, pb, 0.0)
        t = V.run(ve.tensor_copy, pa[:, :, 8:8 + S], pool, after=[t])
        t = V.run(ve.tensor_tensor, pb[:, :, 1:wide], pa[:, :, 0:wide - 1], pa[:, :, 1:wide], ALU.add, after=[t])
        t = V.run(ve.tensor_tensor, pa[:, 1:4, 1:wide - 1], pb[:, 1:4, 0:wide - 2], pb[:, 1:4, 2:wide], ALU.add, after=[t])
        t = V.run(ve.tensor_tensor, pb[:, 2:4, 2:wide - 2], pa[:, 2:4, 0:wide - 4], pa[:, 2:4, 4:wide], ALU.add, after=[t])
        t = V.run(ve.tensor_tensor, pa[:, 3:4, 4:wide - 4], pb[:, 3:4, 0:wide - 8], pb[:, 3:4, 8:wide], ALU.add, after=[t])
        cnt = c_("count").rearrange("p (g t) -> p g t", g=4)
        out = AR[2][:, 0:1024].rearrange("p (g t) -> p g t", g=4)
        for g, place in enumerate((pb, pa, pb, pa)):
            V.run(ve.tensor_tensor, out[:, g, :], place[:, g, 8:8 + S], cnt[:, g, :], ALU.mult, after=[t])
        t = V.run(ve.tensor_tensor, out, out, pool, ALU.subtract, after=[V.last()])
        T.wait(t)
        for g in range(4):
            last = mm(WRK[:, 2 + g // 2, (g % 2) * S:(g % 2 + 1) * S], s_("pool_w")[:, g * P:(g + 1) * P], out[:, g, :])
        t = T.done(last)
        for g in range(4):
            V.run(ve.tensor_scalar, MIX[:, 4 + g, :], WRK[:, 2 + g // 2, (g % 2) * S:(g % 2 + 1) * S],
                  v_("pool_scale", g, 1), None, ALU.mult, after=[t])
        return add_sums(X, out_projection(4, everything()), modulation_of(0, 5, "c"))

    def gmlp(blocks):
        T.wait(*modulated(X, 1, 1, "c", blocks))

        def gelu(i, u, bank, ready):
            next_split(i, u)
            A.run(ac.activation, PROJ[:, bass.ds(i * (2 * R) + 2 * u, 2), :], bank, ACT.Gelu_apprx_tanh, after=[ready])

        project(8, gelu, A, {A: 1})
        u, v = PROJ[:, 0:8, :], PROJ[:, 8:16, :]
        VN = AR[3][:, :].rearrange("p (k t) -> p k t", t=S)
        t = rms_norm(VN, v, v_("v_norm"), everything(), parts=False)[-1]
        vtok = AR[1][:, :].rearrange("p (a g c) -> p a g c", a=2, g=NH)
        T.wait(t)
        for a in range(TT2):
            for g in range(NH):
                last = te.transpose(ACC[:, 2 * a + g // 4, (g % 4) * P:(g % 4 + 1) * P], VN[:, g, a * P:(a + 1) * P], ident)
        t = A.run(ac.activation, AR[1][:, :], flat(ACC, 0, 4), ACT.Copy, after=[T.done(last), V.last()])
        T.wait(t, loaded["bsp"], loaded["w_sp"])
        wsp = KV[:, 0:4, :].rearrange("p b t -> p (b t)").rearrange("p (g q) -> p g q", g=NH)
        for a in range(TT2):
            for g in range(NH):
                o = WRK[:, 2 * a + g // 4, (g % 4) * P:(g % 4 + 1) * P]
                mm(o, vtok[:, a, g, :], wsp[:, g, :], True, False)
                last = mm(o, ones[0:1, :], VNEW[0:1, g, :], False, True)
            t = T.done(last)
            V.run(ve.tensor_tensor, MIX[:, 0:8, a * P:(a + 1) * P],
                  flat(WRK, 2 * a, 2 * a + 2).rearrange("p (g t) -> p g t", g=NH), u[:, :, a * P:(a + 1) * P],
                  ALU.mult, after=[t])
        return add_sums(X, out_projection(4, everything()), modulation_of(1, 5, "c"))


    stream_from(RAW, NSLOT + 1)
    for n in range(PAIRS):
        ring.split(V, A, 0, n)

    H = AR[3][:, :].rearrange("p (k t) -> p k t", t=S)
    G = nc.gpsimd
    memory_keys(0)
    gated_delta_mixer()
    G.wait_ge(V.sem, V.n)
    G.wait_ge(T.sem, T.n)
    for name in ("c", "c_ctx"):
        loaded[name] = (nc.alloc_semaphore("load_" + name), 16)
        G.dma_start(COND[name], src[name].partition_broadcast(P)).then_inc(loaded[name][0], 16)
    T.wait(*everything())
    A.wait(*everything())
    attend(memory_units([PROJ[:, b, :] for b in (34, 35, 0, 1)]))
    blocks = add_sums(X, out_projection(6, everything()))
    free = everything()
    ready = rms_norm(H, X, v_("norm_ffn", 0, DK), [], blocks=blocks)
    for name in ("c", "c_ctx"):
        t = A.run(ac.activation, COND[name], COND[name], ACT.Silu, after=[loaded[name]])
    V.wait(t)
    blocks = add_sums(X, feed_forward(0, free, (8, 0, 0, "c_ctx", modc), ready))

    memory_keys(1)
    sparse_mixer()
    load_side = nc.alloc_semaphore("in_context")
    nc.scalar.wait_ge(V.sem, V.n)
    nc.scalar.wait_ge(T.sem, T.n)
    nc.scalar.dma_start(SIDE[:, :, :], src["ctx"]).then_inc(load_side, 16)
    loaded["w_sp"] = (nc.alloc_semaphore("load_w_sp"), 16)
    nc.scalar.wait_ge(A.sem, A.n)
    nc.scalar.dma_start(KV[:, 0:4, :], src["w_sp"].rearrange("p (k t) -> p k t", t=S)).then_inc(loaded["w_sp"][0], 16)
    blocks = add_sums(X, out_projection(6, everything()))
    free = everything()
    ready = rms_norm(H, X, v_("norm_ffn", DK, DK), [], blocks=blocks)
    blocks = add_sums(X, feed_forward(1, free, (8, 0, 0, "c", mods), ready))
    rms_norm(H, X, v_("final_norm"), [], parts=False, blocks=blocks)
    V.run(ve.tensor_copy, X[:, :, :], H, after=[V.last()])
    add_bias(modc[:, :], 0, 5 * DK)
    add_bias(mods[:, 0:5 * DK], 0, 5 * DK)
    V.wait(V.last())

    for q_ in (V, A):
        q_.wait((load_side, 16))
    ready = []

    def tokens_norm():
        for q_ in (V, A):
            q_.wait((ring.used, ring.g))
        ready.extend(modulated(X, 0, 0, "c", [V.last()] * DK))

    half_ffn(SIDE, 0, 0, "c_ctx", vectors=(8, 40, 0, "c", mods), beside=tokens_norm)
    half_ffn(X, 0, 0, "c", vectors=(8, 80, 0, "c", mods), ready=ready)
    add_bias(mods[:, 5 * DK:15 * DK], 5 * DK, 10 * DK)
    V.wait(V.last())
    blocks = attention_and_pool(None)
    blocks = half_ffn(X, 0, 2, "c", blocks, vectors=(4, 120, 4, "c", mods))
    add_bias(mods[:, 15 * DK:18 * DK], 15 * DK, 3 * DK)
    G.wait_ge(mod_used, taken[0])
    loaded["bsp"] = (nc.alloc_semaphore("load_bsp"), 16)
    G.dma_start(VNEW[0:1, :, :].rearrange("p h d -> p (h d)"), src["bsp"].unsqueeze(0)).then_inc(loaded["bsp"][0], 16)
    V.wait(V.last())
    blocks = half_ffn(X, 1, 0, "c", blocks)
    blocks = gmlp(blocks)
    half_ffn(X, 1, 2, "c", blocks)
    assert ring.g == NSLOT

    stored = nc.alloc_semaphore("out_stored")
    nc.sync.wait_ge(V.sem, V.n)
    nc.sync.dma_start(y_out, X[:, :, :]).then_inc(stored, 16)
    nc.sync.wait_ge(stored, 16)



def shape_constants():
    i = np.arange(P)
    same = (i[:, None] // C) == (i[None, :] // C)
    c = {}
    c["ident"] = np.eye(P)
    c["ones"] = np.ones((P, P))
    c["tri"] = (same & (i[:, None] <= i[None, :]))
    c["half"] = same
    c["neg"] = np.where(c["tri"], 0.0, NEG)
    c["before"] = same & (i[:, None] > i[None, :])
    c["flip"] = np.eye(P)[::-1]
    levels = []
    for s in (1, 2, 4, 8, 16, 32):
        block = (i[:, None] // (2 * s)) == (i[None, :] // (2 * s))
        levels.append(block & ((i[:, None] // s) % 2 == 1) & ((i[None, :] // s) % 2 == 0))
    c["levels"] = np.concatenate(levels, axis=1)
    rope = np.zeros((P, P))
    for m in range(P):
        if m % 32 < 16:
            rope[m + 16, m] = -1.0
        else:
            rope[m - 16, m] = 1.0
    c["rope"] = rope
    half = 32
    inv = (np.float32(10000.0) ** (-np.arange(0, half, 2, dtype=np.float32) / np.float32(half))).astype(np.float32)
    t = np.arange(S)
    axis = np.where(((i % C) // 32 == 0)[:, None], (t // 64)[None, :], (t % 64)[None, :]).astype(np.float32)
    ang = axis * inv[i % 16][:, None]
    c["cos"], c["sin"] = np.cos(ang), np.sin(ang)
    cnt = [1.0 / (np.clip(t + w // 2, 0, S) - np.clip(t - w // 2, 0, S)) for w in (2, 4, 8, 16)]
    c["count"] = np.broadcast_to(np.concatenate(cnt)[None, :], (P, 4 * S))
    c["pick"] = np.zeros((P, 31))
    c["pick"][:, 15] = 1.0
    c["pick_half"] = np.zeros((P, 30))
    c["pick_half"][:C, 14] = c["pick_half"][C:, 15] = 1.0
    out = np.zeros((P, NCST), np.float32)
    for name, (a, b) in CST.items():
        out[:, a:b] = c[name]
    dist = np.arange(S)
    exact = BUCKETS // 2
    logv = (np.log(np.maximum(dist, 1).astype(np.float32) / np.float32(exact)) / np.float32(math.log(128 / exact))).astype(np.float32)
    large = np.minimum(exact + (logv * np.float32(BUCKETS - exact)).astype(np.int32), BUCKETS - 1)
    bucket = np.where(dist < exact, dist, large)
    onehot = np.zeros((BUCKETS + 1, 512), np.float32)
    onehot[bucket, 255 - dist] = 1.0
    onehot[BUCKETS, 256:] = 1.0
    return out, onehot



def fm(x):
    x = np.asarray(x)
    return x.reshape(-1, P).T


def in_slots(w):
    n = w.shape[1] // 256
    return w.reshape(DK, P, n, 2, P).transpose(2, 1, 3, 0, 4).reshape(n, P, TILES * P)


def up_slots(w):
    return w.reshape(DK, P, 2, FB, P).transpose(3, 1, 2, 0, 4).reshape(FB, P, TILES * P)


def down_slots(w):
    return w.reshape(-1, 2, P, D).transpose(0, 2, 1, 3).reshape(-1, P, TILES * P)


def ffn_slots(up, down):
    u, d = up_slots(up), down_slots(down)
    order = [u[0:2]]
    for p in range(1, FB // 2):
        order += [u[2 * p:2 * p + 2], d[p - 1:p]]
    return np.concatenate(order + [d[FB // 2 - 1:]])


def kernel(**inputs):
    import concourse.bacc as bacc
    from concourse.bass_utils import run_bass_kernel_spmd

    g = {k: np.asarray(v) for k, v in inputs.items()}
    tokens = lambda x: np.ascontiguousarray(x.reshape(S, DK, P).transpose(2, 1, 0))
    gdn, nsa = g["gdn_w_in"][0], g["nsa_w_in"][0]
    wa = g["w_in_a_2"][0]
    k0, k1 = wa[:, 512:576], wa[:, 576:640]
    in_a = np.concatenate([k0, k0, k1, k1, wa[:, 640:768], wa[:, 768:896], wa[:, 0:512], wa[:, 896:1280],
                           np.zeros((D, P), np.float32)], axis=1)
    cmp_ = lambda w: w[0].reshape(2, 16, P, P).transpose(0, 2, 1, 3).reshape(2, P, TILES * P)
    parts = {
        "mem_kv0": in_slots(g["mem_w_kv"][0]),
        "gdn_in": in_slots(np.concatenate([gdn[:, :4096], gdn[:, 4112:]], axis=1)),
        "out0": down_slots(g["w_out"][0]),
        "ffn0": ffn_slots(g["ffn_w_up"][0], g["ffn_w_down"][0]),
        "mem_kv1": in_slots(g["mem_w_kv"][1]),
        "nsa_in": in_slots(np.concatenate([nsa[:, :2560], nsa[:, 2584:]], axis=1)),
        "cmp_k": cmp_(g["nsa_cmp_w1_k"]), "cmp_v": cmp_(g["nsa_cmp_w1_v"]),
        "out1": down_slots(g["w_out"][1]),
        "ffn1": ffn_slots(g["ffn_w_up"][1], g["ffn_w_down"][1]),
        "in_ac": in_slots(in_a[:, 0:512]), "in_a": in_slots(in_a), "out_a": down_slots(g["w_out_a_2"][0]),
        "in_c": in_slots(g["w_in_c_2"][0]), "out_c": down_slots(g["w_out_c_2"][0]),
    }
    ff = {(i, j): ffn_slots(g["ffn_w13_2"][i, j], g["ffn_w2_2"][i, j]) for i in range(2) for j in range(2)}
    parts.update(ffn2c=ff[0, 0], ffn2=ff[0, 0], ffn3=ff[0, 1], ffn4=ff[1, 0], ffn5=ff[1, 1])
    weights = np.concatenate([parts[name] for name, _ in STREAM])

    v = {
        "norm_mix": fm(g["norm_mix_w"]), "norm_ffn": fm(g["norm_ffn_w"]), "final_norm": fm(g["final_norm_w"]),
        "mem_norm": fm(g["mem_norm_w"]), "gdn_conv": fm(g["gdn_conv_w"]), "gdn_norm": fm(g["gdn_norm_w"]),
        "ffn_conv": fm(g["ffn_conv_w"]), "ffn_bias": fm(g["ffn_conv_b"]),
        "pos_k": g["nsa_cmp_pos_k"][0].T, "pos_v": g["nsa_cmp_pos_v"][0].T,
        "b_mod": fm(g["b_mod_2"]), "norm_g": fm(g["norm_g_2"]),
        "qk_norm": np.concatenate([g["qk_norm_g_2"][0]] * 2, axis=1).T,
        "pool_scale": fm(g["pool_scale_2"]), "v_norm": fm(g["v_norm_g_2"]),
    }
    kc = lambda w: w.reshape(DK, P, -1).transpose(1, 0, 2).reshape(P, -1)
    sm = {
        "w_ba": kc(gdn[:, 4096:4112]), "w_gate": kc(nsa[:, 2560:2584]),
        "w2_k": g["nsa_cmp_w2_k"][0], "w2_v": g["nsa_cmp_w2_v"][0],
        "pool_w": g["pool_w_2"][0].transpose(1, 0, 2).reshape(P, 4 * P),
    }
    cst, onehot = shape_constants()
    arrays = {
        "x": tokens(g["x"]), "mem": tokens(g["mem"]), "ctx": tokens(g["ctx_2"]),
        "vec": np.concatenate([v[n] for n in VEC], axis=1), "small": np.concatenate([sm[n] for n in SMALL], axis=1),
        "cst": cst, "onehot": onehot, "rows": np.concatenate([g["gdn_a_log"][0], g["gdn_dt_bias"][0]]),
        "tab": g["rel_bias"], "bsp": g["b_sp_2"].reshape(-1), "weights": weights,
        "w_sp": g["w_sp_2"][0].transpose(2, 0, 1).reshape(P, NH * P), "c": g["c_2"].reshape(-1), "c_ctx": g["c_ctx_2"],
        "wmod": g["w_mod_2"].reshape(2, D, NMOD, P).transpose(0, 2, 3, 1).reshape(2 * NMOD, P, D),
    }
    arrays = {k: np.ascontiguousarray(a) for k, a in arrays.items()}

    nc = bacc.Bacc("TRN2", target_bir_lowering=False, num_devices=1)
    aps = {k: nc.dram_tensor("in_" + k, a.shape, F32, kind="ExternalInput").ap() for k, a in arrays.items()}
    y = nc.dram_tensor("y", (P, DK, S), F32, kind="ExternalOutput").ap()
    scratch = nc.dram_tensor("bias_line", (NH, 512), F32, kind="Internal").ap()
    program(nc, aps, aps["weights"], y, scratch)
    r = run_bass_kernel_spmd(nc, [{"in_" + k: a for k, a in arrays.items()}], core_ids=[0])
    return r.results[0]["y"].transpose(2, 1, 0).reshape(1, S, D)
```

```python
import math

import numpy as np

import concourse.bass as bass
from concourse import mybir

F32 = mybir.dt.float32
F32R = mybir.dt.float32r
BF16 = mybir.dt.bfloat16
ALU = mybir.AluOpType
ACT = mybir.ActivationFunctionType
AX_X = mybir.AxisListType.X

P = 128
S = 256
D = 1024
DK = D // P
TT2 = S // P
NH = 8
C = 64
F = 2816
FB = F // P
MEMH = 4
NCMP = (S - 32) // 16 + 1
NMOD = 9 * DK
EPS = 1e-6
SCALE = P ** -0.5
NEG = -1e30
RAW = 3
PAIRS = 2
R = 6
MODS = 4
TILES = 16
BUCKETS = 32



def columns(parts):
    at, out = 0, {}
    for name, width in parts:
        out[name] = (at, at + width)
        at += width
    return out, at


VEC, NVEC = columns([
    ("norm_mix", 2 * DK), ("norm_ffn", 2 * DK), ("final_norm", DK), ("mem_norm", 2 * DK),
    ("gdn_conv", 4 * 3 * NH), ("gdn_norm", 1), ("ffn_conv", 2 * 3 * FB), ("ffn_bias", 2 * FB),
    ("pos_k", 32), ("pos_v", 32), ("b_mod", 2 * NMOD), ("norm_g", 6 * DK), ("qk_norm", 2),
    ("pool_scale", 4), ("v_norm", DK)])
SMALL, NSMALL = columns([
    ("w_ba", DK * 16), ("w_gate", DK * 24), ("w2_k", P), ("w2_v", P), ("pool_w", 4 * P)])
CST, NCST = columns([
    ("ident", P), ("ones", P), ("tri", P), ("half", P), ("neg", P), ("before", P), ("flip", P),
    ("levels", 6 * P), ("rope", P), ("cos", S), ("sin", S), ("count", 4 * S),
    ("pick", 31), ("pick_half", 30)])
STREAM = [("mem_kv0", 4), ("gdn_in", 18), ("out0", 6), ("ffn0", 33),
          ("mem_kv1", 4), ("nsa_in", 12), ("cmp_k", 2), ("cmp_v", 2), ("out1", 6), ("ffn1", 33),
          ("ffn2c", 33), ("ffn2", 33), ("in_ac", 2), ("in_a", 6), ("out_a", 4), ("ffn3", 33),
          ("ffn4", 33), ("in_c", 8), ("out_c", 4), ("ffn5", 33)]
NSLOT = sum(n for _, n in STREAM)



class Queue:

    def __init__(self, engine, sem, apart=None):
        self.engine, self.sem, self.n, self.i = engine, sem, 0, None
        self.seen, self.apart = {}, apart

    def wait(self, *ticks):
        for sem, value in ticks:
            if isinstance(value, int):
                if self.seen.get(sem.name, 0) >= value:
                    continue
                self.seen[sem.name] = value
            self.engine.wait_ge(sem, value)

    def done(self, instruction):
        instruction.then_inc(self.sem, 1)
        if self.i is None:
            self.n += 1
            return (self.sem, self.n)
        self.k += 1
        return (self.sem, self.i * self.per + (self.n + self.k))

    def run(self, op, *args, after=(), **kw):
        self.wait(*after)
        if self.apart is not None and self.i is not None:
            self.engine.sem_inc(self.apart, 1)
        return self.done(op(*args, **kw))

    def last(self):
        return (self.sem, self.n)

    def enter(self, i, per):
        self.i, self.per, self.k = i, per, 0

    def leave(self, times):
        assert self.k == self.per
        self.n += times * self.per
        self.i = None


class Ring:

    def __init__(self, raw, high, low, arrived, rounded, split, used):
        self.raw, self.high, self.low = raw, high, low
        self.arrived, self.rounded, self.split_, self.used = arrived, rounded, split, used
        self.g = 0

    def slot(self, i, u):
        at = self.g + u
        high, low = (x[:, at % PAIRS, :].rearrange("p (t c) -> p t c", c=P) for x in (self.high, self.low))
        return (high, low), (self.split_, i * R + (at + 1)), (self.used, i * R + (at + 1))

    def split(self, V, A, i, u, halves=(0, 1)):
        at = self.g + u
        if 0 in halves:
            A.wait((self.arrived[at % RAW], i * (16 * (R // RAW)) + 16 * (at // RAW + 1)))
            if not isinstance(i, int) or at >= PAIRS:
                A.wait((self.used, i * R + (at - PAIRS + 1)))
        n = TILES * P // 2
        for half in halves:
            cols = slice(half * n, (half + 1) * n)
            A.engine.activation(self.high[:, at % PAIRS, cols], self.raw[:, at % RAW, cols], ACT.Copy
                                ).then_inc(self.rounded, 1)
            V.wait((self.rounded, i * (2 * R) + (2 * at + 1 + half)))
            last = V.engine.tensor_tensor(self.low[:, at % PAIRS, cols], self.raw[:, at % RAW, cols],
                                          self.high[:, at % PAIRS, cols].bitcast(F32), ALU.subtract)
        if 1 in halves:
            last.then_inc(self.split_, 1)


def program(nc, src, weights, y_out, scratch):

    def sbuf(name, shape, dt=F32):
        return nc.alloc_sbuf_tensor(name, [P] + shape, dt)

    V = Queue(nc.vector, nc.alloc_semaphore("vector_done"))
    A = Queue(nc.scalar, nc.alloc_semaphore("scalar_done"), apart=nc.alloc_semaphore("apart"))
    T = Queue(nc.tensor, nc.alloc_semaphore("tensor_done"))
    L = Queue(nc.gpsimd, nc.alloc_semaphore("gpsimd_done"))
    ring = Ring(sbuf("raw", [RAW, TILES * P]), sbuf("high", [PAIRS, TILES * P], F32R),
                sbuf("low", [PAIRS, TILES * P], F32R), [nc.alloc_semaphore(f"arrived{r}") for r in range(RAW)],
                nc.alloc_semaphore("halves_rounded"), nc.alloc_semaphore("slots_split"),
                nc.alloc_semaphore("slots_used"))
    ve, ac, te = nc.vector, nc.scalar, nc.tensor

    X = sbuf("X", [DK, S])
    SIDE = sbuf("SIDE", [DK, S])
    at_proj = nc.sbuf_base
    PROJ = sbuf("PROJ", [36, S])
    MIX = sbuf("MIX", [12, S])
    KV = sbuf("KV", [DK, S])
    at_areas = nc.sbuf_base
    AR = [sbuf(f"AR{n}", [2048]) for n in range(5)]
    STATE = sbuf("STATE", [NH, P])
    VNEW = sbuf("VNEW", [NH, P])
    vec = sbuf("vec", [NVEC])
    small = sbuf("small", [NSMALL])
    cst = sbuf("cst", [NCST])
    rows = sbuf("rows", [16])
    tab = sbuf("tab", [NH])
    onehot = sbuf("onehot", [512])
    RINV = sbuf("RINV", [S])
    RINV2 = sbuf("RINV2", [S])
    zeros = sbuf("zeros", [512], BF16)
    epsc = sbuf("epsc", [4])
    mods = sbuf("mods", [2 * NMOD])
    modc = sbuf("modc", [5 * DK])
    gainA = sbuf("gainA", [DK])
    gainB = sbuf("gainB", [DK])
    tiny = sbuf("tiny", [512])
    XH, XL = (nc.alloc_sbuf_tensor_at(name, [P, 12, S], F32R, offset=at_areas + n * 12 * S * 4)
              for n, name in enumerate(("XH", "XL")))
    HIDH, HIDL = (nc.alloc_sbuf_tensor_at(name, [P, 4, S], F32R, offset=at_proj + n * 4 * S * 4)
                  for n, name in enumerate(("HIDH", "HIDL")))
    BH, BL = (nc.alloc_sbuf_tensor_at(name, [P, 2, 960], F32R, offset=at_areas + n * 2 * 1024 * 4)
              for n, name in enumerate(("BH", "BL")))
    MRING = nc.alloc_sbuf_tensor_at("MRING", [P, MODS, D], F32, offset=at_proj + 8 * S * 4)
    ACC = nc.alloc_psum_tensor("ACC", [P, 4, 512], F32)
    WRK = nc.alloc_psum_tensor("WRK", [P, 4, 512], F32)

    def v_(name, k=0, n=None):
        a, b = VEC[name]
        return vec[:, a + k:(a + k + n if n else b)]

    def s_(name):
        return small[:, SMALL[name][0]:SMALL[name][1]]

    def c_(name):
        return cst[:, CST[name][0]:CST[name][1]]

    ident, ones = c_("ident"), c_("ones")

    def heads(ap, h=NH):
        return ap.rearrange("p (h i) -> p h i", h=h)

    def over_rows(ap, h=NH):
        return ap.unsqueeze(1).broadcast_to([ap.shape[0], h, ap.shape[1]])

    def over_cols(ap, n=P):
        return ap.unsqueeze(2).broadcast_to([ap.shape[0], ap.shape[1], n])

    def flat(ps, a, b):
        return ps[:, a:b, :].rearrange("p b c -> p (b c)")

    def everything():
        return [V.last(), A.last(), T.last(), (ring.used, ring.g)]

    loaded = {}

    def load(name, dst, source):
        loaded[name] = (nc.alloc_semaphore("load_" + name), 16)
        nc.sync.dma_start(dst, source).then_inc(loaded[name][0], 16)

    def fill(n):
        nc.sync.dma_start(ring.raw[:, n % RAW, :], weights[n % NSLOT, :, :]).then_inc(ring.arrived[n % RAW], 16)

    load("side", SIDE[:, :, :], src["mem"])
    load("vec", vec[:, :], src["vec"])
    load("first_cst", cst[:, 0:2 * P], src["cst"][:, 0:2 * P])
    fill(0)
    fill(1)
    load("x", X[:, :, :], src["x"])
    fill(2)
    load("cst", cst[:, 2 * P:NCST], src["cst"][:, 2 * P:NCST])
    load("small", small[:, :], src["small"])
    load("rows", rows[:, :], src["rows"].partition_broadcast(P))
    load("tab", tab[0:BUCKETS, :], src["tab"])
    load("onehot", onehot[0:BUCKETS + 1, :], src["onehot"])

    def stream_from(n0, n1):
        full = (n1 - n0) // R
        with nc.sync.Fori(0, full) as i:
            for u in range(R):
                nc.sync.wait_ge(ring.split_, i * R + (n0 + u - RAW + 1))
                nc.sync.dma_start(ring.raw[:, (n0 + u) % RAW, :],
                                  weights[bass.ds(i * R + (n0 + u), 1), :, :].rearrange("a p n -> p (a n)")
                                  ).then_inc(ring.arrived[(n0 + u) % RAW], 16)
        for n in range(n0 + full * R, n1):
            nc.sync.wait_ge(ring.split_, n - RAW + 1)
            fill(n)

    V.run(ve.memset, zeros[:, :], 0.0)
    V.run(ve.memset, epsc[:, 0:1], EPS)
    V.run(ve.memset, epsc[:, 1:4], 1.0)
    V.run(ve.memset, STATE[:, :, :], 0.0)
    V.run(ve.memset, PROJ[:, 0:2, :], 0.0)
    V.run(ve.memset, tab[BUCKETS:BUCKETS + 1, :], NEG)
    made = V.last()
    for q in (V, A, T):
        q.wait(made, loaded["vec"], loaded["first_cst"])


    def mm(out, lhsT, rhs, start=True, stop=True, **kw):
        return te.matmul(out, lhsT, rhs, start=start, stop=stop, **kw)

    def mm3(out, parts, tile, xh, xl, start, stop, **kw):
        high, low = parts
        mm(out, high[:, tile, :], xh, start, False, **kw)
        mm(out, high[:, tile, :], xl, False, False, **kw)
        return mm(out, low[:, tile, :], xh, False, stop, **kw)

    def next_split(i, u):
        at = ring.g + u + PAIRS
        if isinstance(i, int) and u == held[0]:
            owed.extend([0, 1])
        elif not isinstance(i, int) or at <= NSLOT:
            ring.split(V, A, i, u + PAIRS)

    held = [None]
    owed = []

    def later_split():
        if ring.g + PAIRS - 1 <= NSLOT:
            owed.extend([0, 1])

    def owed_split(n):
        for half in owed[:n]:
            ring.split(V, A, 0, PAIRS - 1, (half,))
        del owed[:n]

    def root_table():
        A.run(ac.activation, epsc[:, 2:3], epsc[:, 3:4], ACT.Sqrt)

    def squares(source, after, blocks=None):
        sq = AR[4][:, :].rearrange("p (k t) -> p k t", t=S)
        A.wait(*after)
        V.wait(*after)
        ticks = []
        for k in range(DK):
            t = A.run(ac.activation, sq[:, k, :], source[:, k, :], ACT.Square, after=[blocks[k]] if blocks else ())
            if k % 2:
                ticks.append(V.run(ve.tensor_tensor, sq[:, k, :], sq[:, k - 1, :], sq[:, k, :], ALU.add, after=[t]))
        return ticks

    def root_of_sums(dst, pairs):
        sums = WRK[:, 3, 0:S]
        for n, t in enumerate(pairs):
            T.wait(t)
            last = mm(sums, ones, AR[4][:, (2 * n + 1) * S:(2 * n + 2) * S], n == 0, n == len(pairs) - 1)
        t = T.done(last)
        owed_split(1)
        return A.run(ac.activation, dst, sums, ACT.Sqrt, scale=1.0 / D, bias=epsc[:, 0:1], after=[t])

    def root_mean_square(dst, pairs):
        return V.run(ve.reciprocal, dst, dst, after=[root_of_sums(dst, pairs)])

    def rms_norm(dst, source, gain, after, shift=None, parts=True, blocks=None):
        T.wait(*after)
        t = root_mean_square(RINV[:, :], squares(source, after, blocks))
        ready = normed(dst, source, gain, RINV, t, shift, parts)
        owed_split(1)
        return ready

    def low_part(k, dst, shift, t):
        return V.run(ve.scalar_tensor_tensor, XL[:, k, :], dst[:, k, :],
                     0.0 if shift is None else shift[:, k:k + 1], XH[:, k, :].bitcast(F32),
                     ALU.add, ALU.subtract, after=[t])

    def high_part(k, dst, shift, t):
        if shift is None:
            return A.run(ac.activation, XH[:, k, :], dst[:, k, :], ACT.Copy, after=[t])
        return A.run(ac.activation, XH[:, k, :], dst[:, k, :], ACT.Identity, bias=shift[:, k:k + 1], after=[t])

    def normed(dst, source, gain, rinv, t, shift=None, parts=True):
        ready = []
        for k in range(DK):
            t = V.run(ve.scalar_tensor_tensor, dst[:, k, :], source[:, k, :], gain[:, k:k + 1], rinv[:, :],
                      ALU.mult, ALU.mult, after=[t] if k == 0 else ())
            if not parts:
                ready.append(t)
                continue
            if k:
                ready.append(low_part(k - 1, dst, shift, high))
            high = high_part(k, dst, shift, t)
        if parts:
            ready.append(low_part(DK - 1, dst, shift, high))
        return ready

    def project_two(n, evacuate, ready, source, gain, blocks, shift=None):
        dst = AR[3][:, :].rearrange("p (k t) -> p k t", t=S)
        pairs = squares(source, [], blocks)
        ticks = []

        def norm():
            root = root_of_sums(RINV2[:, :], pairs)

            def rest():
                t = V.run(ve.reciprocal, RINV2[:, :], RINV2[:, :], after=[root])
                ticks.extend(normed(dst, source, gain, RINV2, t, parts=False))

            return rest

        held[0] = n - 1
        project(n, evacuate, A, {A: 1}, ready=ready, beside={n // 2 - 1: norm})
        held[0] = None
        free = A.last()
        for q in (V, A):
            q.wait((ring.used, ring.g))
        highs = [high_part(k, dst, shift, ticks[k]) for k in range(DK)]
        ready = [low_part(k, dst, shift, highs[k]) for k in range(DK)]
        owed_split(2)
        T.wait(free)
        return ready

    def head_norm(blocks, half, divisor, factor, after):
        n = 4 * len(blocks)
        sq = [AR[p // 2][:, (p % 2) * 1024:(p % 2 + 1) * 1024].rearrange("p (k t) -> p k t", t=S) for p in range(4)]
        sel = AR[3][0:16, :].rearrange("p (h c) -> p h c", c=C if half else P)
        made = V.run(ve.tensor_copy, sel[:, 0:16, :], over_cols(ident[0:16, 0:16], C if half else P), after=after)
        sums = WRK[0:16, 3, 0:S]
        T.wait(*after)
        for p, piece in enumerate(blocks):
            t = A.run(ac.activation, sq[p], piece, ACT.Square, after=after)
            T.wait(t)
            for k in range(4):
                b = 4 * p + k
                pick = c_("pick_half")[:, 14 - 2 * b:30 - 2 * b] if half else c_("pick")[:, 15 - b:31 - b]
                last = mm(sums, pick, sq[p][:, k, :], b == 0, b == n - 1)
        r = RINV[0:16, :]
        t = A.run(ac.activation, r, sums, ACT.Sqrt, scale=1.0 / divisor, bias=epsc[0:16, 0:1], after=[T.done(last)])
        t = V.run(ve.reciprocal, r, r, after=[t, made])
        T.wait(t)
        sel = AR[3][0:16, :].rearrange("p (b c) -> p b c", c=P)
        for p, piece in enumerate(blocks):
            space = (ACC if p < 2 else WRK)[:, 2 * (p % 2):2 * (p % 2) + 2, :]
            for k in range(4):
                last = mm(space[:, k // 2, (k % 2) * S:(k % 2 + 1) * S], sel[:, 4 * p + k, :], r)
            t = T.done(last)
            V.wait(t)
            factor(p, piece, space.rearrange("p b (k t) -> p (b k) t", t=S))
        return V.last()

    def steps(n, body, per):
        full = n // R if n // R > 1 else 0
        if full:
            with nc.Fori(0, full) as i:
                for q, k in per.items():
                    q.enter(i, k * R)
                for u in range(R):
                    body(i, u)
                for q in per:
                    q.leave(full)
        for u in range(full * R, n):
            body(0, u)
        ring.g += n

    def project(n, evacuate, reader, per, ready=(), banks=(), beside={}):
        base, c = reader.n, per[reader]

        def body(i, u):
            parts, made, used = ring.slot(i, u)
            bank = u % 3
            if isinstance(i, int) and u < 3:
                T.wait(*banks[u:u + 1])
            else:
                T.wait((reader.sem, i * (R * c) + (base + c * (u - 2))))
            T.wait(made)
            for b in range(2):
                for k in range(DK):
                    if u == 0 and b == 0:
                        T.wait(*ready[k:k + 1])
                    last = mm3(WRK[:, bank, b * S:(b + 1) * S], parts, b * DK + k, XH[:, k, :], XL[:, k, :],
                               k == 0, k == DK - 1)
            last.then_inc(used[0], 1)
            rest = beside[u]() if isinstance(i, int) and u in beside else None
            evacuate(i, u, WRK[:, bank, :].rearrange("p (b t) -> p b t", b=2), used)
            if rest is not None:
                rest()

        steps(n, body, per)
        return [(reader.sem, max(base + c * max(m + 1, 0), 0)) for m in range(n - 3, n)] if n % 3 == 0 else None

    def to_proj(dst, off=0):
        def evacuate(i, u, bank, ready):
            next_split(i, u)
            A.run(ac.activation, dst[:, bass.ds(i * (2 * R) + (2 * u + off), 2), :], bank, ACT.Copy, after=[ready])
        return evacuate

    def open_sums(after):
        T.wait(*after)
        for b in range(4):
            mm(ACC[:, b, :], zeros[:, 0:P], zeros[:, :], skip_group_check=True)

    def add_down(parts, source):
        for kk in range(2):
            for m in range(DK):
                last = mm3(ACC[:, m // 2, (m % 2) * S:(m % 2 + 1) * S], parts, kk * DK + m, *source(kk),
                           False, True, skip_group_check=True)
        return last

    def last_down(parts, source, used):
        ticks = []
        for m in range(DK):
            for kk in range(2):
                last = mm3(ACC[:, m // 2, (m % 2) * S:(m % 2 + 1) * S], parts, kk * DK + m, *source(kk),
                           False, True, skip_group_check=True)
            if m % 2 and m < DK - 1:
                ticks.append(T.done(last))
        last.then_inc(used[0], 1)
        return ticks + [used]

    def out_projection(n, after):
        open_sums(after)
        V.wait(*after)
        A.wait(*after)
        for k in range(n):
            two = slice(2 * k, 2 * k + 2)
            t = A.run(ac.activation, XH[:, two, :], MIX[:, two, :], ACT.Copy)
            V.run(ve.tensor_tensor, XL[:, two, :], MIX[:, two, :], XH[:, two, :].bitcast(F32), ALU.subtract, after=[t])
        first = V.n - n
        root_table()
        for u in range(n):
            parts, made, used = ring.slot(0, u)
            T.wait(made, (V.sem, first + u + 1))
            source = lambda kk: (XH[:, 2 * u + kk, :], XL[:, 2 * u + kk, :])
            if u < n - 1:
                add_down(parts, source).then_inc(used[0], 1)
                next_split(0, u)
        ring.g += n
        ticks = last_down(parts, source, used)
        later_split()
        return ticks

    def add_sums(dst, ready, gate=None):
        for m in range(DK):
            V.wait(ready[m // 2])
            s = ACC[:, m // 2, (m % 2) * S:(m % 2 + 1) * S]
            if gate is None:
                V.run(ve.tensor_tensor, dst[:, m, :], s, dst[:, m, :], ALU.add)
            else:
                V.run(ve.scalar_tensor_tensor, dst[:, m, :], s, gate[:, m:m + 1], dst[:, m, :], ALU.mult, ALU.add)
        return [(V.sem, V.n - DK + 1 + m) for m in range(DK)]

    def feed_forward(conv, after, vectors=(), ready=(), beside=None, early=None):
        hid = AR[3][:, 0:4 * S].rearrange("p (j t) -> p j t", t=S)
        V.wait(*after)
        A.wait(*after)
        ca, cv = (3, 4) if conv is not None else (2, 2)
        base_v, base_u = V.n, ring.g
        trips = (FB - 2) // 4
        if vectors:
            modulation_loads(vectors, trips, after)

        def up(i, j, u):
            parts, made, used = ring.slot(i, u)
            bank = WRK[:, j % 4, :]
            if not isinstance(i, int) or j >= 4:
                T.wait((V.sem, i * (4 * cv) + (base_v + cv * (j - 3))))
            T.wait(made)
            for b in range(2):
                for k in range(DK):
                    if isinstance(i, int) and j == 0 and b == 0:
                        T.wait(*ready[k:k + 1])
                    last = mm3(bank[:, b * S:(b + 1) * S], parts, b * DK + k, XH[:, k, :], XL[:, k, :],
                               k == 0, k == DK - 1)
            last.then_inc(used[0], 1)
            gate, out = bank[:, 0:S], hid[:, j % 4, :]
            if conv is None:
                next_split(i, u)
                t = A.run(ac.activation, out, gate, ACT.Silu, after=[used])
                parts_of(i, j, by_value(j, t))
            else:
                if j:
                    t = by_value(j - 1, silu(i, j - 1))
                next_split(i, u)
                if j:
                    parts_of(i, j - 1, t)

                def col(tap):
                    at = VEC["ffn_conv"][0] + (conv * 3 + tap) * FB if tap < 3 else VEC["ffn_bias"][0] + conv * FB
                    return vec[:, bass.ds(i * 4 + (at + j), 1)]
                t = A.run(ac.activation, out, gate, ACT.Identity, scale=col(2), bias=col(3), after=[used])
                t = V.run(ve.scalar_tensor_tensor, out[:, 1:S], gate[:, 0:S - 1], col(1), out[:, 1:S],
                          ALU.mult, ALU.add, after=[t])
                V.run(ve.scalar_tensor_tensor, out[:, 2:S], gate[:, 0:S - 2], col(0), out[:, 2:S],
                      ALU.mult, ALU.add, after=[t])

        def silu(i, j):
            out = hid[:, j % 4, :]
            return A.run(ac.activation, out, out, ACT.Silu, after=[(V.sem, i * (4 * cv) + (base_v + cv * j + 2))])

        def by_value(j, t):
            out = hid[:, j % 4, :]
            return V.run(ve.tensor_tensor, out, out, WRK[:, j % 4, S:2 * S], ALU.mult, after=[t])

        def parts_of(i, j, t):
            out = hid[:, j % 4, :]
            if not isinstance(i, int) or i or j >= 4:
                A.wait((ring.used, i * R + (base_u + 3 * ((j - 4) // 2) + 5)))
            t = A.run(ac.activation, HIDH[:, j % 4, :], out, ACT.Copy, after=[t])
            V.run(ve.tensor_tensor, HIDL[:, j % 4, :], out, HIDH[:, j % 4, :].bitcast(F32), ALU.subtract, after=[t])

        def down(i, p, u):
            parts, made, used = ring.slot(i, u)
            T.wait(made, (V.sem, i * (4 * cv) + (base_v + cv * (2 * p + 2))))
            add_down(parts, lambda kk: (HIDH[:, (2 * p + kk) % 4, :], HIDL[:, (2 * p + kk) % 4, :])
                     ).then_inc(used[0], 1)
            next_split(i, u)

        up(0, 0, 0)
        up(0, 1, 1)
        ring.g += 2
        open_sums(after)
        if early is not None:
            n = V.n
            early()
            base_v += V.n - n
        with nc.Fori(0, trips) as i:
            V.enter(i, 4 * cv)
            A.enter(i, 4 * ca)
            for half in range(2):
                for j in range(2):
                    up(i, 2 + 2 * half + j, 3 * half + j)
                    if vectors:
                        modulation_products(vectors, i, 2 * half + j)
                down(i, half, 3 * half + 2)
            V.leave(trips)
            A.leave(trips)
        ring.g += trips * R
        if conv is not None:
            parts_of(trips, 1, by_value(1, silu(trips, 1)))
        if vectors:
            modulation_rest(vectors, trips)
        if beside is not None:
            beside()
        if conv is not None or not beside:
            root_table()
        parts, made, used = ring.slot(0, 0)
        T.wait(made, (V.sem, base_v + cv * FB))
        ticks = last_down(parts, lambda kk: (HIDH[:, (FB - 2 + kk) % 4, :], HIDL[:, (FB - 2 + kk) % 4, :]), used)
        ring.g += 1
        later_split()
        if beside is not None:
            owed_split(2)
        return ticks

    mod_used = nc.alloc_semaphore("mod_blocks_used")
    mod_arrived = [nc.alloc_semaphore(f"mod_arrived{r}") for r in range(MODS)]
    taken = [0]
    COND = {"c": VNEW[:, :, :].rearrange("p h d -> p (h d)"), "c_ctx": STATE[:, :, :].rearrange("p h d -> p (h d)")}

    def modulation_loads(vectors, trips, after):
        each, first, rest = vectors[0:3]
        n, g = each * trips + rest, taken[0]
        G = Queue(nc.gpsimd, None)
        G.wait(*after)

        def fetch(i, u):
            if not isinstance(i, int) or g + u >= MODS:
                nc.gpsimd.wait_ge(mod_used, i * MODS + (g + u - MODS + 1))
            nc.gpsimd.dma_start(MRING[:, (g + u) % MODS, :],
                                src["wmod"][bass.ds(i * MODS + (first + u), 1), :, :].rearrange("a p k -> p (a k)")
                                ).then_inc(mod_arrived[(g + u) % MODS], 16)

        for u in range(MODS):
            fetch(0, u)
        with nc.gpsimd.Fori(0, n // MODS - 1) as i:
            for u in range(MODS):
                fetch(i, u + MODS)
        assert n % MODS == 0

    def modulation_block(vectors, i, per_trip, u):
        what, dst = vectors[3:5]
        g = taken[0] + u
        V.wait((mod_arrived[g % MODS], i * (16 * per_trip // MODS) + 16 * (g // MODS + 1)))
        at = vectors[1] + u
        ve.scalar_tensor_tensor(MRING[:, g % MODS, :], MRING[:, g % MODS, :], 1.0, COND[what], ALU.mult, ALU.mult,
                                accum_out=dst[:, bass.ds(i * per_trip + at, 1)]).then_inc(mod_used, 1)

    def modulation_products(vectors, i, quarter):
        each = vectors[0]
        assert each % MODS == 0
        for b in range(each // 4):
            modulation_block(vectors, i, each, quarter * (each // 4) + b)

    def modulation_rest(vectors, trips):
        each, _, rest = vectors[0:3]
        for u in range(rest):
            modulation_block(vectors, 0, 0, each * trips + u)
        taken[0] += each * trips + rest

    def attend(units):
        copied, weighted = [], []
        for n in range(len(units) + 2):
            if n >= 2:
                T.wait(copied[n - 2])
                if units[n - 2]["values"]:
                    units[n - 2]["values"]()
            if n < len(units):
                scored = units[n]["scores"]()
            if 1 <= n <= len(units):
                u = units[n - 1]
                prob, space = u["prob"], u["space"]
                count, nk = prob.shape[1:3]
                tot = u["stats"][:, count:2 * count]
                t = V.run(ve.reciprocal, tot, tot, after=[weighted[n - 1]])
                if u["gate"] is not None:
                    t = V.run(ve.tensor_tensor, tot, tot, u["gate"], ALU.mult, after=[t])
                t = V.run(ve.tensor_tensor, prob, prob, over_cols(tot, nk), ALU.mult, after=[t])
                T.wait(t)
                kts = nk // P
                for h in range(count):
                    for kt in range(kts):
                        at = h * kts + kt
                        last = te.transpose(space[:, at // 4, (at % 4) * P:(at % 4 + 1) * P],
                                            prob[:, h, kt * P:(kt + 1) * P], ident)
                copied.append(A.run(ac.activation, u["turned"],
                                    flat(space, 0, count * kts // 4).rearrange("p (h k q) -> p h k q", h=count, k=kts),
                                    ACT.Copy, after=[T.done(last)]))
            if n < len(units):
                u = units[n]
                view, prob = u["view"], u["prob"]
                count = view.shape[1]
                mx, tot = u["stats"][:, 0:count], u["stats"][:, count:2 * count]
                t = V.run(ve.tensor_reduce, mx, view, AX_X, ALU.max, after=[scored])
                t = V.run(ve.tensor_scalar, mx, mx, -u["scale"], None, ALU.mult, after=[t])
                for h in range(count):
                    t = A.run(ac.activation, prob[:, h, :], view[:, h, :], ACT.Exp, bias=mx[:, h:h + 1],
                              scale=u["scale"], accum_out=tot[:, h:h + 1], after=[t])
                weighted.append(t)

    def memory_units(qm):
        vtok = MIX[:, 8:12, :].rearrange("p b t -> p (b t)").rearrange("p (m h d) -> p m h d", m=TT2, h=MEMH)
        PT = AR[1][:, :].rearrange("p (h m q) -> p h m q", h=MEMH, m=TT2)

        def unit(a):
            space = WRK[:, 2 * a:2 * a + 2, :]

            def scores():
                for h in range(MEMH):
                    last = mm(space[:, h // 2, (h % 2) * S:(h % 2 + 1) * S], qm[h][:, a * P:(a + 1) * P], KV[:, h, :])
                return T.done(last)

            def values():
                T.wait(V.last())
                for h in range(MEMH):
                    for m in range(TT2):
                        last = mm(ACC[:, h // 2, (h % 2) * S:(h % 2 + 1) * S], vtok[:, m, h, :], PT[:, h, m, :],
                                  m == 0, m == TT2 - 1)
                A.run(ac.activation, MIX[:, 8:12, :], flat(ACC, 0, 2).rearrange("p (h q) -> p h q", h=MEMH), ACT.Copy,
                      after=[T.done(last)])

            return dict(scores=scores, space=space, view=flat(space, 0, 2).rearrange("p (h k) -> p h k", h=MEMH),
                        prob=heads(AR[0][:, a * 1024:(a + 1) * 1024], MEMH), stats=tiny[:, 288 + 16 * a:304 + 16 * a],
                        scale=SCALE, gate=None, turned=PT[:, :, :, a * P:(a + 1) * P], values=values if a else None)

        return [unit(a) for a in range(TT2)]

    def memory_input(layer, after):
        mem_n = AR[3][:, :].rearrange("p (k t) -> p k t", t=S)
        return rms_norm(mem_n, SIDE, v_("mem_norm", layer * DK, DK), after)

    def memory_keys(layer, ready, blocks):
        return project_two(4, to_proj(KV), ready, X, v_("norm_mix", layer * DK, DK), blocks)

    def memory_values():
        T.wait(A.last(), V.last())
        for m in range(TT2):
            for h in range(MEMH):
                last = te.transpose(ACC[:, m, h * P:(h + 1) * P], KV[:, MEMH + h, m * P:(m + 1) * P], ident)
        t = A.run(ac.activation, MIX[:, 8:12, :].rearrange("p b t -> p (b t)"), flat(ACC, 0, 2), ACT.Copy,
                  after=[T.done(last)])
        V.wait(t)
        T.wait(t)


    def gated_delta_mixer(ready):
        for q in (V, A, T):
            q.wait(loaded["cst"])
        H = AR[3][:, :].rearrange("p (k t) -> p k t", t=S)

        def conv_silu(i, u, bank, ready):
            next_split(i, u)
            block = i * (2 * R) + 2 * u
            A.run(ac.activation, before(block), before(block), ACT.Silu, after=[(V.sem, i * (6 * R) + (base + 6 * u))])

            def tap(b, j):
                return vec[:, bass.ds(block + (b + VEC["gdn_conv"][0] + j * 3 * NH), 1)]

            def out(b, j=3):
                return PROJ[:, bass.ds(block + (b + 2), 1), 3 - j:S].rearrange("p a t -> p (a t)")

            t = [A.run(ac.activation, out(b), bank[:, b, :], ACT.Copy, scale=tap(b, 3), after=[ready]) for b in range(2)]
            t[0] = t[1]
            for j in range(3):
                for b in range(2):
                    t[b] = V.run(ve.scalar_tensor_tensor, out(b, j), bank[:, b, 0:S - 3 + j], tap(b, j), out(b, j),
                                 ALU.mult, ALU.add, after=[t[b]])

        def before(block):
            return PROJ[:, bass.ds(block, 2), :]

        base = V.n
        banks = project(12, conv_silu, V, {V: 6, A: 3}, ready=ready)
        A.run(ac.activation, PROJ[:, 24:26, :], PROJ[:, 24:26, :], ACT.Silu, after=[V.last()])

        def z_and_queries(i, u, bank, ready):
            next_split(i, u)
            at = (26 + 2 * u) % 36
            A.run(ac.activation, PROJ[:, at:at + 2, :], bank, ACT.Copy, after=[ready])

        T.wait(loaded["small"])
        ba = tiny[:, 0:32].rearrange("p (t c) -> p t c", t=2)
        wba = s_("w_ba").rearrange("p (k c) -> p k c", c=16)
        for a in range(TT2):
            for k in range(DK):
                last = mm(WRK[:, 3, a * 16:(a + 1) * 16], H[:, k, a * P:(a + 1) * P], wba[:, k, :], k == 0, k == DK - 1)
        ba_done = V.run(ve.tensor_copy, tiny[:, 0:32], WRK[:, 3, 0:32], after=[T.done(last)])
        beta = tiny[:, 32:48].rearrange("p (t h) -> p t h", t=2)
        g = tiny[:, 48:64].rearrange("p (t h) -> p t h", t=2)
        w0 = tiny[:, 64:80].rearrange("p (t h) -> p t h", t=2)
        w1 = tiny[:, 80:96].rearrange("p (t h) -> p t h", t=2)

        def gate_terms():
            V.wait(loaded["rows"])
            A.wait(loaded["rows"])
            t = A.run(ac.activation, beta, ba[:, :, 0:8], ACT.Exp, scale=-1.0, after=[ba_done])
            t = V.run(ve.tensor_scalar, beta, beta, 1.0, None, ALU.add, after=[t])
            t = V.run(ve.reciprocal, beta, beta, after=[t])
            t = V.run(ve.tensor_tensor, w0, ba[:, :, 8:16], over_rows(rows[:, 8:16], 2), ALU.add, after=[t])
            ta = A.run(ac.activation, w1, w0, ACT.Abs, after=[t])
            ta = A.run(ac.activation, w1, w1, ACT.Exp, scale=-1.0, after=[ta])
            ta = A.run(ac.activation, w1, w1, ACT.Ln, bias=epsc[:, 1:2], after=[ta])
            ea = A.run(ac.activation, rows[:, 0:8], rows[:, 0:8], ACT.Exp)
            t = V.run(ve.scalar_tensor_tensor, g, w0, 0.0, w1, ALU.max, ALU.add, after=[ta])
            t = V.run(ve.scalar_tensor_tensor, g, g, -1.0, over_rows(rows[:, 0:8], 2), ALU.mult, ALU.mult, after=[t, ea])
            decays.append(t)

        decays = []
        project(6, z_and_queries, A, {A: 1}, banks=banks, beside={3: lambda: gate_terms})

        T.wait(decays[0])
        for a in range(TT2):
            mm(WRK[:, 0, a * 8:a * 8 + 8], c_("tri"), g[:, a, :])
            last = mm(WRK[:, 0, 16 + a * 8:24 + a * 8], c_("half"), g[:, a, :])
        gc = tiny[:, 96:112].rearrange("p (t h) -> p t h", t=2)
        gtot = tiny[:, 112:128].rearrange("p (t h) -> p t h", t=2)
        t = V.run(ve.tensor_copy, tiny[:, 96:128], WRK[:, 0, 0:32], after=[T.done(last)])
        bg = tiny[:, 128:144].rearrange("p (t h) -> p t h", t=2)
        kg = tiny[:, 144:160].rearrange("p (t h) -> p t h", t=2)
        ta = A.run(ac.activation, bg, gc, ACT.Exp, after=[t])
        V.run(ve.tensor_tensor, bg, bg, beta, ALU.mult, after=[ta])
        t = V.run(ve.tensor_tensor, kg, gtot, gc, ALU.subtract)
        small_done = A.run(ac.activation, kg, kg, ACT.Exp, after=[t])

        memory_values()

        q, k, v, z = (PROJ[:, 8 * n + 2:8 * n + 10, :] for n in range(4))

        ev = everything()
        qk = [PROJ[:, 4 * n + 2:4 * n + 6, :] for n in range(4)]
        ev = [head_norm(qk, False, 1, lambda n, piece, spread: V.run(
            ve.scalar_tensor_tensor, piece, spread, SCALE if n < 2 else 1.0, piece, ALU.mult, ALU.mult), ev)]

        EA, EG, LT = AR[1], AR[2], AR[3]
        fre = everything()
        eg_done = []
        for a in range(TT2):
            work = heads(AR[0][:, a * 1024:(a + 1) * 1024])
            E = heads(EA[:, a * 1024:(a + 1) * 1024])
            G = heads(EG[:, a * 1024:(a + 1) * 1024])
            L = heads(LT[:, a * 1024:(a + 1) * 1024])
            tok = slice(a * P, (a + 1) * P)
            t = V.run(ve.tensor_tensor, work, over_rows(c_("tri")), over_cols(g[:, a, :]), ALU.mult, after=fre)
            T.wait(t, *fre)
            for b in range(2):
                last = mm(ACC[:, b, :], ones, AR[0][:, a * 1024 + b * 512:a * 1024 + (b + 1) * 512])
            t = T.done(last)
            gsum = flat(ACC, 0, 2).rearrange("p (h i) -> p h i", h=NH)
            te_ = A.run(ac.activation, G, gsum, ACT.Exp, after=[t])
            t = V.run(ve.tensor_tensor, E, gsum, over_cols(gc[:, a, :]), ALU.subtract, after=[te_])
            t = V.run(ve.tensor_tensor, E, E, over_rows(c_("neg")), ALU.add, after=[t])
            decayed = A.run(ac.activation, E, E, ACT.Exp, after=[t])
            t = V.run(ve.tensor_tensor, work, over_rows(ident), over_cols(beta[:, a, :]), ALU.mult, after=[t])
            T.wait(t)
            for b in range(2):
                mm(ACC[:, 2 + b, :], c_("before"), AR[0][:, a * 1024 + b * 512:a * 1024 + (b + 1) * 512])
            for h in range(NH):
                mm(WRK[:, h // 4, (h % 4) * P:(h % 4 + 1) * P], k[:, h, tok], k[:, h, tok])
            for h in range(NH):
                last = mm(WRK[:, 2 + h // 4, (h % 4) * P:(h % 4 + 1) * P], k[:, h, tok], q[:, h, tok])
            t = T.done(last)
            t = V.run(ve.tensor_tensor, L, flat(ACC, 2, 4).rearrange("p (h i) -> p h i", h=NH), E, ALU.mult, after=[t, decayed])
            V.run(ve.tensor_tensor, L, flat(WRK, 0, 2).rearrange("p (h i) -> p h i", h=NH), L, ALU.mult, after=[t])
            t = V.run(ve.tensor_tensor, E, flat(WRK, 2, 4).rearrange("p (h i) -> p h i", h=NH), E, ALU.mult)
            fre = [t, te_]
        AT = EA
        gl = tiny[:, 160:192].rearrange("p (n h) -> p n h", n=4)
        for a in range(TT2):
            G = heads(EG[:, a * 1024:(a + 1) * 1024])
            for r in range(2):
                V.run(ve.tensor_copy, gl[:, 2 * a + r, :], G[:, :, r * C + C - 1], after=fre)
            V.run(ve.tensor_tensor, q[:, :, a * P:(a + 1) * P], q[:, :, a * P:(a + 1) * P], G, ALU.mult, after=fre)

        TI, TTr, PM = AR[2], AR[4], AR[0]
        t = V.last()
        for a in range(TT2):
            V.run(ve.tensor_copy, heads(TI[:, a * 1024:(a + 1) * 1024]), over_rows(ident), after=[t])
            V.run(ve.tensor_copy, heads(TTr[:, a * 1024:(a + 1) * 1024]), over_rows(ident))
        T.wait(V.last())
        base = V.n
        per = 6
        with nc.Fori(0, 6) as lv:
            V.enter(lv, per)
            mask = cst[:, bass.ds(lv * P + CST["levels"][0], P)]
            for a in range(TT2):
                hs = [slice(a * 1024 + h * P, a * 1024 + (h + 1) * P) for h in range(NH)]
                bank = ACC if a == 0 else WRK
                T.wait((V.sem, lv * per + (base - 1 if a == 0 else base)))
                for h in range(NH):
                    last = mm(bank[:, h // 4, (h % 4) * P:(h % 4 + 1) * P], LT[:, hs[h]], TI[:, hs[h]])
                last.then_inc(T.sem, 1)
            for a in range(TT2):
                bank = ACC if a == 0 else WRK
                V.run(ve.tensor_tensor, heads(PM[:, a * 1024:(a + 1) * 1024]),
                      flat(bank, 0, 2).rearrange("p (h i) -> p h i", h=NH),
                      mask.unsqueeze(1).broadcast_to([P, NH, P]), ALU.mult, after=[(T.sem, lv * 4 + (T.n + 1 + a))])
            for a in range(TT2):
                hs = [slice(a * 1024 + h * P, a * 1024 + (h + 1) * P) for h in range(NH)]
                bank = ACC if a == 0 else WRK
                T.wait((V.sem, lv * per + (base + 1 + a)))
                for h in range(NH):
                    mm(bank[:, h // 4, (h % 4) * P:(h % 4 + 1) * P], TTr[:, hs[h]], PM[:, hs[h]])
                for h in range(NH):
                    last = mm(bank[:, 2 + h // 4, (h % 4) * P:(h % 4 + 1) * P], PM[:, hs[h]], TTr[:, hs[h]])
                last.then_inc(T.sem, 1)
            for a in range(TT2):
                bank = ACC if a == 0 else WRK
                for n, dst in enumerate((TI, TTr)):
                    part = dst[:, a * 1024:(a + 1) * 1024]
                    V.run(ve.tensor_tensor, part, part, flat(bank, 2 * n, 2 * n + 2), ALU.subtract,
                          after=[(T.sem, lv * 4 + (T.n + 3 + a))])
            V.leave(6)
        T.n += 24

        KB, KD, VB = AR[3], AR[2], AR[0]
        U = v.rearrange("p b t -> p (b t)")
        WT = k.rearrange("p b t -> p (b t)")
        done = V.last()
        T.wait(done)
        for a in range(TT2):
            tok = slice(a * P, (a + 1) * P)
            cols = slice(a * 1024, (a + 1) * 1024)
            if a:
                T.wait(V.last())
            for h in range(NH):
                te.transpose(ACC[:, h // 4, (h % 4) * P:(h % 4 + 1) * P], k[:, h, tok], ident)
            for h in range(NH):
                last = te.transpose(ACC[:, 2 + h // 4, (h % 4) * P:(h % 4 + 1) * P], v[:, h, tok], ident)
            t = T.done(last)
            kt = flat(ACC, 0, 2).rearrange("p (h i) -> p h i", h=NH)
            vt = flat(ACC, 2, 4).rearrange("p (h i) -> p h i", h=NH)
            V.run(ve.tensor_tensor, heads(KB[:, cols]), kt, over_cols(bg[:, a, :]), ALU.mult, after=[t, done])
            V.run(ve.tensor_tensor, heads(KD[:, cols]), kt, over_cols(kg[:, a, :]), ALU.mult, after=[small_done])
            V.run(ve.tensor_tensor, heads(VB[:, cols]), vt, over_cols(beta[:, a, :]), ALU.mult)
        T.wait(V.last())
        moved = []
        for a in range(TT2):
            hs = [slice(a * 1024 + h * P, a * 1024 + (h + 1) * P) for h in range(NH)]
            cols = slice(a * 1024, (a + 1) * 1024)
            bank = ACC if a == 0 else WRK
            for h in range(NH):
                mm(bank[:, h // 4, (h % 4) * P:(h % 4 + 1) * P], TTr[:, hs[h]], VB[:, hs[h]])
            for h in range(NH):
                last = mm(bank[:, 2 + h // 4, (h % 4) * P:(h % 4 + 1) * P], KB[:, hs[h]], TTr[:, hs[h]])
            t = T.done(last)
            V.run(ve.tensor_copy, U[:, cols], flat(bank, 0, 2), after=[t])
            A.run(ac.activation, WT[:, cols], flat(bank, 2, 4), ACT.Copy, after=[t])

        qm = [PROJ[:, b, :] for b in (34, 35, 0, 1)]
        space, PT = WRK[:, 2:4, :], AR[3][:, :].rearrange("p (h m q) -> p h m q", h=MEMH, m=TT2)
        scores = flat(space, 0, 2).rearrange("p (h k) -> p h k", h=MEMH)
        memory = {}

        def memory_piece(a, piece):
            prob = heads(AR[0][:, a * 1024:(a + 1) * 1024], MEMH)
            mx, tot = tiny[:, 288 + 16 * a:292 + 16 * a], tiny[:, 292 + 16 * a:296 + 16 * a]
            if piece == 0:
                T.wait(*([memory["copied"]] if a else ()))
                for h in range(MEMH):
                    last = mm(scores[:, h, :], qm[h][:, a * P:(a + 1) * P], KV[:, h, :])
                memory["scored"] = T.done(last)
            elif piece == 1:
                t = V.run(ve.tensor_reduce, mx, scores, AX_X, ALU.max, after=[memory["scored"]])
                t = V.run(ve.tensor_scalar, mx, mx, -SCALE, None, ALU.mult, after=[t])
                for h in range(MEMH):
                    memory["exp"] = A.run(ac.activation, prob[:, h, :], scores[:, h, :], ACT.Exp, bias=mx[:, h:h + 1],
                                          scale=SCALE, accum_out=tot[:, h:h + 1], after=[t])
            elif piece == 2:
                t = V.run(ve.reciprocal, tot, tot, after=[memory["exp"]])
                memory["prob"] = V.run(ve.tensor_tensor, prob, prob, over_cols(tot, S), ALU.mult, after=[t])
            elif piece == 3:
                T.wait(memory["prob"])
                for h in range(MEMH):
                    for m in range(TT2):
                        last = te.transpose(space[:, h // 2, (h % 2 * 2 + m) * P:(h % 2 * 2 + m + 1) * P],
                                            prob[:, h, m * P:(m + 1) * P], ident)
                memory["turned"] = T.done(last)
            else:
                memory["copied"] = A.run(ac.activation, PT[:, :, :, a * P:(a + 1) * P],
                                         flat(space, 0, 2).rearrange("p (h m q) -> p h m q", h=MEMH, m=TT2), ACT.Copy,
                                         after=[memory["turned"]])

        ready = [V.last(), A.last()]
        T.wait(*ready)
        state = STATE[:, :, :].rearrange("p h d -> p (h d)")
        for n in range(S // C):
            a, r = n // 2, n % 2
            rows_ = slice(r * C, (r + 1) * C)
            cols = slice(a * 1024, (a + 1) * 1024)
            hs = [slice(a * 1024 + h * P, a * 1024 + (h + 1) * P) for h in range(NH)]
            at = [slice(a * 1024 + h * P + r * C, a * 1024 + h * P + (r + 1) * C) for h in range(NH)]
            for h in range(NH):
                last = mm(WRK[rows_, h // 4, (h % 4) * P:(h % 4 + 1) * P], WT[:, at[h]], STATE[:, h, :])
            t = T.done(last)
            vn = VNEW[rows_, :, :].rearrange("p h d -> p (h d)")
            t = V.run(ve.tensor_tensor, vn, U[rows_, cols], WRK[rows_, 0:2, :].rearrange("p b c -> p (b c)"),
                      ALU.subtract, after=[t])
            if r:
                memory_piece(a, 2)
            for h in range(NH):
                mm(ACC[:, 2 + n % 2, h * C:(h + 1) * C], STATE[:, h, :], q[:, h, n * C:(n + 1) * C],
                   h == 0, True, skip_group_check=True)
            T.wait(t)
            for h in range(NH):
                last = mm(ACC[:, 2 + n % 2, h * C:(h + 1) * C], VNEW[rows_, h, :], AT[rows_, at[h]],
                          False, True, skip_group_check=True)
            out_t = T.done(last)
            if n < S // C - 1:
                for h in range(NH):
                    last = mm(ACC[:, h // 4, (h % 4) * P:(h % 4 + 1) * P], KD[rows_, hs[h]], VNEW[rows_, h, :])
                t = T.done(last)
                memory_piece(a, 3 if r else 0)
                s1 = V.run(ve.tensor_tensor, STATE[:, :, :], STATE[:, :, :], over_cols(gl[:, n, :]), ALU.mult, after=[out_t])
                t = V.run(ve.tensor_tensor, state, flat(ACC, 0, 2), state, ALU.add, after=[t, s1])
            else:
                memory_piece(a, 3)
            ob = A.run(ac.activation, MIX[:, 0:8, n * C:(n + 1) * C], heads(ACC[:, 2 + n % 2, :]), ACT.Copy, after=[out_t])
            memory_piece(a, 4 if r else 1)
            T.wait(t, ob)
        T.wait(memory["copied"])
        vtok = MIX[:, 8:12, :].rearrange("p b t -> p (b t)").rearrange("p (m h d) -> p m h d", m=TT2, h=MEMH)
        for h in range(MEMH):
            for m in range(TT2):
                last = mm(space[:, h // 2, (h % 2) * S:(h % 2 + 1) * S], vtok[:, m, h, :], PT[:, h, m, :],
                          m == 0, m == TT2 - 1)
        A.run(ac.activation, MIX[:, 8:12, :], flat(space, 0, 2).rearrange("p (h q) -> p h q", h=MEMH), ACT.Copy,
              after=[T.done(last)])

        ev = everything()
        o = MIX[:, 0:8, :]
        tz = A.run(ac.activation, z, z, ACT.Silu)
        t = head_norm([o[:, 0:4, :], o[:, 4:8, :]], False, P, lambda n, piece, spread: V.run(
            ve.scalar_tensor_tensor, piece, spread, v_("gdn_norm"), piece, ALU.mult, ALU.mult), ev)
        V.run(ve.tensor_tensor, o, o, z, ALU.mult, after=[t, tz])


    def bias_table():
        T.wait(loaded["tab"], loaded["onehot"])
        last = mm(WRK[0:NH, 3, :], tab[0:BUCKETS + 1, :], onehot[0:BUCKETS + 1, :])
        t = A.run(ac.activation, tiny[0:NH, :], WRK[0:NH, 3, :], ACT.Copy, after=[T.done(last), V.last()])
        T.wait(t)
        put = nc.alloc_semaphore("bias_line_stored")
        loaded["table"] = (nc.alloc_semaphore("bias_table_loaded"), 16)
        nc.gpsimd.wait_ge(*t)
        nc.gpsimd.dma_start(scratch, tiny[0:NH, :]).then_inc(put, 16)
        nc.gpsimd.wait_ge(put, 16)
        over = bass.AP(tensor=scratch.tensor, offset=0, ap=[[1, P], [512, NH], [1, 384]])
        nc.gpsimd.dma_start(PROJ[:, 24:36, :].rearrange("p b t -> p (b t)").rearrange("p (h y) -> p h y", h=NH), over
                            ).then_inc(loaded["table"][0], 16)

    def sparse_mixer(ready):
        H = AR[3][:, :].rearrange("p (k t) -> p k t", t=S)
        table = PROJ[:, 24:36, :].rearrange("p b t -> p (b t)").rearrange("p (h y) -> p h y", h=NH)
        project(12, to_proj(PROJ), A, {A: 1}, ready=ready)
        memory_values()
        A.wait(loaded["table"])
        q, kvp, qm = PROJ[:, 0:8, :], PROJ[:, 8:20, :], [PROJ[:, 20 + h, :] for h in range(MEMH)]
        ev = everything()

        small_ = AR[2][:, 1024:2048]
        hidden = [small_[:, 0:30], small_[:, 32:62]]
        kcT = small_[:, 64:94].rearrange("p (g c) -> p g c", g=2)
        vc = small_[0:NCMP, 128:384].rearrange("p (g d) -> p g d", g=2)
        for n, (part, pos) in enumerate((("k", "pos_k"), ("v", "pos_v"))):
            blk = AR[4][:, n * 1024:n * 1024 + 960].rearrange("p (l g c) -> p l g c", l=32, g=2)
            for g in range(2):
                for hl in range(2):
                    x = kvp[:, 2 * n + g, hl * 16:hl * 16 + 16 * NCMP].rearrange("p (c l) -> p l c", l=16)
                    V.run(ve.tensor_tensor, blk[:, hl * 16:(hl + 1) * 16, g, :], x,
                          v_(pos, hl * 16, 16).unsqueeze(2).broadcast_to([P, 16, NCMP]), ALU.add, after=ev)
        t, windows = V.last(), []
        for n in range(2):
            blk = AR[4][:, n * 1024:n * 1024 + 960]
            t = A.run(ac.activation, BH[:, n, :], blk, ACT.Copy, after=[t])
            windows.append(V.run(ve.tensor_tensor, BL[:, n, :], blk, BH[:, n, :].bitcast(F32), ALU.subtract, after=[t]))
        wg = s_("w_gate").rearrange("p (k c) -> p k c", c=24)
        for a in range(TT2):
            for k in range(DK):
                last = mm(WRK[:, 3, a * 24:(a + 1) * 24], H[:, k, a * P:(a + 1) * P], wg[:, k, :], k == 0, k == DK - 1)
        gates = tiny[:, 192:240].rearrange("p (t h c) -> p t h c", t=2, c=3)
        t = A.run(ac.activation, tiny[:, 192:240], WRK[:, 3, 0:48], ACT.Exp, scale=-1.0, after=[T.done(last)])
        t = V.run(ve.tensor_scalar, tiny[:, 192:240], tiny[:, 192:240], 1.0, None, ALU.add, after=[t])
        V.run(ve.reciprocal, tiny[:, 192:240], tiny[:, 192:240], after=[t])
        qs = V.run(ve.tensor_scalar, q, q, SCALE, None, ALU.mult, after=ev)
        for n in range(2):
            for s in range(2):
                u = 2 * n + s
                parts, made, used = ring.slot(0, u)
                T.wait(made, windows[n], *ev)
                for l in range(16):
                    at = slice((s * 16 + l) * 30, (s * 16 + l) * 30 + 30)
                    high, low = parts
                    mm(WRK[0:30, n, 0:P], BH[:, n, at], high[:, l, :], s == 0 and l == 0, False)
                    mm(WRK[0:30, n, 0:P], BL[:, n, at], high[:, l, :], False, False)
                    last = mm(WRK[0:30, n, 0:P], BH[:, n, at], low[:, l, :], False, s == 1 and l == 15)
                last.then_inc(used[0], 1)
                next_split(0, u)
            hid_t = small_[0:30, 384 + n * P:384 + (n + 1) * P]
            T.wait(A.run(ac.activation, hid_t, WRK[0:30, n, 0:P], ACT.Silu, after=[used]))
            t = T.done(te.transpose(WRK[:, 2 + n, 0:30], hid_t, ident[0:30, 0:30]))
            A.run(ac.activation, hidden[n], WRK[:, 2 + n, 0:30], ACT.Copy, after=[t])
        ring.g += 4
        T.wait(A.last())
        mm(WRK[:, 2, 0:30], s_("w2_k"), hidden[0])
        for g in range(2):
            last = mm(WRK[0:NCMP, 3, g * P:(g + 1) * P], hidden[1][:, g * NCMP:(g + 1) * NCMP], s_("w2_v"))
        t = T.done(last)
        A.run(ac.activation, kcT, WRK[:, 2, 0:30].rearrange("p (g c) -> p g c", g=2), ACT.Copy, after=[t])
        cmp_done = A.run(ac.activation, vc, WRK[0:NCMP, 3, 0:S].rearrange("p (g d) -> p g d", g=2), ACT.Copy, after=[t])

        vtok = AR[2][:, 0:1024].rearrange("p (m j d) -> p m j d", m=TT2, j=4)
        T.wait(cmp_done)
        for m in range(TT2):
            for j in range(4):
                block = (6 if j < 2 else 10) + j % 2
                last = te.transpose(WRK[:, m, j * P:(j + 1) * P], kvp[:, block, m * P:(m + 1) * P], ident)
        vt_done = A.run(ac.activation, AR[2][:, 0:1024], flat(WRK, 0, 2), ACT.Copy, after=[T.done(last)])

        T.wait(loaded["table"], qs)
        flip = c_("flip")
        PCT = MIX[:, 0:8, :]
        pcT = AR[4][0:NCMP, :].rearrange("p (h q) -> p h q", h=NH)
        V.wait(vt_done)
        for a in range(TT2):
            pc = AR[3][:, a * 256:a * 256 + 120].rearrange("p (h c) -> p h c", h=NH)
            sc = WRK[:, 2, a * 128:a * 128 + 120].rearrange("p (h c) -> p h c", h=NH)
            y0 = 31 + P * (1 - a)
            mm(sc, flip, table[:, :, y0:y0 + 16 * (NCMP - 1) + 1:16], skip_group_check=True)
            for h in range(NH):
                last = mm(sc[:, h, :], q[:, h, a * P:(a + 1) * P], kcT[:, h // 4, :], False, True, skip_group_check=True)
            t = T.done(last)
            mx, tot = tiny[:, 256 + a * 16:264 + a * 16], tiny[:, 264 + a * 16:272 + a * 16]
            t = V.run(ve.tensor_reduce, mx, sc, AX_X, ALU.max, after=[t])
            t = V.run(ve.tensor_scalar, mx, mx, NEG / 10, None, ALU.max, after=[t])
            t = V.run(ve.tensor_tensor, pc, sc, over_cols(mx, NCMP), ALU.subtract, after=[t])
            t = A.run(ac.activation, pc, pc, ACT.Exp, after=[t])
            t = V.run(ve.tensor_reduce, tot, pc, AX_X, ALU.add, after=[t])
            t = V.run(ve.tensor_scalar, tot, tot, 1e-30, None, ALU.max, after=[t])
            t = V.run(ve.reciprocal, tot, tot, after=[t])
            t = V.run(ve.tensor_tensor, tot, tot, gates[:, a, :, 0], ALU.mult, after=[t])
            t = V.run(ve.tensor_tensor, pc, pc, over_cols(tot, NCMP), ALU.mult, after=[t])
            T.wait(t)
            for h in range(NH):
                last = te.transpose(WRK[0:NCMP, h // 4, (h % 4) * P:(h % 4 + 1) * P], pc[:, h, :], ident)
            t = A.run(ac.activation, pcT[:, :, a * P:(a + 1) * P],
                      WRK[0:NCMP, 0:2, :].rearrange("p b c -> p (b c)").rearrange("p (h q) -> p h q", h=NH), ACT.Copy,
                      after=[T.done(last)])
            T.wait(t)

        out = flat(ACC, 0, 4).rearrange("p (h q) -> p h q", h=NH)
        for b in range(4):
            mm(ACC[:, b, :], zeros[:, 0:P], zeros[:, :], skip_group_check=True)
        for h in range(NH):
            last = mm(out[:, h, :], vc[:, h // 4, :], pcT[:, h, :], False, True, skip_group_check=True)
        pc_done = T.done(last)
        V.wait(pc_done)
        A.wait(pc_done)
        PTs = AR[1][:, :].rearrange("p (h m q) -> p h m q", h=4, m=TT2)

        def unit(j, a):
            br, g = j // 2, j % 2
            kblock = (4 if j < 2 else 8) + j % 2
            nk = (a + 1) * P
            space = WRK[:, 2 * a:2 * a + 2, :]
            sc = flat(space, 0, 2).rearrange("p (h k) -> p h k", h=4)[:, :, 0:nk]

            def scores():
                y0 = P * (1 - a)
                for b in range(2):
                    mm(sc[:, 2 * b:2 * b + 2, :], flip, table[:, g * 4 + 2 * b:g * 4 + 2 * b + 2, y0:y0 + nk],
                       skip_group_check=True)
                for h in range(4):
                    last = mm(sc[:, h, :], q[:, g * 4 + h, a * P:(a + 1) * P], kvp[:, kblock, 0:nk], False, True,
                              skip_group_check=True)
                return T.done(last)

            def values():
                for h in range(4):
                    mm(out[:, g * 4 + h, :], vtok[:, 0, j, :], PTs[:, h, 0, :], False, True, skip_group_check=True)
                    last = mm(out[:, g * 4 + h, P:S], vtok[:, 1, j, :], PTs[:, h, 1, P:S], False, True,
                              skip_group_check=True)
                if j >= 2:
                    V.run(ve.tensor_copy, MIX[:, 4 * g:4 * g + 4, :], out[:, 4 * g:4 * g + 4, :], after=[T.done(last)])

            return dict(scores=scores, space=space, view=sc, stats=tiny[:, 288 + 16 * a:304 + 16 * a], scale=1.0,
                        prob=heads(AR[0][:, a * 1024:(a + 1) * 1024], 4)[:, :, 0:nk], gate=gates[:, a, g * 4:g * 4 + 4, 1 + br],
                        turned=PTs[:, :, 0:a + 1, a * P:(a + 1) * P], values=values if a else None)

        attend([unit(j, a) for j in range(4) for a in range(TT2)] + memory_units(qm))


    def modulation_of(layer, part, which):
        if which == "c_ctx":
            return modc[:, part * DK:(part + 1) * DK]
        return mods[:, layer * NMOD + part * DK:layer * NMOD + (part + 1) * DK]

    def add_bias(dst, first, n):
        V.run(ve.tensor_tensor, dst, dst, v_("b_mod", first, n), ALU.add, after=[(mod_used, taken[0])])

    def input_gain(layer, n, which, after=()):
        V.run(ve.scalar_tensor_tensor, gainA[:, :], modulation_of(layer, 3 * n + 1, which), 1.0,
              v_("norm_g", (layer * 3 + n) * DK, DK), ALU.add, ALU.mult, after=[V.last()] + list(after))
        return gainA

    def modulated(source, layer, n, which, blocks):
        dst = AR[3][:, :].rearrange("p (k t) -> p k t", t=S)
        ev = everything() if blocks is None else []
        input_gain(layer, n, which, ev)
        return rms_norm(dst, source, gainA, ev, modulation_of(layer, 3 * n, which), blocks=blocks)

    def half_ffn(stream, layer, n, which, blocks=None, vectors=(), ready=None, beside=None, early=None):
        free = everything()
        gate = tiny[:, 320:328]
        V.run(ve.tensor_scalar, gate, modulation_of(layer, 3 * n + 2, which), 0.5, None, ALU.mult, after=[V.last()])
        if ready is None:
            ready = modulated(stream, layer, n, which, blocks)
        return add_sums(stream, feed_forward(None, free, vectors, ready, beside, early), gate)

    def attention_and_pool(ready, blocks):
        KK = PROJ[:, 4:8, :].rearrange("p b t -> p (b t)").rearrange("p (g t) -> p g t", g=2)
        VT = PROJ[:, 8:10, :].rearrange("p b t -> p (b t)")
        pool = PROJ[:, 10:14, :]

        def keys_values(w):
            def evacuate(i, u, bank, ready):
                next_split(i, u)
                block = 2 * u
                if block == 0:
                    A.run(ac.activation, KK[:, :, w * S:(w + 1) * S], bank, ACT.Copy, after=[ready])
                elif block == 2:
                    A.run(ac.activation, VT[:, w * S:(w + 1) * S], bank[:, 0, :], ACT.Copy, after=[ready])
                    if w == 1:
                        A.run(ac.activation, pool[:, 0, :], bank[:, 1, :], ACT.Copy, after=[ready])
                elif block in (4, 6):
                    A.run(ac.activation, PROJ[:, block - 4:block - 2, :], bank, ACT.Copy, after=[ready])
                elif block == 8:
                    A.run(ac.activation, pool[:, 1:3, :], bank, ACT.Copy, after=[ready])
                else:
                    A.run(ac.activation, pool[:, 3, :], bank[:, 0, :], ACT.Copy, after=[ready])
            return evacuate

        gain = input_gain(0, 1, "c")
        ready = project_two(2, keys_values(0), ready, X, gain, blocks, modulation_of(0, 3, "c"))
        base = A.n
        for u in range(6):
            parts, made, used = ring.slot(0, u)
            if u >= 3:
                T.wait((A.sem, base + (1, 3, 4)[u - 3]))
            T.wait(made)
            for b in range(2):
                if u == 5 and b == 1:
                    continue
                for k in range(DK):
                    if u == 0 and b == 0:
                        T.wait(ready[k])
                    last = mm3(WRK[:, u % 3, b * S:(b + 1) * S], parts, b * DK + k, XH[:, k, :], XL[:, k, :],
                               k == 0, k == DK - 1)
            last.then_inc(used[0], 1)
            keys_values(1)(0, u, WRK[:, u % 3, :].rearrange("p (b t) -> p b t", b=2), used)
        ring.g += 6
        ev = everything()


        wide = S + 16
        pa = AR[1][:, 0:4 * wide].rearrange("p (g t) -> p g t", g=4)
        pb = AR[4][:, 0:4 * wide].rearrange("p (g t) -> p g t", g=4)
        L.run(nc.gpsimd.memset, pa, 0.0, after=ev)
        t = L.run(nc.gpsimd.memset, pb, 0.0)
        t = L.run(nc.gpsimd.tensor_copy, pa[:, :, 8:8 + S], pool, after=[t])
        t = L.run(nc.gpsimd.tensor_tensor, pb[:, :, 1:wide], pa[:, :, 0:wide - 1], pa[:, :, 1:wide], ALU.add, after=[t])
        t = L.run(nc.gpsimd.tensor_tensor, pa[:, 1:4, 1:wide - 1], pb[:, 1:4, 0:wide - 2], pb[:, 1:4, 2:wide], ALU.add, after=[t])
        t = L.run(nc.gpsimd.tensor_tensor, pb[:, 2:4, 2:wide - 2], pa[:, 2:4, 0:wide - 4], pa[:, 2:4, 4:wide], ALU.add, after=[t])
        t = L.run(nc.gpsimd.tensor_tensor, pa[:, 3:4, 4:wide - 4], pb[:, 3:4, 0:wide - 8], pb[:, 3:4, 8:wide], ALU.add, after=[t])
        cnt = c_("count").rearrange("p (g t) -> p g t", g=4)
        out = AR[2][:, 1024:2048].rearrange("p (g t) -> p g t", g=4)
        for g, place in enumerate((pb, pa, pb, pa)):
            L.run(nc.gpsimd.tensor_tensor, out[:, g, :], place[:, g, 8:8 + S], cnt[:, g, :], ALU.mult, after=[t])
        pooled = L.run(nc.gpsimd.tensor_tensor, out, out, pool, ALU.subtract, after=[L.last()])

        sq = AR[0]
        ev = [head_norm([PROJ[:, 0:4, :], PROJ[:, 4:8, :]], True, C, lambda n, piece, spread: V.run(
            ve.scalar_tensor_tensor, piece, spread, v_("qk_norm", n, 1), piece, ALU.mult, ALU.mult), ev)]
        T.wait(*ev)
        for b in range(4):
            mm(WRK[:, b // 2, (b % 2) * S:(b % 2 + 1) * S], c_("rope"), PROJ[:, b, :])
        for g in range(2):
            last = mm(WRK[:, 2, g * S:(g + 1) * S], c_("rope"), KK[:, g, S:2 * S])
        t = T.done(last)
        swapped = flat(WRK, 0, 3).rearrange("p (b t) -> p b t", t=S)
        turn = sq[:, 0:1536].rearrange("p (b t) -> p b t", t=S)
        V.run(ve.tensor_tensor, turn, swapped, over_rows(c_("sin"), 6), ALU.mult, after=[t])
        for dst, part in ((PROJ[:, 0:4, :], turn[:, 0:4, :]), (KK[:, :, S:2 * S], turn[:, 4:6, :])):
            n = dst.shape[1]
            t = V.run(ve.tensor_tensor, dst, dst, over_rows(c_("cos"), n), ALU.mult, after=[V.last()])
            V.run(ve.tensor_tensor, dst, dst, part, ALU.add, after=[t])
        ev = everything()

        T.wait(*ev)
        for kt in range(4):
            last = te.transpose(WRK[:, 3, kt * P:(kt + 1) * P], VT[:, kt * P:(kt + 1) * P], ident)
        t = A.run(ac.activation, AR[2][:, 0:512], WRK[:, 3, :], ACT.Copy, after=[T.done(last)] + ev)
        vtok = AR[2][:, 0:512].rearrange("p (k d) -> p k d", k=4)
        PTs = PROJ[:, 14:30, :].rearrange("p b t -> p (b t)").rearrange("p (h k q) -> p h k q", h=4, k=4)
        T.wait(t)

        def unit(g, a):
            space = ACC if a == 0 else WRK

            def scores():
                for h in range(4):
                    part = slice(((g * 4 + h) % 2) * C, ((g * 4 + h) % 2 + 1) * C)
                    last = mm(space[:, h, :], PROJ[part, (g * 4 + h) // 2, a * P:(a + 1) * P], KK[part, g, :])
                return T.done(last)

            def values():
                for h in range(4):
                    part = slice(((g * 4 + h) % 2) * C, ((g * 4 + h) % 2 + 1) * C)
                    for kt in range(4):
                        last = mm(WRK[part, h // 2, 0:S], vtok[:, kt, g * C:(g + 1) * C], PTs[:, h, kt, :],
                                  kt == 0, kt == 3)
                T.wait(A.run(ac.activation, MIX[:, 2 * g:2 * g + 2, :], WRK[:, 0:2, 0:S], ACT.Copy, after=[T.done(last)]))

            return dict(scores=scores, space=space, view=space[:, :, :], prob=heads(AR[0 if a == 0 else 3][:, :], 4),
                        stats=tiny[:, 336 + 8 * a:344 + 8 * a], scale=C ** -0.5, gate=None,
                        turned=PTs[:, :, :, a * P:(a + 1) * P], values=values if a else None)

        attend([unit(g, a) for g in range(2) for a in range(TT2)])

        T.wait(pooled)
        for g in range(4):
            last = mm(WRK[:, 2 + g // 2, (g % 2) * S:(g % 2 + 1) * S], s_("pool_w")[:, g * P:(g + 1) * P], out[:, g, :])
        t = T.done(last)
        for g in range(4):
            V.run(ve.tensor_scalar, MIX[:, 4 + g, :], WRK[:, 2 + g // 2, (g % 2) * S:(g % 2 + 1) * S],
                  v_("pool_scale", g, 1), None, ALU.mult, after=[t])
        return add_sums(X, out_projection(4, everything()), modulation_of(0, 5, "c"))

    def gmlp(blocks):
        T.wait(*modulated(X, 1, 1, "c", blocks))

        def gelu(i, u, bank, ready):
            next_split(i, u)
            A.run(ac.activation, PROJ[:, bass.ds(i * (2 * R) + 2 * u, 2), :], bank, ACT.Gelu_apprx_tanh, after=[ready])

        project(8, gelu, A, {A: 1})
        u, v = PROJ[:, 0:8, :], PROJ[:, 8:16, :]
        VN = AR[3][:, :].rearrange("p (k t) -> p k t", t=S)
        t = rms_norm(VN, v, v_("v_norm"), everything(), parts=False)[-1]
        vtok = AR[1][:, :].rearrange("p (a g c) -> p a g c", a=2, g=NH)
        T.wait(t)
        for a in range(TT2):
            for g in range(NH):
                last = te.transpose(ACC[:, 2 * a + g // 4, (g % 4) * P:(g % 4 + 1) * P], VN[:, g, a * P:(a + 1) * P], ident)
        t = A.run(ac.activation, AR[1][:, :], flat(ACC, 0, 4), ACT.Copy, after=[T.done(last), V.last()])
        T.wait(t, loaded["bsp"], loaded["w_sp"])
        wsp = KV[:, 0:4, :].rearrange("p b t -> p (b t)").rearrange("p (g q) -> p g q", g=NH)
        for a in range(TT2):
            for g in range(NH):
                o = WRK[:, 2 * a + g // 4, (g % 4) * P:(g % 4 + 1) * P]
                mm(o, vtok[:, a, g, :], wsp[:, g, :], True, False)
                last = mm(o, ones[0:1, :], VNEW[0:1, g, :], False, True)
            t = T.done(last)
            V.run(ve.tensor_tensor, MIX[:, 0:8, a * P:(a + 1) * P],
                  flat(WRK, 2 * a, 2 * a + 2).rearrange("p (g t) -> p g t", g=NH), u[:, :, a * P:(a + 1) * P],
                  ALU.mult, after=[t])
        return add_sums(X, out_projection(4, everything()), modulation_of(1, 5, "c"))


    stream_from(RAW, NSLOT + 1)

    H = AR[3][:, :].rearrange("p (k t) -> p k t", t=S)
    G = nc.gpsimd
    pairs = squares(SIDE, [loaded["side"]])
    ring.split(V, A, 0, 0)
    t = root_mean_square(RINV[:, :], pairs)
    ready = normed(H, SIDE, v_("mem_norm", 0, DK), RINV, t)
    ring.split(V, A, 0, 1)
    for q_ in (A, V):
        q_.wait(loaded["x"])
    gated_delta_mixer(memory_keys(0, ready, None))
    G.wait_ge(V.sem, V.n)
    G.wait_ge(T.sem, T.n)
    for name in ("c", "c_ctx"):
        loaded[name] = (nc.alloc_semaphore("load_" + name), 16)
        G.dma_start(COND[name], src[name].partition_broadcast(P)).then_inc(loaded[name][0], 16)
    blocks = add_sums(X, out_projection(6, everything()))
    free = everything()
    ready = rms_norm(H, X, v_("norm_ffn", 0, DK), [], blocks=blocks)
    for name in ("c", "c_ctx"):
        t = A.run(ac.activation, COND[name], COND[name], ACT.Silu, after=[loaded[name]])
    V.wait(t)
    inputs = []

    def memory_norm():
        bias_table()
        inputs.append(memory_input(1, [(ring.used, ring.g)]))

    blocks = add_sums(X, feed_forward(0, free, (8, 0, 0, "c_ctx", modc), ready, memory_norm))

    sparse_mixer(memory_keys(1, inputs[-1], blocks))
    load_side = nc.alloc_semaphore("in_context")
    nc.scalar.wait_ge(V.sem, V.n)
    nc.scalar.wait_ge(T.sem, T.n)
    nc.scalar.dma_start(SIDE[:, :, :], src["ctx"]).then_inc(load_side, 16)
    loaded["w_sp"] = (nc.alloc_semaphore("load_w_sp"), 16)
    nc.scalar.wait_ge(A.sem, A.n)
    nc.scalar.dma_start(KV[:, 0:4, :], src["w_sp"].rearrange("p (k t) -> p k t", t=S)).then_inc(loaded["w_sp"][0], 16)
    blocks = add_sums(X, out_projection(6, everything()))
    free = everything()
    ready = rms_norm(H, X, v_("norm_ffn", DK, DK), [], blocks=blocks)

    def context_norm():
        add_bias(modc[:, :], 0, 5 * DK)
        add_bias(mods[:, 0:5 * DK], 0, 5 * DK)
        V.wait(V.last(), (ring.used, ring.g))
        A.wait(V.last(), (ring.used, ring.g), (load_side, 16))
        inputs.append(modulated(SIDE, 0, 0, "c_ctx", [V.last()] * DK))

    blocks = add_sums(X, feed_forward(1, free, (8, 0, 0, "c", mods), ready, context_norm))

    def final_norm():
        V.wait(rms_norm(X, X, v_("final_norm"), [], parts=False, blocks=blocks)[-1])

    ready = []

    def tokens_norm():
        for q_ in (V, A):
            q_.wait((ring.used, ring.g))
        ready.extend(modulated(X, 0, 0, "c", [V.last()] * DK))

    half_ffn(SIDE, 0, 0, "c_ctx", vectors=(8, 40, 0, "c", mods), ready=inputs[-1], beside=tokens_norm, early=final_norm)

    def context_input():
        add_bias(mods[:, 5 * DK:15 * DK], 5 * DK, 10 * DK)
        for q_ in (V, A):
            q_.wait((ring.used, ring.g), V.last())
        inputs.append(modulated(SIDE, 0, 1, "c_ctx", [V.last()] * DK))

    blocks = half_ffn(X, 0, 0, "c", vectors=(8, 80, 0, "c", mods), ready=ready, beside=context_input)
    blocks = attention_and_pool(inputs[-1], blocks)
    blocks = half_ffn(X, 0, 2, "c", blocks, vectors=(4, 120, 4, "c", mods))
    add_bias(mods[:, 15 * DK:18 * DK], 15 * DK, 3 * DK)
    G.wait_ge(mod_used, taken[0])
    loaded["bsp"] = (nc.alloc_semaphore("load_bsp"), 16)
    G.dma_start(VNEW[0:1, :, :].rearrange("p h d -> p (h d)"), src["bsp"].unsqueeze(0)).then_inc(loaded["bsp"][0], 16)
    V.wait(V.last())
    blocks = half_ffn(X, 1, 0, "c", blocks)
    blocks = gmlp(blocks)
    half_ffn(X, 1, 2, "c", blocks)
    assert ring.g == NSLOT

    stored = nc.alloc_semaphore("out_stored")
    nc.sync.wait_ge(V.sem, V.n)
    nc.sync.dma_start(y_out, X[:, :, :]).then_inc(stored, 16)
    nc.sync.wait_ge(stored, 16)



def shape_constants():
    i = np.arange(P)
    same = (i[:, None] // C) == (i[None, :] // C)
    c = {}
    c["ident"] = np.eye(P)
    c["ones"] = np.ones((P, P))
    c["tri"] = (same & (i[:, None] <= i[None, :]))
    c["half"] = same
    c["neg"] = np.where(c["tri"], 0.0, NEG)
    c["before"] = same & (i[:, None] > i[None, :])
    c["flip"] = np.eye(P)[::-1]
    levels = []
    for s in (1, 2, 4, 8, 16, 32):
        block = (i[:, None] // (2 * s)) == (i[None, :] // (2 * s))
        levels.append(block & ((i[:, None] // s) % 2 == 1) & ((i[None, :] // s) % 2 == 0))
    c["levels"] = np.concatenate(levels, axis=1)
    rope = np.zeros((P, P))
    for m in range(P):
        if m % 32 < 16:
            rope[m + 16, m] = -1.0
        else:
            rope[m - 16, m] = 1.0
    c["rope"] = rope
    half = 32
    inv = (np.float32(10000.0) ** (-np.arange(0, half, 2, dtype=np.float32) / np.float32(half))).astype(np.float32)
    t = np.arange(S)
    axis = np.where(((i % C) // 32 == 0)[:, None], (t // 64)[None, :], (t % 64)[None, :]).astype(np.float32)
    ang = axis * inv[i % 16][:, None]
    c["cos"], c["sin"] = np.cos(ang), np.sin(ang)
    cnt = [1.0 / (np.clip(t + w // 2, 0, S) - np.clip(t - w // 2, 0, S)) for w in (2, 4, 8, 16)]
    c["count"] = np.broadcast_to(np.concatenate(cnt)[None, :], (P, 4 * S))
    c["pick"] = np.zeros((P, 31))
    c["pick"][:, 15] = 1.0
    c["pick_half"] = np.zeros((P, 30))
    c["pick_half"][:C, 14] = c["pick_half"][C:, 15] = 1.0
    out = np.zeros((P, NCST), np.float32)
    for name, (a, b) in CST.items():
        out[:, a:b] = c[name]
    dist = np.arange(S)
    exact = BUCKETS // 2
    logv = (np.log(np.maximum(dist, 1).astype(np.float32) / np.float32(exact)) / np.float32(math.log(128 / exact))).astype(np.float32)
    large = np.minimum(exact + (logv * np.float32(BUCKETS - exact)).astype(np.int32), BUCKETS - 1)
    bucket = np.where(dist < exact, dist, large)
    onehot = np.zeros((BUCKETS + 1, 512), np.float32)
    onehot[bucket, 255 - dist] = 1.0
    onehot[BUCKETS, 256:] = 1.0
    return out, onehot



def fm(x):
    x = np.asarray(x)
    return x.reshape(-1, P).T


def in_slots(w):
    n = w.shape[1] // 256
    return w.reshape(DK, P, n, 2, P).transpose(2, 1, 3, 0, 4).reshape(n, P, TILES * P)


def up_slots(w):
    return w.reshape(DK, P, 2, FB, P).transpose(3, 1, 2, 0, 4).reshape(FB, P, TILES * P)


def down_slots(w):
    return w.reshape(-1, 2, P, D).transpose(0, 2, 1, 3).reshape(-1, P, TILES * P)


def ffn_slots(up, down):
    u, d = up_slots(up), down_slots(down)
    order = [u[0:2]]
    for p in range(1, FB // 2):
        order += [u[2 * p:2 * p + 2], d[p - 1:p]]
    return np.concatenate(order + [d[FB // 2 - 1:]])


def kernel(**inputs):
    import concourse.bacc as bacc
    from concourse.bass_utils import run_bass_kernel_spmd

    g = {k: np.asarray(v) for k, v in inputs.items()}
    tokens = lambda x: np.ascontiguousarray(x.reshape(S, DK, P).transpose(2, 1, 0))
    gdn, nsa = g["gdn_w_in"][0], g["nsa_w_in"][0]
    wa = g["w_in_a_2"][0]
    k0, k1 = wa[:, 512:576], wa[:, 576:640]
    in_a = np.concatenate([k0, k0, k1, k1, wa[:, 640:768], wa[:, 768:896], wa[:, 0:512], wa[:, 896:1280],
                           np.zeros((D, P), np.float32)], axis=1)
    cmp_ = lambda w: w[0].reshape(2, 16, P, P).transpose(0, 2, 1, 3).reshape(2, P, TILES * P)
    parts = {
        "mem_kv0": in_slots(g["mem_w_kv"][0]),
        "gdn_in": in_slots(np.concatenate([gdn[:, :4096], gdn[:, 4112:]], axis=1)),
        "out0": down_slots(g["w_out"][0]),
        "ffn0": ffn_slots(g["ffn_w_up"][0], g["ffn_w_down"][0]),
        "mem_kv1": in_slots(g["mem_w_kv"][1]),
        "nsa_in": in_slots(np.concatenate([nsa[:, :2560], nsa[:, 2584:]], axis=1)),
        "cmp_k": cmp_(g["nsa_cmp_w1_k"]), "cmp_v": cmp_(g["nsa_cmp_w1_v"]),
        "out1": down_slots(g["w_out"][1]),
        "ffn1": ffn_slots(g["ffn_w_up"][1], g["ffn_w_down"][1]),
        "in_ac": in_slots(in_a[:, 0:512]), "in_a": in_slots(in_a), "out_a": down_slots(g["w_out_a_2"][0]),
        "in_c": in_slots(g["w_in_c_2"][0]), "out_c": down_slots(g["w_out_c_2"][0]),
    }
    ff = {(i, j): ffn_slots(g["ffn_w13_2"][i, j], g["ffn_w2_2"][i, j]) for i in range(2) for j in range(2)}
    parts.update(ffn2c=ff[0, 0], ffn2=ff[0, 0], ffn3=ff[0, 1], ffn4=ff[1, 0], ffn5=ff[1, 1])
    weights = np.concatenate([parts[name] for name, _ in STREAM])

    v = {
        "norm_mix": fm(g["norm_mix_w"]), "norm_ffn": fm(g["norm_ffn_w"]), "final_norm": fm(g["final_norm_w"]),
        "mem_norm": fm(g["mem_norm_w"]), "gdn_conv": fm(g["gdn_conv_w"]), "gdn_norm": fm(g["gdn_norm_w"]),
        "ffn_conv": fm(g["ffn_conv_w"]), "ffn_bias": fm(g["ffn_conv_b"]),
        "pos_k": g["nsa_cmp_pos_k"][0].T, "pos_v": g["nsa_cmp_pos_v"][0].T,
        "b_mod": fm(g["b_mod_2"]), "norm_g": fm(g["norm_g_2"]),
        "qk_norm": np.concatenate([g["qk_norm_g_2"][0]] * 2, axis=1).T,
        "pool_scale": fm(g["pool_scale_2"]), "v_norm": fm(g["v_norm_g_2"]),
    }
    kc = lambda w: w.reshape(DK, P, -1).transpose(1, 0, 2).reshape(P, -1)
    sm = {
        "w_ba": kc(gdn[:, 4096:4112]), "w_gate": kc(nsa[:, 2560:2584]),
        "w2_k": g["nsa_cmp_w2_k"][0], "w2_v": g["nsa_cmp_w2_v"][0],
        "pool_w": g["pool_w_2"][0].transpose(1, 0, 2).reshape(P, 4 * P),
    }
    cst, onehot = shape_constants()
    arrays = {
        "x": tokens(g["x"]), "mem": tokens(g["mem"]), "ctx": tokens(g["ctx_2"]),
        "vec": np.concatenate([v[n] for n in VEC], axis=1), "small": np.concatenate([sm[n] for n in SMALL], axis=1),
        "cst": cst, "onehot": onehot, "rows": np.concatenate([g["gdn_a_log"][0], g["gdn_dt_bias"][0]]),
        "tab": g["rel_bias"], "bsp": g["b_sp_2"].reshape(-1), "weights": weights,
        "w_sp": g["w_sp_2"][0].transpose(2, 0, 1).reshape(P, NH * P), "c": g["c_2"].reshape(-1), "c_ctx": g["c_ctx_2"],
        "wmod": g["w_mod_2"].reshape(2, D, NMOD, P).transpose(0, 2, 3, 1).reshape(2 * NMOD, P, D),
    }
    arrays = {k: np.ascontiguousarray(a) for k, a in arrays.items()}

    nc = bacc.Bacc("TRN2", target_bir_lowering=False, num_devices=1)
    aps = {k: nc.dram_tensor("in_" + k, a.shape, F32, kind="ExternalInput").ap() for k, a in arrays.items()}
    y = nc.dram_tensor("y", (P, DK, S), F32, kind="ExternalOutput").ap()
    scratch = nc.dram_tensor("bias_line", (NH, 512), F32, kind="Internal").ap()
    program(nc, aps, aps["weights"], y, scratch)
    r = run_bass_kernel_spmd(nc, [{"in_" + k: a for k, a in arrays.items()}], core_ids=[0])
    return r.results[0]["y"].transpose(2, 1, 0).reshape(1, S, D)
```
